# Optimizing a Trainium2 kernel written in Bass

```python
import jax, jax.numpy as jnp
from jax import lax
import numpy as np

D_MODEL = 1024
BATCH = 1
SEQ = 512
DEPTH = 2

N_MIXERS = 2
N_MEM = 256
GRID_W = 64
TOKEN_W = 3 * D_MODEL // 4
MEM_W = D_MODEL // 4
MIX_W = TOKEN_W + MEM_W
HEAD_DIM = 64
NA_HEADS = TOKEN_W // HEAD_DIM
WIN_H = 8
WIN_W = 16
ML_HEADS = 4
ML_DH = TOKEN_W // ML_HEADS
ML_CHUNK = 64
CONV_K = 5
ML_PROJ = 4 * TOKEN_W + 4 * ML_HEADS
MEM_HEADS = 4
MEM_DH = MEM_W // MEM_HEADS
N_GROUPS = 4
EXPERTS_PER_GROUP = 8
N_EXPERTS = N_GROUPS * EXPERTS_PER_GROUP
TOP_K = 2
D_EXPERT = D_MODEL // 2
MOE_BLOCK = 128
LN_EPS = 1e-5
ALPHA = (2 * DEPTH) ** 0.25
BETA = (8 * DEPTH) ** -0.25
N_NA_LAYERS = (DEPTH + 1) // 2
N_ML_LAYERS = DEPTH // 2
NA_IN = 3 * TOKEN_W + MEM_W
ML_IN = ML_PROJ + MEM_W

kernel_name = "hybrid_natten_mlstm_hmoe_encoder"

def layer_norm(x, g, b):
    xf = x.astype(jnp.float32)
    mu = xf.mean(-1, keepdims=True)
    var = jnp.square(xf - mu).mean(-1, keepdims=True)
    y = (xf - mu) * lax.rsqrt(var + LN_EPS)
    return (y * g + b).astype(x.dtype)

def neighbourhood_attention(q, k, v, rpb):
    B, T, H, Dh = q.shape
    rows = T // GRID_W
    kh = min(WIN_H, rows)
    to_grid = lambda a: a.reshape(B, rows, GRID_W, H, Dh).transpose(1, 0, 3, 2, 4)
    qg, kg, vg = to_grid(q), to_grid(k), to_grid(v)
    cols = jnp.arange(GRID_W)
    col_start = jnp.clip(cols - WIN_W // 2, 0, GRID_W - WIN_W)
    col_idx = col_start[:, None] + jnp.arange(WIN_W)
    col_bias_idx = col_idx - cols[:, None] + (WIN_W - 1)
    scale = Dh ** -0.5

    def row_block(r):
        row_start = jnp.clip(r - kh // 2, 0, rows - kh)
        k_band = lax.dynamic_slice_in_dim(kg, row_start, kh, axis=0)
        v_band = lax.dynamic_slice_in_dim(vg, row_start, kh, axis=0)
        k_win = k_band[:, :, :, col_idx]
        v_win = v_band[:, :, :, col_idx]
        q_row = lax.dynamic_index_in_dim(qg, r, axis=0, keepdims=False)
        row_bias_idx = row_start + jnp.arange(kh) - r + (WIN_H - 1)
        bias = rpb[:, row_bias_idx[None, :, None], col_bias_idx[:, None, :]]
        s = jnp.einsum('bhqd,rbhqkd->bhqrk', q_row, k_win).astype(jnp.float32) * scale + bias
        p = jax.nn.softmax(s.reshape(B, H, GRID_W, kh * WIN_W), axis=-1)
        p = p.reshape(B, H, GRID_W, kh, WIN_W).astype(v.dtype)
        return jnp.einsum('bhqrk,rbhqkd->bhqd', p, v_win)

    out = lax.map(row_block, jnp.arange(rows))
    return out.transpose(1, 0, 3, 2, 4).reshape(B, T, H * Dh)

def mlstm_scan(q, k, v, log_i, log_f):
    B, H, T, Dh = q.shape
    L = min(ML_CHUNK, T)
    nc = T // L
    to_chunks = lambda a: jnp.moveaxis(a.reshape(B, H, nc, L, *a.shape[3:]), 2, 0)
    tril = jnp.tril(jnp.ones((L, L), dtype=bool))

    def step(carry, inp):
        C, n, m = carry
        qc, kc, vc, lic, lfc = inp
        b = jnp.cumsum(lfc, axis=-1)
        D = b[..., :, None] - b[..., None, :] + lic[..., None, :]
        D = jnp.where(tril, D, -jnp.inf)
        inter = b + m[..., None]
        m_t = jnp.maximum(inter, D.max(-1))
        w_inter = jnp.exp(inter - m_t)
        S = jnp.einsum('bhld,bhsd->bhls', qc, kc) * jnp.exp(D - m_t[..., None])
        num = w_inter[..., None] * jnp.einsum('bhld,bhde->bhle', qc, C) + jnp.einsum('bhls,bhse->bhle', S, vc)
        den = w_inter * jnp.einsum('bhld,bhd->bhl', qc, n) + S.sum(-1)
        h = num / jnp.maximum(jnp.abs(den), jnp.exp(-m_t))[..., None]
        b_last = b[..., -1]
        m_new = m_t[..., -1]
        decay = jnp.exp(b_last + m - m_new)
        w_src = jnp.exp(b_last[..., None] - b + lic - m_new[..., None])
        C_new = decay[..., None, None] * C + jnp.einsum('bhs,bhsd,bhse->bhde', w_src, kc, vc)
        n_new = decay[..., None] * n + jnp.einsum('bhs,bhsd->bhd', w_src, kc)
        return (C_new, n_new, m_new), h

    init = (jnp.zeros((B, H, Dh, Dh), jnp.float32), jnp.zeros((B, H, Dh), jnp.float32),
            jnp.zeros((B, H), jnp.float32))
    _, hs = lax.scan(step, init, (to_chunks(q), to_chunks(k), to_chunks(v), to_chunks(log_i), to_chunks(log_f)))
    return jnp.moveaxis(hs, 0, 2).reshape(B, H, T, Dh)

def centred_dwconv(x, w, b):
    C = x.shape[-1]
    y = lax.conv_general_dilated(x, w[:, None, :], window_strides=(1,),
                                 padding=[(CONV_K // 2, CONV_K // 2)],
                                 dimension_numbers=('NWC', 'WIO', 'NWC'),
                                 feature_group_count=C)
    return y + b

def mlstm_mixer(proj, conv_w, conv_b, gate_b, norm_g):
    B, T, _ = proj.shape
    qk_pre = proj[..., :2 * TOKEN_W]
    v = proj[..., 2 * TOKEN_W:3 * TOKEN_W]
    o_pre = proj[..., 3 * TOKEN_W:4 * TOKEN_W]
    gates = proj[..., 4 * TOKEN_W:]
    qk = jax.nn.silu(centred_dwconv(qk_pre, conv_w, conv_b))
    q, k = qk[..., :TOKEN_W], qk[..., TOKEN_W:]
    heads = lambda a: a.reshape(B, T, ML_HEADS, ML_DH).transpose(0, 2, 1, 3).astype(jnp.float32)
    qh, kh, vh = heads(q) * (ML_DH ** -0.5), heads(k), heads(v)
    g = (gates.reshape(B, T, 4, ML_HEADS).astype(jnp.float32) + gate_b).transpose(2, 0, 3, 1)
    log_i = g[:2]
    log_f = jax.nn.log_sigmoid(g[2:])
    flip = lambda a: jnp.flip(a, axis=2)
    h_fwd = mlstm_scan(qh, kh, vh, log_i[0], log_f[0])
    h_bwd = flip(mlstm_scan(flip(qh), flip(kh), flip(vh), flip(log_i[1]), flip(log_f[1])))
    h = (h_fwd + h_bwd).transpose(0, 2, 1, 3)
    mu = h.mean(-1, keepdims=True)
    var = jnp.square(h - mu).mean(-1, keepdims=True)
    h = ((h - mu) * lax.rsqrt(var + LN_EPS)).reshape(B, T, TOKEN_W) * norm_g
    return (jax.nn.sigmoid(o_pre.astype(jnp.float32)) * h).astype(proj.dtype)

def memory_attention(q, mem_k, mem_v):
    B, T, _ = q.shape
    qh = q.reshape(B, T, MEM_HEADS, MEM_DH)
    s = jnp.einsum('bthd,bmhd->bhtm', qh, mem_k).astype(jnp.float32) * (MEM_DH ** -0.5)
    p = jax.nn.softmax(s, axis=-1).astype(mem_v.dtype)
    return jnp.einsum('bhtm,bmhd->bthd', p, mem_v).reshape(B, T, MEM_W)

def hierarchical_moe(x, wg, bg, we, be, w1, w3, w2):
    B, T, D = x.shape
    xt = x.reshape(-1, D)
    N = xt.shape[0]
    g_logits = (xt @ wg).astype(jnp.float32) + bg
    g_prob = jax.nn.softmax(g_logits, axis=-1)
    g_idx = jnp.argmax(g_logits, axis=-1)
    g_gate = jnp.take_along_axis(g_prob, g_idx[:, None], axis=-1)
    e_logits = ((xt @ we).astype(jnp.float32) + be).reshape(N, N_GROUPS, EXPERTS_PER_GROUP)
    e_logits = jnp.take_along_axis(e_logits, g_idx[:, None, None], axis=1)[:, 0]
    top_p, top_i = lax.top_k(jax.nn.softmax(e_logits, axis=-1), TOP_K)
    gate = (g_gate * top_p / top_p.sum(-1, keepdims=True)).reshape(-1)
    eid = (g_idx[:, None] * EXPERTS_PER_GROUP + top_i).reshape(-1)
    tok = jnp.repeat(jnp.arange(N), TOP_K)
    A = N * TOP_K
    order = jnp.argsort(eid)
    s_eid, s_tok, s_gate = eid[order], tok[order], gate[order]
    counts = jnp.bincount(eid, length=N_EXPERTS)
    start = jnp.cumsum(counts) - counts
    padded = (counts + MOE_BLOCK - 1) // MOE_BLOCK * MOE_BLOCK
    pad_end = jnp.cumsum(padded)
    pad_start = pad_end - padded
    dest = pad_start[s_eid] + jnp.arange(A) - start[s_eid]
    n_blocks = -(-(A + N_EXPERTS * (MOE_BLOCK - 1)) // MOE_BLOCK)
    P = n_blocks * MOE_BLOCK
    row_tok = jnp.zeros((P,), jnp.int32).at[dest].set(s_tok.astype(jnp.int32))
    row_gate = jnp.zeros((P,), jnp.float32).at[dest].set(s_gate)
    block_eid = jnp.minimum(jnp.searchsorted(pad_end, jnp.arange(n_blocks) * MOE_BLOCK, side='right'),
                            N_EXPERTS - 1)
    xb = xt[row_tok].reshape(n_blocks, MOE_BLOCK, D)

    def expert_block(args):
        xblk, e = args
        h = jax.nn.silu(xblk @ w1[e]) * (xblk @ w3[e])
        return h @ w2[e]

    yb = lax.map(expert_block, (xb, block_eid)).reshape(P, D)
    y = jax.ops.segment_sum(yb * row_gate[:, None].astype(yb.dtype), row_tok, num_segments=N)
    return y.reshape(B, T, D)

def setup_inputs(seed: int = 0) -> dict:
    key = jax.random.key(seed)
    ks = jax.random.split(key, 24)
    nrm = lambda k, shape, s: jax.random.normal(k, shape, jnp.float32) * s
    D = D_MODEL
    f_init = jnp.linspace(3.0, 6.0, ML_HEADS)
    ml_gate_b = jnp.concatenate([nrm(ks[7], (N_ML_LAYERS, 2, ML_HEADS), 0.1),
                                 f_init + nrm(ks[8], (N_ML_LAYERS, 2, ML_HEADS), 0.1)], axis=1)
    return {
        "x": nrm(ks[0], (BATCH, SEQ, D), 1.0),
        "mem": nrm(ks[1], (BATCH, N_MEM, D), 1.0),
        "w_mem_kv": nrm(ks[2], (D, 2 * MEM_W), D ** -0.5),
        "na_w_in": nrm(ks[3], (N_NA_LAYERS, D, NA_IN), D ** -0.5),
        "na_rpb": nrm(ks[4], (N_NA_LAYERS, NA_HEADS, 2 * WIN_H - 1, 2 * WIN_W - 1), 0.02),
        "ml_w_in": nrm(ks[5], (N_ML_LAYERS, D, ML_IN), D ** -0.5),
        "ml_conv_w": nrm(ks[6], (N_ML_LAYERS, CONV_K, 2 * TOKEN_W), CONV_K ** -0.5),
        "ml_conv_b": nrm(ks[9], (N_ML_LAYERS, 2 * TOKEN_W), 0.01),
        "ml_gate_b": ml_gate_b,
        "ml_norm_g": 1.0 + nrm(ks[10], (N_ML_LAYERS, TOKEN_W), 0.02),
        "w_out": nrm(ks[11], (DEPTH, MIX_W, D), MIX_W ** -0.5 * BETA),
        "ln1_g": 1.0 + nrm(ks[12], (DEPTH, D), 0.02),
        "ln1_b": nrm(ks[13], (DEPTH, D), 0.02),
        "ln2_g": 1.0 + nrm(ks[14], (DEPTH, D), 0.02),
        "ln2_b": nrm(ks[15], (DEPTH, D), 0.02),
        "moe_wg": nrm(ks[16], (DEPTH, D, N_GROUPS), D ** -0.5),
        "moe_bg": nrm(ks[17], (DEPTH, N_GROUPS), 0.01),
        "moe_we": nrm(ks[18], (DEPTH, D, N_EXPERTS), D ** -0.5),
        "moe_be": nrm(ks[19], (DEPTH, N_EXPERTS), 0.01),
        "moe_w1": nrm(ks[20], (DEPTH, N_EXPERTS, D, D_EXPERT), D ** -0.5),
        "moe_w3": nrm(ks[21], (DEPTH, N_EXPERTS, D, D_EXPERT), D ** -0.5),
        "moe_w2": nrm(ks[22], (DEPTH, N_EXPERTS, D_EXPERT, D), D_EXPERT ** -0.5 * BETA),
    }

def reference(x, mem, w_mem_kv, na_w_in, na_rpb, ml_w_in, ml_conv_w, ml_conv_b, ml_gate_b,
              ml_norm_g, w_out, ln1_g, ln1_b, ln2_g, ln2_b, moe_wg, moe_bg, moe_we, moe_be,
              moe_w1, moe_w3, moe_w2):
    B, T, D = x.shape
    mem_kv = (mem @ w_mem_kv).reshape(B, N_MEM, 2, MEM_HEADS, MEM_DH)
    mem_k, mem_v = mem_kv[:, :, 0], mem_kv[:, :, 1]
    for layer in range(DEPTH):
        j = layer // N_MIXERS
        if layer % N_MIXERS == 0:
            proj = x @ na_w_in[j]
            qkv = proj[..., :3 * TOKEN_W].reshape(B, T, 3, NA_HEADS, HEAD_DIM)
            tok = neighbourhood_attention(qkv[:, :, 0], qkv[:, :, 1], qkv[:, :, 2], na_rpb[j])
            q_mem = proj[..., 3 * TOKEN_W:]
        else:
            proj = x @ ml_w_in[j]
            tok = mlstm_mixer(proj[..., :ML_PROJ], ml_conv_w[j], ml_conv_b[j], ml_gate_b[j], ml_norm_g[j])
            q_mem = proj[..., ML_PROJ:]
        mixed = jnp.concatenate([tok, memory_attention(q_mem, mem_k, mem_v)], axis=-1)
        x = layer_norm(ALPHA * x + mixed @ w_out[layer], ln1_g[layer], ln1_b[layer])
        ffn = hierarchical_moe(x, moe_wg[layer], moe_bg[layer], moe_we[layer], moe_be[layer],
                               moe_w1[layer], moe_w3[layer], moe_w2[layer])
        x = layer_norm(ALPHA * x + ffn, ln2_g[layer], ln2_b[layer])
    return x


_drawn_inputs = setup_inputs


def setup_inputs(seed=0):
    import zlib

    import numpy as np

    out = dict(_drawn_inputs(seed))
    spreads = {}
    factors = {'na_rpb': 30.84, 'ml_conv_b': 8.0, 'ml_norm_g': 24.877, 'moe_bg': 27.087, 'moe_be': 6.489}
    for name, (base, spread) in spreads.items():
        noise = np.random.default_rng([zlib.crc32(name.encode()), seed]).standard_normal(out[name].shape)
        drawn = base * np.exp(spread * noise) if base else spread * noise
        out[name] = __import__('jax').numpy.asarray(drawn.astype(out[name].dtype))
    for name, factor in factors.items():
        out[name] = (out[name] * factor).astype(out[name].dtype)
    return out
```

```python
from contextlib import ExitStack

import concourse.bass as bass
from concourse import mybir
import numpy as np

F32 = mybir.dt.float32
I32 = mybir.dt.int32
U32 = mybir.dt.uint32
ALU = mybir.AluOpType
ACT = mybir.ActivationFunctionType
AX = mybir.AxisListType.X

P = 128
D = 1024
T = 512
TT = T // P
KT = D // P
DEPTH = 2
NMEM = 256
GRID_W = 64
ROWS = T // GRID_W
WIN_H, WIN_W = 8, 16
TOKEN_W = 768
MEM_W = 256
HD = 64
NA_HEADS = 12
ML_HEADS = 4
ML_DH = 192
VW = ML_DH + 1
CONV_K = 5
NG, EPG = 4, 8
NE = NG * EPG
FE = 512
FT = FE // P
CAP = 64
MAX_BLOCKS = NE + (2 * T - 1) // CAP + 1
LN_EPS = 1e-5
ALPHA = (2 * DEPTH) ** 0.25
NEG = -1e30

QC = 16
KC = 32
NBLK = GRID_W // QC
KEY0 = [min(max(QC * b - WIN_W // 2, 0), GRID_W - KC) for b in range(NBLK)]
SHIFT = [KEY0[b] - QC * b + 16 for b in range(NBLK)]
VARIANT = [0, 1, 1, 2]
RPB_ROW = 2 * WIN_W - 1
RPB_HEAD = (2 * WIN_H - 1) * RPB_ROW
RPB_RUN = (ROWS - 1) * RPB_ROW + 48
RPB_PAD = 64

CHUNK = 2176


def constants():
    p = np.arange(P)
    ident = np.eye(P)
    anti = ident[::-1]
    earlier = (p[:, None] < p[None, :]) * 1.0
    ones = np.ones((P, P))
    na = np.zeros((P, 3, KC))
    for b in (0, 1, 3):
        c = QC * b + 15 - p % QC
        start = np.clip(c - WIN_W // 2, 0, GRID_W - WIN_W)[:, None]
        kc = KEY0[b] + np.arange(KC)[None, :]
        na[:, VARIANT[b], :] = np.where((kc >= start) & (kc < start + WIN_W), 0.0, NEG)
    fwd = np.where(p[None, :] >= p[:, None], 0.0, NEG)
    bwd = np.where(p[None, :] <= p[:, None], 0.0, NEG)
    count = np.tile(np.arange(NE), (P, 1)) * 1.0
    f = np.concatenate([ident, anti, earlier, ones, na.reshape(P, -1), fwd, bwd, count], axis=1).astype(np.float32)
    tokens = (np.arange(TT)[None, :] * P + p[:, None]).astype(np.int32)
    return f, tokens


class Jobs:

    def __init__(self, order):
        self.number, self.engine, self.ordinal = {}, {}, {}
        self.by = []
        seen = {"act": 0, "dve": 0}
        for n, (name, engine) in enumerate(order):
            seen[engine] += 1
            self.number[name], self.engine[name], self.ordinal[name] = n, engine, seen[engine]
            self.by.append(name)


def chunk_list(layer):
    if layer == 0:
        return ([("v", c, 2 * TOKEN_W + 256 * c, 256) for c in range(3)]
                + [("q", c, 256 * c, 256) for c in range(3)]
                + [("k", c, TOKEN_W + 256 * c, 256) for c in range(3)] + [("m", 0, 3 * TOKEN_W, 256)])
    return ([("q", c, 256 * c, 256) for c in range(3)] + [("k", c, TOKEN_W + 256 * c, 256) for c in range(3)]
            + [("m", 0, 4 * TOKEN_W, 16 + 256)]
            + [("v", c, 2 * TOKEN_W + 256 * c, 256) for c in range(3)]
            + [("o", c, 3 * TOKEN_W + 256 * c, 256) for c in range(3)])


def job_order(layer):
    order = [(("xT", k), ("act", "dve")[k % 2]) for k in range(KT)]
    if layer == 0:
        order += [(("memT", k), ("act", "dve")[k % 2]) for k in range(4)]
        order += [(("memk", 0), "act"), (("memv", 0), "dve")]
    for kind, c, _, _ in chunk_list(layer):
        if layer == 1 and kind == "m":
            order.append((("gates", 0), "dve"))
        for s in range(2):
            drain = ("act", "dve")[s] if layer == 0 else "act"
            order.append(((kind, c, s), drain))
    if layer == 1:
        order += [(("rows", 0), "dve"), (("rows", 1), "dve"), (("cols", 0), "dve")]
        order += [(("hT", i), ("act", "dve")[i % 2]) for i in range(6)]
    order += [(("out", c, s), "dve") for c in range(4) for s in range(2)]
    order += [(("x1T", k), ("act", "dve")[k % 2]) for k in range(KT)]
    order += [(("logits", 0), "dve"), (("rank", 0), "dve")]
    return order


def attention_units(layer):
    units = []
    if layer == 0:
        units += [(b, par, i, False) for b in range(NBLK) for par in range(2) for i in range(3)]
    units += [(t, par, 0, True) for t in range(TT) for par in range(2)]
    return units


def encoder(nc, x, mem, w_mem_kv, na_w_in, na_rpb, ml_w_in, ml_conv_w, ml_conv_b, ml_gate_b, ml_norm_g, w_out,
            ln1_g, ln1_b, ln2_g, ln2_b, moe_wg, moe_bg, moe_we, moe_be, moe_w1, moe_w3, moe_w2,
            const_f, const_tok, out):
    ctx = ExitStack()
    with ctx:
        ctx.enter_context(nc.allow_non_contiguous_dma("small parameters"))

        def sb(name, shape, dt=F32):
            return ctx.enter_context(nc.sbuf_tensor(name, shape, dt))

        def sem(name):
            return ctx.enter_context(nc.semaphore(name))

        def sems(name, n=DEPTH):
            return [sem(f"{name}{i}") for i in range(n)]

        def dram(name, shape, dt=F32):
            return nc.dram_tensor(name, shape, dt, kind="Internal").ap()

        rpb_pad = dram("rpb_pad", [RPB_PAD * 2 + NA_HEADS * RPB_HEAD])
        v_rows = dram("v_rows", [T, TOKEN_W])
        x_rows = dram("x_rows", [T, D])
        slot_token = dram("slot_token", [MAX_BLOCKS * CAP, 1], I32)
        y_rows = dram("y_rows", [(MAX_BLOCKS + T // CAP) * CAP, D])

        X = sb("X", [P, TT, D])
        XT = sb("XT", [P, KT, T])
        RING = sb("RING", [P, 3 * 12288])
        AREA = sb("AREA", [P, 4864])
        CF = sb("CF", [P, 128 * 4 + 96 + 256 + 32])
        ctok = sb("ctok", [P, TT], I32)
        memk = sb("memk", [P, 2, NMEM])
        memv = sb("memv", [P, 2, MEM_W])
        wr = sb("wr", [P, KT, NG + NE])
        rbias = sb("rbias", [P, NG + NE])
        gates = sb("gates", [P, TT, 2])
        dest = sb("dest", [P, TT, 2], I32)
        blk_i = sb("blk_i", [1, 2 * NE + 1], I32)
        slot_tab = sb("slot_tab", [CAP, MAX_BLOCKS], I32)
        idx_now = sb("idx_now", [CAP, 1], I32)
        zrow = sb("zrow", [1, 64])
        small = sb("small", [P, 192])
        PS = ctx.enter_context(nc.psum_tensor("PS", [P, 8, 512], F32))

        ident = CF[:, 0:128]
        anti = CF[:, 128:256]
        earlier = CF[:, 256:384]
        ones = CF[:, 384:512]
        na_mask = CF[:, 512:608].rearrange("p (v k) -> p v k", v=3)
        ml_mask = CF[:, 608:864].rearrange("p (d k) -> p d k", d=2)
        count = CF[:, 864:896]

        def ring(off, *dims):
            n = int(np.prod(dims))
            assert off + n <= 3 * 12288
            v = RING[:, off:off + n]
            if len(dims) == 2:
                v = v.rearrange("p (a b) -> p a b", b=dims[1])
            elif len(dims) == 3:
                v = v.rearrange("p (a b c) -> p a b c", b=dims[1], c=dims[2])
            return v

        qT = ring(0, 6, T)
        kT = ring(3072, 6, T)
        v_win = ring(6144, 2 * NBLK, TOKEN_W)
        bias_tab = ring(12288, 3, NA_HEADS, ROWS * KC)
        rpb_tab = ring(21504, NA_HEADS, RPB_RUN)
        v_nat = ring(24704, TT, TOKEN_W)
        o_na = ring(27776, NBLK, TOKEN_W)
        o_mem0 = ring(30848, TT, MEM_W)
        qm0 = ring(31872, 2, T)
        sneg = ring(32896, 3, 512)
        prob0 = ring(34432, 3, 512)
        probT0 = ring(24704, 2, 512)
        memT = ring(27776, KT, NMEM)
        w_kv = ring(6144, KT, 2 * MEM_W)
        zeros = ring(12288, D)
        mem_in = ring(30848, 2, D)
        qk = ring(0, 12, T)
        pre = ring(6144, 4, T + 4)
        v_ml = ring(8208, TT, ML_HEADS, VW)
        o_gate = ring(11296, TT, TOKEN_W)
        H = ring(14368, TT, TOKEN_W)
        W = ring(17440, 2, TT, T)
        E = ring(21536, 2, TT, T)
        qm1 = ring(25632, 2, T)
        Rd = ring(26656, 2, 512)
        r_F = ring(27680, T)
        r_a = ring(28192, T)
        r_M = ring(28704, T)
        r_m = ring(29216, T)
        prob1 = ring(29728, 3, 512)
        probT1 = ring(31264, 2, 512)
        o_mem1 = ring(32288, TT, MEM_W)
        norm_g = ring(33312, TOKEN_W)
        conv_w = ring(34080, 12, CONV_K)
        conv_b = ring(34140, 12)
        g_in = ring(34160, TT, 64)
        g_fo = ring(34416, TT, 64)
        g_tok = ring(34672, TT, 16)
        g_abs = ring(34736, TT, 8)
        g_ln = ring(34768, TT, 8)
        g_bias = ring(34800, 16)
        ml_st = ring(34816, 16, 6)
        ml_mv = ring(34912, 16, 2)
        ml_rstd = ring(34944, 16)
        acol = ring(34960, TT, 8)
        mcol = ring(34992, TT, 8)
        em = ring(35024, TT, 8)
        den = ring(35056, 16, 2)
        rden = ring(35088, 16, 2)
        qm, prob, probT, o_mem = [qm0, qm1], [prob0, prob1], [probT0, probT1], [o_mem0, o_mem1]
        mixT = XT

        w1_s = [RING[:, 12288 * s:12288 * s + 4096] for s in range(3)]
        w3_s = [RING[:, 12288 * s + 4096:12288 * s + 8192] for s in range(3)]
        w2_s = [RING[:, 12288 * s + 8192:12288 * (s + 1)] for s in range(3)]
        y_got = ring(24576, 2 * TT, D)
        ln2_p = ring(24576 + 8192, 2, D)

        chunk_buf = [AREA[:, CHUNK * i:CHUNK * (i + 1)] for i in range(2)]
        xg = AREA[0:CAP, 0:1024]
        xgT = AREA[:, 1024:1536].rearrange("p (k s) -> p k s", s=CAP)
        hs = AREA[:, 1536:1792]
        hT = AREA[:, 1792:2048].rearrange("p (k s) -> p k s", s=CAP)
        yT = AREA[:, 2048:2560].rearrange("p (k s) -> p k s", s=CAP)
        y_blk = AREA[0:CAP, 2560:3584]

        msum = sb("msum", [P, 40, 2])
        mneg = sb("mneg", [P, 40, 2])
        mraw = sb("mraw", [P, 8, 2])
        rsum = small[:, 0:16].rearrange("p (a b) -> p a b", b=8)
        ln_st = small[:, 16:64].rearrange("p (t a s) -> p t a s", t=TT, a=2)
        ln_mv = small[:, 64:72].rearrange("p (t s) -> p t s", s=2)
        ln_ve = small[:, 72:76]
        ln_sd = small[:, 76:80]
        ln_rs = small[:, 80:84]

        const_in, x_in, mem_in_s, kv_in = sem("const_in"), sem("x_in"), sem("mem_in_s"), sem("kv_in")
        zero_set, pads_in, rpb_in, mlp_in = sem("zero_set"), sem("pads_in"), sem("rpb_in"), sem("mlp_in")
        slots_zeroed, zeros_set, y_zeroed = sem("slots_zeroed"), sem("zeros_set"), sem("y_zeroed")
        v_out, v_in, bias_built = sem("v_out"), sem("v_in"), sem("bias_built")
        chunk_in = [sems(f"chunk_in_l{l}_", 2) for l in range(DEPTH)]
        ln_in, ln2_in, route_in = sems("ln_in"), sems("ln2_in"), sems("route_in")
        bank_full = sems("bank_full")
        act_drained, dve_drained = sems("act_drained"), sems("dve_drained")
        scores_full, max_ready, probs_ready = sems("scores_full"), sems("max_ready"), sems("probs_ready")
        probsT_full, probsT_ready, values_summed = sems("probsT_full"), sems("probsT_ready"), sems("values_summed")
        heads_ready, mix_full, mix_ready = sems("heads_ready"), sems("mix_full"), sems("mix_ready")
        dve_step, act_step, pool_step = sem("dve_step"), sem("act_step"), sem("pool_step")
        pads_zero = sem("pads_zero")
        conv_done, silu_done, o_scaled = sem("conv_done"), sem("silu_done"), sem("o_scaled")
        lf_abs, lf_ln, gates_set = sem("lf_abs"), sem("lf_ln"), sem("gates_set")
        rows_set, mcol_set, em_set = sem("rows_set"), sem("mcol_set"), sem("em_set")
        r_full, r_masked, e_ready = sem("r_full"), sem("r_masked"), sem("e_ready")
        s_full, w_ready, num_full, h_added = sem("s_full"), sem("w_ready"), sem("num_full"), sem("h_added")
        ml_var, ml_sd, h_ready = sem("ml_var"), sem("ml_sd"), sem("h_ready")
        var_ready, sd_ready, scaled, x1_ready = sems("var_ready"), sems("sd_ready"), sems("scaled"), sems("x1_ready")
        var2_ready, sd2_ready, scaled2, x2_ready = sems("var2_ready"), sems("sd2_ready"), sems("scaled2"), sems("x2_ready")
        gdiff, gexp, ediff, eexp = sems("gdiff"), sems("gexp"), sems("ediff"), sems("eexp")
        picks_ready, blocks_ready, dest_ready = sems("picks_ready"), sems("blocks_ready"), sems("dest_ready")
        x_stored, slots_set, slots_in = sems("x_stored"), sems("slots_set"), sems("slots_in")
        idx_set, x_gathered = sems("idx_set"), sems("x_gathered")
        xgT_full, xgT_ready = sems("xgT_full"), sems("xgT_ready")
        h1_full, h3_full, silu_ready, hT_ready = sems("h1_full"), sems("h3_full"), sems("silu_ready"), sems("hT_ready")
        yT_full, yT_ready, y_full, y_ready, y_stored = (sems("yT_full"), sems("yT_ready"), sems("y_full"),
                                                       sems("y_ready"), sems("y_stored"))
        w13_in = [sems(f"w13_in_l{l}_", 3) for l in range(DEPTH)]
        w2_in = [sems(f"w2_in_l{l}_", 3) for l in range(DEPTH)]
        y_got_in = [sems(f"y_got_in_l{l}_", TT) for l in range(DEPTH)]
        out_done = sem("out_done")

        jobs = [Jobs(job_order(l)) for l in range(DEPTH)]
        units = [attention_units(l) for l in range(DEPTH)]
        chunks = [chunk_list(l) for l in range(DEPTH)]
        n_proj = [len(c) for c in chunks]

        def bank_of(l, name):
            return PS[:, jobs[l].number[name] % 8, :]

        def wait_drained(eng, l, name):
            s = act_drained if jobs[l].engine[name] == "act" else dve_drained
            eng.wait_ge(s[l], jobs[l].ordinal[name])

        def wait_full(eng, l, name):
            eng.wait_ge(bank_full[l], jobs[l].number[name] + 1)

        def last_mix_round(l, blk_index):
            return sum(1 if m else 2 for m in block_kinds(l)[:blk_index + 1])

        def block_kinds(l):
            return ([False] * NBLK if l == 0 else []) + [True] * TT

        def block_no(l, unit):
            b, _, _, is_mem = unit
            return b + (NBLK if l == 0 and is_mem else 0)

        def steps(l):
            us = units[l]
            for i in range(len(us) + 6):
                at = lambda lag: us[i - lag] if 0 <= i - lag < len(us) else None
                yield i, at

        def ends_group(u):
            return u is not None and (u[3] or u[2] == 2)

        def group_no(l, u):
            return 2 * block_no(l, u) + u[1]

        def experts_use(e):
            return (e + 3) // 3

        def routing_views(l):
            base = chunk_buf[(n_proj[l] + 3) % 2]
            views, at = {}, 0
            for name, dims in (("lg", (TT, 36)), ("gp", (TT, 8)), ("gm", (TT, 8)), ("gi", (TT, 8)), ("gd", (TT, 4)),
                               ("ge", (TT, 4)), ("z", (TT, 1)), ("gif", (TT, 1)), ("oh", (TT, 4)),
                               ("prod", (TT, NG, EPG)), ("es", (TT, 8)), ("e8", (TT, 8)), ("ei", (TT, 8)),
                               ("ed", (TT, 1)), ("e2", (TT, 1)), ("dn", (TT, 1)), ("eif", (TT, 2)), ("eid", (TT, 2)),
                               ("pick", (TT, 2, NE)), ("picks", (TT, NE)), ("ci", (NE,)), ("cs", (NE,)),
                               ("nb", (NE,)), ("inc", (NE,)), ("ex", (NE,)), ("slot", (TT, NE)), ("ps", (TT, 2, NE)),
                               ("df", (TT, 2))):
                n = int(np.prod(dims))
                v = base[:, at:at + n]
                if name in ("gi", "ei"):
                    v = v.bitcast(U32)
                if name in ("ci", "cs"):
                    v = v.bitcast(I32)
                if len(dims) == 2:
                    v = v.rearrange("p (a b) -> p a b", b=dims[1])
                elif len(dims) == 3:
                    v = v.rearrange("p (a b c) -> p a b c", b=dims[1], c=dims[2])
                views[name] = v
                at += n
            assert at <= CHUNK
            return views

        def ln1_params(l):
            return chunk_buf[(n_proj[l] + 2) % 2][:, 0:2 * D].rearrange("p (a d) -> p a d", d=D)

        def settle(eng):
            eng.wait_ge(const_in, 32)

        block = ctx.enter_context(nc.Block())

        @block.tensor
        def _(pe):
            def begin(l, name):
                n = jobs[l].number[name]
                if n >= 8:
                    wait_drained(pe, l, jobs[l].by[n - 8])
                return bank_of(l, name)

            def transposed_x(l, kind):
                for k in range(KT):
                    bank = begin(l, (kind, k))
                    for t in range(TT):
                        mm = nc.tensor.transpose(bank[:, t * P:(t + 1) * P], X[:, t, k * P:(k + 1) * P], ident)
                    mm.then_inc(bank_full[l], 1)

            def memory_kv():
                pe.wait_ge(mem_in_s, 16)
                for k2 in range(4):
                    bank = begin(0, ("memT", k2))
                    for kk in range(2):
                        for m in range(2):
                            k = 2 * k2 + kk
                            mm = nc.tensor.transpose(bank[:, kk * NMEM + m * P:kk * NMEM + (m + 1) * P],
                                                     mem_in[:, m, k * P:(k + 1) * P], ident)
                    mm.then_inc(bank_full[0], 1)
                pe.wait_ge(kv_in, 16)
                wait_drained(pe, 0, ("memT", 2))
                wait_drained(pe, 0, ("memT", 3))
                bank = begin(0, ("memk", 0))
                for i in range(2):
                    for k in range(KT):
                        mm = nc.tensor.matmul(bank[:, i * NMEM:(i + 1) * NMEM], w_kv[:, k, i * P:(i + 1) * P],
                                              memT[:, k, :], start=(k == 0), stop=(k == KT - 1))
                mm.then_inc(bank_full[0], 1)
                bank = begin(0, ("memv", 0))
                for m in range(2):
                    for k in range(KT):
                        mm = nc.tensor.matmul(bank[:, m * MEM_W:(m + 1) * MEM_W], memT[:, k, m * P:(m + 1) * P],
                                              w_kv[:, k, MEM_W:2 * MEM_W], start=(k == 0), stop=(k == KT - 1))
                mm.then_inc(bank_full[0], 1)

            def projection(l):
                wait_drained(pe, l, ("xT", KT - 2))
                wait_drained(pe, l, ("xT", KT - 1))
                for c, (kind, i, _, width) in enumerate(chunks[l]):
                    pe.wait_ge(chunk_in[l][c % 2], 16 * (c // 2 + 1))
                    w = chunk_buf[c % 2][:, 0:KT * width].rearrange("p (k f) -> p k f", f=width)
                    first = width - 256
                    if first:
                        bank = begin(l, ("gates", 0))
                        for t in range(TT):
                            for k in range(KT):
                                mm = nc.tensor.matmul(bank[:, 16 * t:16 * t + 16], XT[:, k, t * P:(t + 1) * P],
                                                      w[:, k, 0:16], start=(k == 0), stop=(k == KT - 1))
                        mm.then_inc(bank_full[l], 1)
                    for s in range(2):
                        bank = begin(l, (kind, i, s))
                        if kind in "qkm":
                            for k in range(KT):
                                mm = nc.tensor.matmul(bank, w[:, k, first + s * P:first + (s + 1) * P], XT[:, k, :],
                                                      start=(k == 0), stop=(k == KT - 1))
                        else:
                            for j in range(2):
                                t = 2 * s + j
                                for k in range(KT):
                                    mm = nc.tensor.matmul(bank[:, 256 * j:256 * j + 256],
                                                          XT[:, k, t * P:(t + 1) * P], w[:, k, 0:256],
                                                          start=(k == 0), stop=(k == KT - 1))
                        mm.then_inc(bank_full[l], 1)

            def attention(l):
                def scores(n, u):
                    b, par, i, is_mem = u
                    lo = HD * par
                    if n >= 3:
                        pe.wait_ge(probs_ready[l], 2 * (n - 2))
                    bank = PS[:, (0, 1, 7)[n % 3], :]
                    if l == 0 and n == 0:
                        wait_drained(pe, 0, ("k", 2, 0)), wait_drained(pe, 0, ("k", 2, 1))
                    if is_mem:
                        wait_drained(pe, l, ("m", 0, 0)), wait_drained(pe, l, ("m", 0, 1))
                    for j in range(2):
                        if is_mem:
                            mm = nc.tensor.matmul(bank[:, 256 * j:256 * j + 256],
                                                  qm[l][lo:lo + HD, j, b * P:(b + 1) * P],
                                                  memk[lo:lo + HD, j, :], start=True, stop=True)
                        else:
                            tile = 2 * i + j
                            keys = kT[lo:lo + HD, tile, :].rearrange("p (r c) -> p r c", c=GRID_W)
                            mm = nc.tensor.matmul(bank[:, 256 * j:256 * j + 256],
                                                  qT[lo:lo + HD, tile, b * P:(b + 1) * P],
                                                  keys[:, :, KEY0[b]:KEY0[b] + KC], start=True, stop=True)
                    mm.then_inc(scores_full[l], 1)

                def turn(n, u):
                    pe.wait_ge(probs_ready[l], 2 * (n + 1))
                    if n >= 2:
                        pe.wait_ge(probsT_ready[l], n - 1)
                    for j in range(4):
                        mm = nc.tensor.transpose(PS[:, 2 + n % 2, j * P:(j + 1) * P],
                                                 prob[l][:, n % 3, j * P:(j + 1) * P], ident)
                    mm.then_inc(probsT_full[l], 1)

                def values(n, u):
                    b, par, i, is_mem = u
                    pe.wait_ge(probsT_ready[l], n + 1)
                    if (is_mem or i == 0) and group_no(l, u) >= 2:
                        pe.wait_ge(heads_ready[l], group_no(l, u) - 1)
                    if l == 0 and n == 0:
                        pe.wait_ge(v_in, 16 * 2 * NBLK)
                    for j in range(2):
                        dst = PS[:, 4 + par, (2 * i + j) * HD:(2 * i + j + 1) * HD]
                        h = 2 * (2 * i + j) + par
                        for kt in range(2):
                            vals = (memv[:, kt, h * HD:(h + 1) * HD] if is_mem
                                    else v_win[:, 2 * b + kt, h * HD:(h + 1) * HD])
                            mm = nc.tensor.matmul(dst, probT[l][:, n % 2, (2 * j + kt) * P:(2 * j + kt + 1) * P], vals,
                                                  start=(kt == 0), stop=(kt == 1))
                    mm.then_inc(values_summed[l], 1)

                def mix(u):
                    b, par, _, is_mem = u
                    pe.wait_ge(heads_ready[l], group_no(l, u) + 1)
                    done = last_mix_round(l, block_no(l, u) - 1) if block_no(l, u) else 0
                    for r in range(1 if is_mem else 2):
                        if done + r:
                            pe.wait_ge(mix_ready[l], done + r)
                        for i in range(2 if is_mem else 3):
                            f = (3 * r + i) * P
                            src = o_mem[l][:, b, f:f + P] if is_mem else o_na[:, b, f:f + P]
                            mm = nc.tensor.matmul(PS[:, 6, i * P:(i + 1) * P], src, ident if is_mem else anti,
                                                  start=True, stop=True)
                        mm.then_inc(mix_full[l], 1)

                for s, at in steps(l):
                    if at(0):
                        scores(s, at(0))
                    if at(2):
                        turn(s - 2, at(2))
                    if at(3):
                        values(s - 3, at(3))
                    if ends_group(at(5)) and at(5)[1] == 1:
                        mix(at(5))

            def mlstm():
                j = jobs[1]
                for r, src in enumerate((g_in, g_fo)):
                    if r == 0:
                        pe.wait_ge(gates_set, 3)
                    bank = begin(1, ("rows", r))
                    for t in range(TT):
                        mm = nc.tensor.transpose(bank[0:64, t * P:(t + 1) * P], src[:, t, :], ident)
                    mm.then_inc(bank_full[1], 1)
                pe.wait_ge(rows_set, 1)
                bank = begin(1, ("cols", 0))
                for g, src in enumerate((r_a, r_m)):
                    for t in range(TT):
                        mm = nc.tensor.transpose(bank[:, g * 256 + t * 64:g * 256 + (t + 1) * 64],
                                                 src[0:64, t * P:(t + 1) * P], ident[0:64, 0:64])
                mm.then_inc(bank_full[1], 1)
                wait_drained(pe, 1, ("cols", 0))
                pe.wait_ge(silu_done, 12)
                parts = [[(0, 0, 128), (1, 0, 64)], [(1, 64, 128), (2, 0, 128)],
                         [(3, 0, 128), (4, 0, 64)], [(4, 64, 128), (5, 0, 128)]]
                for h in range(ML_HEADS + 1):
                    if h < ML_HEADS:
                        for d in range(2):
                            n = 2 * h + d
                            if n >= 2:
                                pe.wait_ge(e_ready, n - 1)
                            row = 32 * d + h
                            nc.tensor.matmul(PS[:, (0, 7)[d], :], ident[0:64, row:row + 1].to_broadcast([64, P]),
                                             r_M[0:64, :], start=True, stop=True).then_inc(r_full, 1)
                        for i in range(TT):
                            if h:
                                pe.wait_ge(w_ready, TT * (h - 1) + i + 1)
                            for a, (tile, lo, hi) in enumerate(parts[h]):
                                mm = nc.tensor.matmul(PS[:, 1 + i, :], qk[lo:hi, 6 + tile, i * P:(i + 1) * P],
                                                      qk[lo:hi, tile, :], start=(a == 0), stop=(a == 1))
                            mm.then_inc(s_full, 1)
                    if h >= 1:
                        g = h - 1
                        pe.wait_ge(w_ready, TT * (g + 1))
                        for t in range(TT):
                            n = TT * g + t
                            if n >= 2:
                                pe.wait_ge(h_added, n - 1)
                            bank = PS[:, 5 + n % 2, :]
                            for d in range(2):
                                tiles = range(0, t + 1) if d == 0 else range(t, TT)
                                for i in tiles:
                                    mm = nc.tensor.matmul(bank[:, 256 * d:256 * d + VW], W[:, d, i, t * P:(t + 1) * P],
                                                          v_ml[:, i, g, :], start=(i == tiles[0]), stop=(i == tiles[-1]))
                            mm.then_inc(num_full, 1)
                pe.wait_ge(h_ready, TT)
                for i in range(6):
                    bank = begin(1, ("hT", i))
                    for t in range(TT):
                        mm = nc.tensor.transpose(bank[:, t * P:(t + 1) * P], H[:, t, i * P:(i + 1) * P], ident)
                    mm.then_inc(bank_full[1], 1)
                wait_drained(pe, 1, ("hT", 4))
                wait_drained(pe, 1, ("hT", 5))

            def output_projection(l):
                for c in range(4):
                    n = n_proj[l] + c
                    pe.wait_ge(chunk_in[l][n % 2], 16 * (n // 2 + 1))
                    w = chunk_buf[n % 2][:, 0:KT * 256].rearrange("p (k f) -> p k f", f=256)
                    for s in range(2):
                        bank = begin(l, ("out", c, s))
                        for j in range(2):
                            t = 2 * s + j
                            for k in range(KT):
                                mm = nc.tensor.matmul(bank[:, 256 * j:256 * j + 256], mixT[:, k, t * P:(t + 1) * P],
                                                      w[:, k, :], start=(k == 0), stop=(k == KT - 1))
                        mm.then_inc(bank_full[l], 1)

            def routing(l, picks):
                pe.wait_ge(route_in[l], 64)
                wait_drained(pe, l, ("x1T", KT - 2))
                wait_drained(pe, l, ("x1T", KT - 1))
                bank = begin(l, ("logits", 0))
                for t in range(TT):
                    for k in range(KT):
                        mm = nc.tensor.matmul(bank[:, 36 * t:36 * t + 36], XT[:, k, t * P:(t + 1) * P], wr[:, k, :],
                                              start=(k == 0), stop=(k == KT - 1))
                mm.then_inc(bank_full[l], 1)
                pe.wait_ge(picks_ready[l], 1)
                bank = begin(l, ("rank", 0))
                for t in range(TT):
                    for t2 in range(t + 1):
                        nc.tensor.matmul(bank[:, NE * t:NE * t + NE], earlier if t2 == t else ones, picks[:, t2, :],
                                         start=(t2 == 0), stop=(t2 == t))
                for t in range(TT):
                    mm = nc.tensor.matmul(bank[:, NE * TT:NE * TT + NE], ones, picks[:, t, :],
                                          start=(t == 0), stop=(t == TT - 1))
                mm.then_inc(bank_full[l], 1)

            def expert(l, e, slot, use):
                n = pe.value_load(blk_i[0:1, bass.ds(e, 1)], min_val=1, max_val=T // CAP)
                g0 = pe.value_load(blk_i[0:1, bass.ds(e + NE, 1)], min_val=0, max_val=MAX_BLOCKS - 1)
                n13, n2 = (use * 32, use * 16) if isinstance(use, int) else (pe.to_reg(use * 32), pe.to_reg(use * 16))
                settle(pe)
                pe.wait_ge(w13_in[l][slot], n13)
                pe.wait_ge(w2_in[l][slot], n2)
                w1v = w1_s[slot].rearrange("p (k f) -> p k f", k=KT)
                w3v = w3_s[slot].rearrange("p (k f) -> p k f", k=KT)
                w2v = w2_s[slot].rearrange("p (k f) -> p k f", k=FT)
                with pe.Fori(0, n) as i:
                    g = g0 + i
                    gathered = pe.to_reg(16 * (g + 1))
                    settle(pe)
                    pe.wait_ge(x_gathered[l], gathered)
                    for k in range(KT):
                        mm = nc.tensor.transpose(PS[:, 0, k * CAP:(k + 1) * CAP], xg[:, k:D:KT], ident[0:CAP, 0:CAP])
                    mm.then_inc(xgT_full[l], 1)
                    pe.wait_ge(xgT_ready[l], g + 1)
                    for bank, wv, full in ((1, w1v, h1_full), (2, w3v, h3_full)):
                        for m in range(FT):
                            for k in range(KT):
                                mm = nc.tensor.matmul(PS[:, bank, m * CAP:(m + 1) * CAP], wv[:, k, m * P:(m + 1) * P],
                                                      xgT[:, k, :], start=(k == 0), stop=(k == KT - 1))
                        mm.then_inc(full[l], 1)
                    pe.wait_ge(hT_ready[l], g + 1)
                    for m in range(KT):
                        for k in range(FT):
                            mm = nc.tensor.matmul(PS[:, 3, m * CAP:(m + 1) * CAP], w2v[:, k, m * P:(m + 1) * P],
                                                  hT[:, k, :], start=(k == 0), stop=(k == FT - 1))
                    mm.then_inc(yT_full[l], 1)
                    settle(pe)
                    pe.wait_ge(yT_ready[l], g + 1)
                    pe.wait_ge(y_ready[l], g + 1)
                    for m in range(KT):
                        mm = nc.tensor.transpose(PS[0:CAP, 4 + m // 4, (m % 4) * P:(m % 4 + 1) * P], yT[:, m, :], ident)
                    mm.then_inc(y_full[l], 1)

            pe.wait_ge(const_in, 32)
            for l in range(DEPTH):
                if l == 0:
                    pe.wait_ge(x_in, 16)
                else:
                    pe.wait_ge(x2_ready[0], TT)
                transposed_x(l, "xT")
                if l == 0:
                    memory_kv()
                projection(l)
                tail = jobs[l].by[:jobs[l].number[("out", 0, 0) if l == 0 else ("rows", 0)]][-8:]
                for name in tail:
                    wait_drained(pe, l, name)
                attention(l)
                pe.wait_ge(mix_ready[l], last_mix_round(l, len(block_kinds(l)) - 1))
                if l == 1:
                    mlstm()
                output_projection(l)
                pe.wait_ge(x1_ready[l], TT)
                transposed_x(l, "x1T")
                routing(l, routing_views(l)["picks"])
                pe.wait_ge(blocks_ready[l], 1)
                wait_drained(pe, l, ("rank", 0))
                with pe.Fori(0, NE - 2, 3) as e:
                    for s in range(3):
                        expert(l, e + s, s, experts_use(e))
                expert(l, NE - 2, 0, NE // 3 + 1)
                expert(l, NE - 1, 1, NE // 3 + 1)

        w1_v = moe_w1.rearrange("l e (p k) f -> (l e) p (k f)", k=KT)
        w3_v = moe_w3.rearrange("l e (p k) f -> (l e) p (k f)", k=KT)
        w2_v = moe_w2.rearrange("l e (k p) f -> (l e) p k f", p=P)

        @block.sync
        def _(sp):
            def load_chunk(l, n):
                if n >= 2:
                    if n - 2 < n_proj[l]:
                        kind, c = chunks[l][n - 2][:2]
                        wait_full(sp, l, (kind, c, 1))
                    else:
                        wait_full(sp, l, ("out", n - 2 - n_proj[l], 1))
                elif l == 1:
                    pass
                if n < n_proj[l]:
                    _, _, col, width = chunks[l][n]
                    src = (na_w_in, ml_w_in)[l][0].rearrange("(k p) f -> p k f", p=P)[:, :, col:col + width]
                else:
                    c, width = n - n_proj[l], 256
                    src = w_out[l].rearrange("(k p) f -> p k f", p=P)[:, :, 256 * c:256 * c + 256]
                dst = chunk_buf[n % 2][:, 0:KT * width].rearrange("p (k f) -> p k f", f=width)
                sp.dma_start(dst, src).then_inc(chunk_in[l][n % 2], 16)

            def load_expert(l, e, slot):
                sp.dma_start(w1_s[slot], w1_v[bass.ds(l * NE + e, 1)].rearrange("a p n -> (a p) n"))\
                    .then_inc(w13_in[l][slot], 16)
                sp.dma_start(w3_s[slot], w3_v[bass.ds(l * NE + e, 1)].rearrange("a p n -> (a p) n"))\
                    .then_inc(w13_in[l][slot], 16)
                sp.dma_start(w2_s[slot].rearrange("p (k f) -> p k f", k=FT),
                             w2_v[bass.ds(l * NE + e, 1)].rearrange("a p k f -> (a p) k f"))\
                    .then_inc(w2_in[l][slot], 16)

            def store_blocks(l, e):
                n = sp.value_load(blk_i[0:1, bass.ds(e, 1)], min_val=1, max_val=T // CAP)
                g0 = sp.value_load(blk_i[0:1, bass.ds(e + NE, 1)], min_val=0, max_val=MAX_BLOCKS - 1)
                with sp.Fori(0, n) as i:
                    g = g0 + i
                    sp.wait_ge(y_ready[l], g + 2)
                    sp.dma_start(y_rows[bass.ds(g * CAP, CAP), :], y_blk).then_inc(y_stored[l], 16)

            sp.dma_start(X[:], x[0].rearrange("(t p) d -> p t d", p=P)).then_inc(x_in, 16)
            sp.dma_start(CF[:], const_f).then_inc(const_in, 16)
            sp.dma_start(ctok[:], const_tok).then_inc(const_in, 16)
            sp.dma_start(mem_in, mem[0].rearrange("(m p) d -> p m d", p=P)).then_inc(mem_in_s, 16)
            sp.dma_start(w_kv, w_mem_kv.rearrange("(k p) f -> p k f", p=P)).then_inc(kv_in, 16)
            for l in range(DEPTH):
                if l == 1:
                    sp.wait_ge(x2_ready[0], TT)
                    sp.dma_start(norm_g, ml_norm_g[0:1, :].partition_broadcast(P)).then_inc(mlp_in, 16)
                    sp.dma_start(g_bias, ml_gate_b.rearrange("a j h -> a (j h)")[0:1, :].partition_broadcast(P))\
                        .then_inc(mlp_in, 16)
                    for j in range(CONV_K):
                        sp.dma_start(conv_w[:, :, j], ml_conv_w[0, j].rearrange("(m p) -> p m", p=P)).then_inc(mlp_in, 16)
                    sp.dma_start(conv_b, ml_conv_b[0].rearrange("(m p) -> p m", p=P)).then_inc(mlp_in, 16)
                for n in range(n_proj[l]):
                    load_chunk(l, n)
                    if l == 0 and n == 2:
                        sp.wait_ge(pads_in, 48)
                        for r in range(ROWS):
                            src = bass.AP(tensor=rpb_pad.tensor, offset=RPB_PAD - 16 + RPB_ROW * r,
                                          ap=[[1, QC], [RPB_HEAD, NA_HEADS], [1, RPB_RUN]])
                            sp.dma_start(rpb_tab[QC * r:QC * r + QC], src).then_inc(rpb_in, 16)
                    if l == 0 and n == 5:
                        wait_drained(sp, 0, ("v", 2, 0)), wait_drained(sp, 0, ("v", 2, 1))
                        sp.dma_start(v_rows.rearrange("(t p) f -> p t f", p=P), v_nat).then_inc(v_out, 16)
                        wait_drained(sp, 0, ("memk", 0)), wait_drained(sp, 0, ("memv", 0))
                        sp.wait_ge(v_out, 16)
                        rows = v_rows.rearrange("(r c) f -> r c f", c=GRID_W)
                        for b in range(NBLK):
                            for j in range(2):
                                sp.dma_start(v_win[:, 2 * b + j, :],
                                             rows[4 * j:4 * j + 4, KEY0[b]:KEY0[b] + KC, :]).then_inc(v_in, 16)
                load_chunk(l, n_proj[l])
                load_chunk(l, n_proj[l] + 1)
                sp.dma_start(wr[:, :, 0:NG], moe_wg[l].rearrange("(k p) g -> p k g", p=P)).then_inc(route_in[l], 16)
                sp.dma_start(wr[:, :, NG:], moe_we[l].rearrange("(k p) g -> p k g", p=P)).then_inc(route_in[l], 16)
                sp.dma_start(rbias[:, 0:NG], moe_bg[l:l + 1, :].partition_broadcast(P)).then_inc(route_in[l], 16)
                sp.dma_start(rbias[:, NG:], moe_be[l:l + 1, :].partition_broadcast(P)).then_inc(route_in[l], 16)
                if l == 0:
                    sp.wait_ge(mix_ready[l], last_mix_round(l, len(block_kinds(l)) - 1))
                else:
                    wait_full(sp, l, ("hT", 5))
                load_chunk(l, n_proj[l] + 2)
                load_expert(l, 0, 0)
                load_chunk(l, n_proj[l] + 3)
                load_expert(l, 1, 1)
                wait_full(sp, l, ("out", 2, 1))
                params = ln1_params(l)
                sp.dma_start(params[:, 0, :], ln1_g[l:l + 1, :].partition_broadcast(P)).then_inc(ln_in[l], 16)
                sp.dma_start(params[:, 1, :], ln1_b[l:l + 1, :].partition_broadcast(P)).then_inc(ln_in[l], 16)
                load_expert(l, 2, 2)
                sp.sem_inc(y_stored[l], 16)
                sp.wait_ge(blocks_ready[l], 1)
                with sp.Fori(0, NE - 5, 3) as e:
                    for s in range(3):
                        store_blocks(l, e + s)
                        load_expert(l, e + s + 3, s)
                for e in range(NE - 5, NE):
                    store_blocks(l, e)
                    if e + 3 < NE:
                        load_expert(l, e + 3, e % 3)
                    if e == NE - 3:
                        sp.dma_start(ln2_p[:, 0, :], ln2_g[l:l + 1, :].partition_broadcast(P)).then_inc(ln2_in[l], 16)
                        sp.dma_start(ln2_p[:, 1, :], ln2_b[l:l + 1, :].partition_broadcast(P)).then_inc(ln2_in[l], 16)
            for t in range(TT):
                sp.wait_ge(x2_ready[1], t + 1)
                sp.dma_start(out[0, t * P:(t + 1) * P, :], X[:, t, :]).then_inc(out_done, 16)
            sp.wait_ge(out_done, 16 * TT)

        @block.scalar
        def _(act):
            def drain(l, name, dst, func=ACT.Copy):
                wait_full(act, l, name)
                nc.scalar.activation(dst, bank_of(l, name), func).then_inc(act_drained[l], 1)

            def blocked(dst):
                return dst.rearrange("p (b r c) -> p b r c", r=ROWS, c=QC)

            def attention(l):
                for s, at in steps(l):
                    u = at(0)
                    if u:
                        if s >= 3:
                            act.wait_ge(probsT_full[l], s - 2)
                        act.wait_ge(max_ready[l], s + 1)
                        for j in range(2):
                            src = PS[:, (0, 1, 7)[s % 3], 256 * j:256 * j + 256] if u[3] \
                                else sneg[:, s % 3, 256 * j:256 * j + 256]
                            nc.scalar.activation(prob[l][:, s % 3, 256 * j:256 * j + 256], src, ACT.Exp,
                                                 bias=mneg[:, s, j:j + 1], scale=HD ** -0.5 if u[3] else -1.0,
                                                 accum_out=msum[:, s, j:j + 1]).then_inc(probs_ready[l], 1)
                    if at(2):
                        n = s - 2
                        act.wait_ge(probsT_full[l], n + 1)
                        if n >= 2:
                            act.wait_ge(values_summed[l], n - 1)
                        nc.scalar.activation(probT[l][:, n % 2, :], PS[:, 2 + n % 2, :], ACT.Copy)\
                            .then_inc(probsT_ready[l], 1)

            def square_root(var, sd, ready, done):
                act.wait_ge(ready, 1)
                nc.scalar.activation(sd, var, ACT.Sqrt).then_inc(done, 1)

            for l in range(DEPTH):
                for k in range(0, KT, 2):
                    drain(l, ("xT", k), XT[:, k, :])
                if l == 0:
                    for k2 in (0, 2):
                        drain(0, ("memT", k2), memT[:, 2 * k2:2 * k2 + 2, :].rearrange("p a b -> p (a b)"))
                    drain(0, ("memk", 0), memk[:].rearrange("p a b -> p (a b)"))
                    for kind, c, _, _ in chunks[0]:
                        name = (kind, c, 0)
                        wait_full(act, 0, name)
                        bank = bank_of(0, name)
                        if kind == "v":
                            ins = nc.scalar.activation(v_nat[:, 0:2, 256 * c:256 * c + 256],
                                                       bank.rearrange("p (t f) -> p t f", t=2), ACT.Copy)
                        elif kind == "q":
                            ins = nc.scalar.activation(
                                blocked(qT[:, 2 * c, :]),
                                bank.rearrange("p (r b c) -> p b r c", b=NBLK, c=QC)[:, :, ::-1, ::-1], ACT.Copy)
                        elif kind == "k":
                            ins = nc.scalar.activation(kT[:, 2 * c, :], bank, ACT.Copy)
                        else:
                            ins = nc.scalar.activation(qm0[:, 0, :], bank, ACT.Copy)
                        ins.then_inc(act_drained[0], 1)
                else:
                    def silu(m):
                        act.wait_ge(conv_done, m + 1)
                        nc.scalar.activation(qk[:, m, :], qk[:, m, :], ACT.Silu).then_inc(silu_done, 1)

                    act.wait_ge(pads_zero, 1)
                    for m in range(12):
                        if m >= 4:
                            act.wait_ge(conv_done, m - 3)
                        kind, c, s = "qk"[m // 6], (m % 6) // 2, m % 2
                        drain(1, (kind, c, s), pre[:, m % 4, 2:T + 2])
                        if m >= 2:
                            silu(m - 2)
                    for s in range(2):
                        drain(1, ("m", 0, s), qm1[:, s, :])
                    silu(10)
                    silu(11)
                    for c in range(3):
                        for s in range(2):
                            name = ("v", c, s)
                            wait_full(act, 1, name)
                            bank = bank_of(1, name).rearrange("p (t f) -> p t f", t=2)
                            lo = 256 * c
                            while lo < 256 * c + 256:
                                h = lo // ML_DH
                                hi = min(256 * c + 256, ML_DH * (h + 1))
                                ins = nc.scalar.activation(
                                    v_ml[:, 2 * s:2 * s + 2, h, lo - ML_DH * h:hi - ML_DH * h],
                                    bank[:, :, lo - 256 * c:hi - 256 * c], ACT.Copy)
                                lo = hi
                            ins.then_inc(act_drained[1], 1)
                    for c in range(3):
                        for s in range(2):
                            name = ("o", c, s)
                            wait_full(act, 1, name)
                            nc.scalar.activation(o_gate[:, 2 * s:2 * s + 2, 256 * c:256 * c + 256],
                                                 bank_of(1, name).rearrange("p (t f) -> p t f", t=2), ACT.Sigmoid)\
                                .then_inc(act_drained[1], 1)
                    act.wait_ge(lf_abs, 1)
                    nc.scalar.activation(g_abs, g_abs, ACT.Exp, scale=-1.0).then_inc(lf_ln, 1)
                    act.wait_ge(lf_abs, 2)
                    nc.scalar.activation(g_ln, g_abs, ACT.Ln).then_inc(lf_ln, 1)
                attention(l)
                if l == 1:
                    act.wait_ge(mcol_set, 1)
                    nc.scalar.activation(em, mcol, ACT.Exp, scale=-1.0).then_inc(em_set, 1)
                    for h in range(ML_HEADS):
                        for d in range(2):
                            n = 2 * h + d
                            act.wait_ge(r_masked, n + 1)
                            if h:
                                act.wait_ge(w_ready, TT * h)
                            for i in range(TT):
                                col = acol[:, i, 4 * d + h:4 * d + h + 1]
                                lo, hi = (i + 1, TT) if d == 0 else (0, i)
                                if hi > lo:
                                    nc.scalar.activation(E[:, d, i, lo * P:hi * P], PS[:, (0, 7)[d], lo * P:hi * P],
                                                         ACT.Exp, bias=col)
                                ins = nc.scalar.activation(E[:, d, i, i * P:(i + 1) * P], Rd[:, d, i * P:(i + 1) * P],
                                                           ACT.Exp, bias=col)
                            ins.then_inc(e_ready, 1)
                    square_root(ml_rstd, ml_rstd, ml_var, ml_sd)
                    for i in range(0, 6, 2):
                        drain(1, ("hT", i), mixT[:, i, :])
                square_root(ln_ve, ln_sd, var_ready[l], sd_ready[l])
                for t in range(TT):
                    act.wait_ge(x1_ready[l], t + 1)
                    act.dma_start(x_rows[t * P:(t + 1) * P, :], X[:, t, :]).then_inc(x_stored[l], 16)
                for k in range(0, KT, 2):
                    drain(l, ("x1T", k), XT[:, k, :])
                rv = routing_views(l)
                act.wait_ge(gdiff[l], 1)
                nc.scalar.activation(rv["ge"], rv["gd"], ACT.Exp).then_inc(gexp[l], 1)
                act.wait_ge(ediff[l], 1)
                nc.scalar.activation(rv["e2"], rv["ed"], ACT.Exp).then_inc(eexp[l], 1)

                def expert(e):
                    n = act.value_load(blk_i[0:1, bass.ds(e, 1)], min_val=1, max_val=T // CAP)
                    g0 = act.value_load(blk_i[0:1, bass.ds(e + NE, 1)], min_val=0, max_val=MAX_BLOCKS - 1)
                    with act.Fori(0, n) as i:
                        g = g0 + i
                        act.wait_ge(xgT_full[l], g + 1)
                        nc.scalar.activation(xgT.rearrange("p k s -> p (k s)"), PS[:, 0, :], ACT.Copy)\
                            .then_inc(xgT_ready[l], 1)
                        act.wait_ge(h1_full[l], g + 1)
                        nc.scalar.activation(hs, PS[:, 1, 0:FT * CAP], ACT.Silu).then_inc(silu_ready[l], 1)
                        act.wait_ge(yT_full[l], g + 1)
                        nc.scalar.activation(yT.rearrange("p k s -> p (k s)"), PS[:, 3, :], ACT.Copy)\
                            .then_inc(yT_ready[l], 1)

                act.wait_ge(blocks_ready[l], 1)
                with act.Fori(0, NE) as e:
                    expert(e)
                square_root(ln_ve, ln_sd, var2_ready[l], sd2_ready[l])

        @block.vector
        def _(dve):
            done = [0]

            def link(ins):
                done[0] += 1
                ins.then_inc(dve_step, 1)
                dve.wait_ge(dve_step, done[0])

            def drain(l, name, dst):
                wait_full(dve, l, name)
                nc.vector.tensor_copy(dst, bank_of(l, name)).then_inc(dve_drained[l], 1)

            def softmax_front(l, n, u):
                b, par, i, is_mem = u
                dve.wait_ge(scores_full[l], n + 1)
                bank = PS[:, (0, 1, 7)[n % 3], :].rearrange("p (j k) -> p j k", j=2)
                if is_mem:
                    m = n % 8
                    link(nc.vector.tensor_reduce(mraw[:, m, :], bank, AX, ALU.max))
                    nc.vector.tensor_scalar(mneg[:, n, :], mraw[:, m, :], -(HD ** -0.5), None, ALU.mult)\
                        .then_inc(max_ready[l], 1)
                    return
                if n >= 3:
                    dve.wait_ge(probs_ready[l], 2 * (n - 2))
                if n == 0:
                    dve.wait_ge(bias_built, 3)
                h = 4 * i + par
                dst = sneg[:, n % 3, :].rearrange("p (j k) -> p j k", j=2)
                link(nc.vector.scalar_tensor_tensor(
                    out=dst, in0=bank, scalar=-(HD ** -0.5), in1=bias_tab[:, VARIANT[b], h:h + 3:2, :],
                    op0=ALU.mult, op1=ALU.subtract))
                nc.vector.tensor_reduce(mneg[:, n, :], dst, AX, ALU.min).then_inc(max_ready[l], 1)

            def heads_out(l, n, u):
                b, par, i, is_mem = u
                k = 2 if is_mem else 6
                first = n - (0 if is_mem else 2)
                dve.wait_ge(probs_ready[l], 2 * (n + 1))
                r = rsum[:, group_no(l, u) % 2, 0:k]
                link(nc.vector.reciprocal(r, msum[:, first:n + 1, :].rearrange("p a b -> p (a b)")))
                dve.wait_ge(values_summed[l], n + 1)
                dst = (o_mem[l][:, b, :] if is_mem else o_na[:, b, :]).rearrange("p (s q d) -> p s q d", q=2, d=HD)
                src = PS[:, 4 + par, 0:k * HD].rearrange("p (s d) -> p s d", d=HD)
                nc.vector.tensor_tensor(dst[:, :, par, :], src, r.unsqueeze(2).to_broadcast([P, k, HD]), ALU.mult)\
                    .then_inc(heads_ready[l], 1)

            def mix_out(l, u):
                b, _, _, is_mem = u
                done_ = last_mix_round(l, block_no(l, u) - 1) if block_no(l, u) else 0
                for r in range(1 if is_mem else 2):
                    dve.wait_ge(mix_full[l], done_ + r + 1)
                    if is_mem:
                        ins = nc.vector.tensor_copy(mixT[:, 6:8, b * P:(b + 1) * P],
                                                    PS[:, 6, 0:256].rearrange("p (i c) -> p i c", i=2))
                    else:
                        for i in range(3):
                            dst = mixT[:, 3 * r + i, :].rearrange("p (r c) -> p r c", c=GRID_W)[:, :, QC * b:QC * b + QC]
                            ins = nc.vector.tensor_copy(dst, PS[:, 6, i * P:(i + 1) * P].rearrange("p (r c) -> p r c", c=QC))
                    ins.then_inc(mix_ready[l], 1)

            def attention(l):
                for s, at in steps(l):
                    if at(0):
                        softmax_front(l, s, at(0))
                    if ends_group(at(4)):
                        heads_out(l, s - 4, at(4))
                    if ends_group(at(5)) and at(5)[1] == 1:
                        mix_out(l, at(5))

            def norm(l, params, param_sem, var_s, sd_s, scaled_s):
                for t in range(TT):
                    for a in range(2):
                        ins = nc.vector.bn_stats(ln_st[:, t, a, :], X[:, t, 512 * a:512 * a + 512])
                link(ins)
                for t in range(TT):
                    ins = nc.vector.bn_aggr(ln_mv[:, t, :], ln_st[:, t, :, :].rearrange("p a s -> p (a s)"))
                link(ins)
                nc.vector.tensor_scalar(ln_ve, ln_mv[:, :, 1], LN_EPS, None, ALU.add).then_inc(var_s[l], 1)
                dve.wait_ge(sd_s[l], 1)
                link(nc.vector.reciprocal(ln_rs, ln_sd))
                dve.wait_ge(param_sem[l], 32)
                for t in range(TT):
                    link(nc.vector.tensor_scalar(X[:, t, :], X[:, t, :], ln_mv[:, t, 0:1], ln_rs[:, t:t + 1],
                                                 ALU.subtract, ALU.mult))
                    nc.vector.tensor_tensor(X[:, t, :], X[:, t, :], params[:, 0, :], ALU.mult).then_inc(scaled_s[l], 1)

            def gate_rows():
                wait_full(dve, 1, ("gates", 0))
                dve.wait_ge(mlp_in, 16 * 8)
                done[0] += 1
                nc.vector.tensor_tensor(g_tok, bank_of(1, ("gates", 0))[:, 0:64].rearrange("p (t g) -> p t g", t=TT),
                                        g_bias.unsqueeze(1).to_broadcast([P, TT, 16]), ALU.add)\
                    .then_inc(dve_drained[1], 1)
                done[0] -= 1
                wait_drained(dve, 1, ("gates", 0))
                nc.vector.scalar_tensor_tensor(out=g_abs, in0=g_tok[:, :, 8:16], scalar=-1.0, in1=g_tok[:, :, 8:16],
                                               op0=ALU.mult, op1=ALU.max).then_inc(lf_abs, 1)
                split = lambda v: v.rearrange("p t (a b) -> p t a b", b=32)[:, :, :, 0:4]
                dve.wait_ge(gates_set, 2)
                for dd in range(2):
                    link(nc.vector.tensor_copy(g_in[:, :, 32 * dd:32 * dd + 4], g_tok[:, :, 4 * dd:4 * dd + 4]))

            def forget_rows():
                dve.wait_ge(lf_ln, 1)
                nc.vector.tensor_scalar(g_abs, g_abs, 1.0, None, ALU.add).then_inc(lf_abs, 1)
                dve.wait_ge(lf_ln, 2)
                for dd in range(2):
                    ins = nc.vector.scalar_tensor_tensor(
                        out=g_fo[:, :, 32 * dd:32 * dd + 4], in0=g_tok[:, :, 8 + 4 * dd:12 + 4 * dd], scalar=0.0,
                        in1=g_ln[:, :, 4 * dd:4 * dd + 4], op0=ALU.min, op1=ALU.subtract)
                ins.then_inc(gates_set, 1)

            def convolve(m):
                kind, c, s = "qk"[m // 6], (m % 6) // 2, m % 2
                wait_drained(dve, 1, (kind, c, s))
                src = pre[:, m % 4, :]
                dst = qk[:, m, :]
                link(nc.vector.tensor_scalar(dst, src[:, 0:T], conv_w[:, m, 0:1], conv_b[:, m:m + 1], ALU.mult, ALU.add))
                for j in range(1, CONV_K):
                    ins = nc.vector.scalar_tensor_tensor(out=dst, in0=src[:, j:j + T], scalar=conv_w[:, m, j:j + 1],
                                                         in1=dst, op0=ALU.mult, op1=ALU.add)
                    if j < CONV_K - 1:
                        link(ins)
                ins.then_inc(conv_done, 1)

            def mlstm():
                wait_full(dve, 1, ("rows", 1))
                li, lf = bank_of(1, ("rows", 0)), bank_of(1, ("rows", 1))
                one = ones[:, 0:1]
                for lo, step in ((0, 1), (32, -1)):
                    hi = lo + 32
                    ins = nc.vector.tensor_tensor_scan(r_F[lo:hi, ::step], one[lo:hi].to_broadcast([32, T]),
                                                       lf[lo:hi, ::step], 0.0, ALU.mult, ALU.add)
                    link(ins)
                link(nc.vector.tensor_tensor(r_a[0:64, :], li[0:64, :], r_F[0:64, :], ALU.subtract))
                for lo, step in ((0, 1), (32, -1)):
                    hi = lo + 32
                    link(nc.vector.tensor_tensor_scan(r_M[lo:hi, ::step], r_a[lo:hi, ::step], r_a[lo:hi, ::step], 0.0,
                                                      ALU.max, ALU.max))
                link(nc.vector.tensor_tensor(r_m[0:64, :], r_F[0:64, :], r_M[0:64, :], ALU.add))
                nc.vector.tensor_scalar(r_M[0:64, :], r_M[0:64, :], -1.0, None, ALU.mult).then_inc(rows_set, 1)
                dve.wait_ge(rows_set, 1)
                dve.sem_inc(dve_drained[1], 2)
                wait_full(dve, 1, ("cols", 0))
                view = bank_of(1, ("cols", 0)).rearrange("p (g t a b) -> p g t a b", g=2, t=TT, b=32)
                for dd in range(2):
                    nc.vector.tensor_copy(mcol[:, :, 4 * dd:4 * dd + 4], view[:, 1, :, dd, 0:4])
                    ins = nc.vector.tensor_copy(acol[:, :, 4 * dd:4 * dd + 4], view[:, 0, :, dd, 0:4])
                ins.then_inc(dve_drained[1], 1)
                wait_drained(dve, 1, ("cols", 0))
                dve.sem_inc(mcol_set, 1)
                dve.wait_ge(em_set, 1)
                for h in range(ML_HEADS + 1):
                    if h < ML_HEADS:
                        for d in range(2):
                            n = 2 * h + d
                            dve.wait_ge(r_full, n + 1)
                            if n >= 2:
                                dve.wait_ge(e_ready, n - 1)
                            nc.vector.tensor_tensor(Rd[:, d, :].rearrange("p (t c) -> p t c", c=P),
                                                    PS[:, (0, 7)[d], :].rearrange("p (t c) -> p t c", c=P),
                                                    ml_mask[:, d:d + 1, :].to_broadcast([P, TT, P]), ALU.add)\
                                .then_inc(r_masked, 1)
                    if h >= 1:
                        g = h - 1
                        for t in range(TT):
                            n = TT * g + t
                            dve.wait_ge(num_full, n + 1)
                            bank = PS[:, 5 + n % 2, :].rearrange("p (d f) -> p d f", d=2)
                            link(nc.vector.tensor_copy(den[:, n, :], bank[:, :, ML_DH]))
                            link(nc.vector.scalar_tensor_tensor(out=den[:, n, :], in0=den[:, n, :], scalar=-1.0,
                                                                in1=den[:, n, :], op0=ALU.mult, op1=ALU.max))
                            link(nc.vector.tensor_tensor(den[:, n, :], den[:, n, :], em[:, t, g:8:4], ALU.max))
                            link(nc.vector.reciprocal(rden[:, n, :], den[:, n, :]))
                            dst = H[:, t, ML_DH * g:ML_DH * (g + 1)]
                            link(nc.vector.tensor_scalar(dst, bank[:, 0, 0:ML_DH], rden[:, n, 0:1], None, ALU.mult))
                            nc.vector.scalar_tensor_tensor(out=dst, in0=bank[:, 1, 0:ML_DH], scalar=rden[:, n, 1:2],
                                                           in1=dst, op0=ALU.mult, op1=ALU.add).then_inc(h_added, 1)
                    if h < ML_HEADS:
                        dve.wait_ge(e_ready, 2 * h + 2)
                        for i in range(TT):
                            dve.wait_ge(s_full, TT * h + i + 1)
                            for d in range(2):
                                lo, hi = (i, TT) if d == 0 else (0, i + 1)
                                ins = nc.vector.scalar_tensor_tensor(
                                    out=W[:, d, i, lo * P:hi * P], in0=PS[:, 1 + i, lo * P:hi * P],
                                    scalar=ML_DH ** -0.5, in1=E[:, d, i, lo * P:hi * P], op0=ALU.mult, op1=ALU.mult)
                            ins.then_inc(w_ready, 1)
                dve.wait_ge(h_added, 16)
                Hh = H.rearrange("p t (h f) -> p (t h) f", f=ML_DH)
                for n in range(16):
                    ins = nc.vector.bn_stats(ml_st[:, n, :], Hh[:, n, :])
                link(ins)
                for n in range(16):
                    ins = nc.vector.bn_aggr(ml_mv[:, n, :], ml_st[:, n, :])
                link(ins)
                nc.vector.tensor_scalar(ml_rstd, ml_mv[:, :, 1], LN_EPS, None, ALU.add).then_inc(ml_var, 1)
                dve.wait_ge(ml_sd, 1)
                link(nc.vector.reciprocal(ml_rstd, ml_rstd))
                for n in range(16):
                    ins = nc.vector.tensor_scalar(Hh[:, n, :], Hh[:, n, :], ml_mv[:, n, 0:1], ml_rstd[:, n:n + 1],
                                                  ALU.subtract, ALU.mult)
                link(ins)
                dve.wait_ge(o_scaled, 1)
                for t in range(TT):
                    nc.vector.tensor_tensor(H[:, t, :], H[:, t, :], o_gate[:, t, :], ALU.mult).then_inc(h_ready, 1)
                for i in range(1, 6, 2):
                    drain(1, ("hT", i), mixT[:, i, :])

            def routing(l):
                v = routing_views(l)
                nc.vector.memset(v["gp"], -3e38)
                wait_full(dve, l, ("logits", 0))
                nc.vector.tensor_tensor(v["lg"], bank_of(l, ("logits", 0))[:, 0:144].rearrange("p (t g) -> p t g", t=TT),
                                        rbias[:].unsqueeze(1).to_broadcast([P, TT, 36]), ALU.add)\
                    .then_inc(dve_drained[l], 1)
                wait_drained(dve, l, ("logits", 0))
                link(nc.vector.tensor_copy(v["gp"][:, :, 0:NG], v["lg"][:, :, 0:NG]))
                for t in range(TT):
                    ins = nc.vector.max(v["gm"][:, t, :], v["gp"][:, t, :])
                link(ins)
                for t in range(TT):
                    ins = nc.vector.max_index(v["gi"][:, t, :], v["gm"][:, t, :], v["gp"][:, t, :])
                nc.vector.tensor_tensor(v["gd"], v["lg"][:, :, 0:NG], v["gm"][:, :, 0:1].to_broadcast([P, TT, NG]),
                                        ALU.subtract).then_inc(gdiff[l], 1)
                dve.wait_ge(gdiff[l], 1)
                link(nc.vector.tensor_copy(v["gif"], v["gi"][:, :, 0:1]))
                link(nc.vector.tensor_tensor(v["oh"], count[:, 0:NG].unsqueeze(1).to_broadcast([P, TT, NG]),
                                             v["gif"].to_broadcast([P, TT, NG]), ALU.is_equal))
                link(nc.vector.tensor_tensor(v["prod"], v["lg"][:, :, NG:].rearrange("p t (g e) -> p t g e", g=NG),
                                             v["oh"].unsqueeze(3).to_broadcast([P, TT, NG, EPG]), ALU.mult))
                link(nc.vector.tensor_reduce(v["es"], v["prod"].rearrange("p t g e -> p t e g"), AX, ALU.add))
                for t in range(TT):
                    ins = nc.vector.max(v["e8"][:, t, :], v["es"][:, t, :])
                link(ins)
                for t in range(TT):
                    ins = nc.vector.max_index(v["ei"][:, t, :], v["e8"][:, t, :], v["es"][:, t, :])
                link(ins)
                nc.vector.tensor_tensor(v["ed"], v["e8"][:, :, 1:2], v["e8"][:, :, 0:1], ALU.subtract)\
                    .then_inc(ediff[l], 1)
                link(nc.vector.tensor_copy(v["eif"], v["ei"][:, :, 0:2]))
                link(nc.vector.scalar_tensor_tensor(out=v["eid"], in0=v["gif"].to_broadcast([P, TT, 2]),
                                                    scalar=float(EPG), in1=v["eif"], op0=ALU.mult, op1=ALU.add))
                link(nc.vector.tensor_tensor(v["pick"],
                                             count.unsqueeze(1).unsqueeze(1).to_broadcast([P, TT, 2, NE]),
                                             v["eid"].unsqueeze(3).to_broadcast([P, TT, 2, NE]), ALU.is_equal))
                nc.vector.tensor_tensor(v["picks"], v["pick"][:, :, 0, :], v["pick"][:, :, 1, :], ALU.add)\
                    .then_inc(picks_ready[l], 1)
                dve.wait_ge(gexp[l], 1)
                link(nc.vector.tensor_reduce(v["z"], v["ge"], AX, ALU.add))
                dve.wait_ge(eexp[l], 1)
                link(nc.vector.scalar_tensor_tensor(out=v["dn"], in0=v["e2"], scalar=1.0, in1=v["z"],
                                                    op0=ALU.add, op1=ALU.mult))
                link(nc.vector.reciprocal(gates[:, :, 0:1], v["dn"]))
                link(nc.vector.tensor_tensor(gates[:, :, 1:2], gates[:, :, 0:1], v["e2"], ALU.mult))
                wait_full(dve, l, ("rank", 0))
                bank = bank_of(l, ("rank", 0))
                link(nc.vector.tensor_scalar(v["ci"], bank[:, NE * TT:NE * TT + NE], float(CAP - 1), None, ALU.add))
                link(nc.vector.tensor_scalar(v["cs"], v["ci"], CAP.bit_length() - 1, None, ALU.logical_shift_right))
                link(nc.vector.tensor_scalar(v["nb"], v["cs"], 1.0, None, ALU.max))
                link(nc.vector.tensor_tensor_scan(v["inc"], ones[:, 0:NE], v["nb"], 0.0, ALU.mult, ALU.add))
                link(nc.vector.tensor_tensor(v["ex"], v["inc"], v["nb"], ALU.subtract))
                nc.vector.tensor_copy(blk_i[:, 0:NE], v["nb"][0:1])
                nc.vector.tensor_copy(blk_i[:, NE:2 * NE], v["ex"][0:1])
                nc.vector.tensor_copy(blk_i[:, 2 * NE:], v["inc"][0:1, NE - 1:NE]).then_inc(blocks_ready[l], 1)
                nc.vector.scalar_tensor_tensor(
                    out=v["slot"], in0=v["ex"].unsqueeze(1).to_broadcast([P, TT, NE]), scalar=float(CAP),
                    in1=bank[:, 0:NE * TT].rearrange("p (t e) -> p t e", t=TT), op0=ALU.mult, op1=ALU.add)\
                    .then_inc(dve_drained[l], 1)
                wait_drained(dve, l, ("rank", 0))
                link(nc.vector.tensor_tensor(v["ps"], v["pick"], v["slot"].unsqueeze(2).to_broadcast([P, TT, 2, NE]),
                                             ALU.mult))
                link(nc.vector.tensor_reduce(v["df"], v["ps"], AX, ALU.add))
                nc.vector.tensor_copy(dest[:], v["df"]).then_inc(dest_ready[l], 1)

            def expert(l, e):
                n = dve.value_load(blk_i[0:1, bass.ds(e, 1)], min_val=1, max_val=T // CAP)
                g0 = dve.value_load(blk_i[0:1, bass.ds(e + NE, 1)], min_val=0, max_val=MAX_BLOCKS - 1)
                with dve.Fori(0, n) as i:
                    g = g0 + i
                    dve.wait_ge(silu_ready[l], g + 1)
                    dve.wait_ge(h3_full[l], g + 1)
                    nc.vector.tensor_tensor(hT.rearrange("p k s -> p (k s)"), hs, PS[:, 2, 0:FT * CAP], ALU.mult)\
                        .then_inc(hT_ready[l], 1)
                    dve.wait_ge(y_full[l], g + 1)
                    dve.wait_ge(y_stored[l], 16 * (g + 1))
                    nc.vector.tensor_copy(y_blk.rearrange("p (a b) -> p a b", b=512), PS[0:CAP, 4:6, :])\
                        .then_inc(y_ready[l], 1)

            def combine(l):
                for t in range(TT):
                    dve.wait_ge(y_got_in[l][t], 32)
                    y1, y2 = y_got[:, 2 * t, :], y_got[:, 2 * t + 1, :]
                    link(nc.vector.tensor_scalar(y1, y1, gates[:, t, 0:1], None, ALU.mult))
                    link(nc.vector.scalar_tensor_tensor(out=y2, in0=y2, scalar=gates[:, t, 1:2], in1=y1,
                                                        op0=ALU.mult, op1=ALU.add))
                    link(nc.vector.scalar_tensor_tensor(out=X[:, t, :], in0=X[:, t, :], scalar=ALPHA, in1=y2,
                                                        op0=ALU.mult, op1=ALU.add))

            nc.vector.memset(zrow[:], 0.0).then_inc(zero_set, 1)
            for l in range(DEPTH):
                if l == 1:
                    dve.wait_ge(x2_ready[0], TT)
                    for i in range(4):
                        nc.vector.memset(pre[:, i, 0:2], 0.0)
                        ins = nc.vector.memset(pre[:, i, T + 2:T + 4], 0.0)
                    ins.then_inc(pads_zero, 1)
                    nc.vector.memset(v_ml[:, :, :, ML_DH:VW], 1.0)
                    nc.vector.memset(g_in, 0.0).then_inc(gates_set, 1)
                    nc.vector.memset(g_fo, 0.0).then_inc(gates_set, 1)
                for k in range(1, KT, 2):
                    drain(l, ("xT", k), XT[:, k, :])
                if l == 0:
                    for k2 in (1, 3):
                        drain(0, ("memT", k2), memT[:, 2 * k2:2 * k2 + 2, :].rearrange("p a b -> p (a b)"))
                    drain(0, ("memv", 0), memv[:].rearrange("p a b -> p (a b)"))
                    for kind, c, _, _ in chunks[0]:
                        name = (kind, c, 1)
                        wait_full(dve, 0, name)
                        bank = bank_of(0, name)
                        if kind == "v":
                            ins = nc.vector.tensor_copy(v_nat[:, 2:4, 256 * c:256 * c + 256],
                                                        bank.rearrange("p (t f) -> p t f", t=2))
                        elif kind == "q":
                            ins = nc.vector.tensor_copy(
                                qT[:, 2 * c + 1, :].rearrange("p (b r c) -> p b r c", r=ROWS, c=QC),
                                bank.rearrange("p (r b c) -> p b r c", b=NBLK, c=QC)[:, :, ::-1, ::-1])
                        elif kind == "k":
                            ins = nc.vector.tensor_copy(kT[:, 2 * c + 1, :], bank)
                        else:
                            ins = nc.vector.tensor_copy(qm0[:, 1, :], bank)
                        ins.then_inc(dve_drained[0], 1)
                else:
                    dve.wait_ge(mlp_in, 16 * 8)
                    for m in range(12):
                        convolve(m)
                    gate_rows()
                    forget_rows()
                attention(l)
                if l == 1:
                    mlstm()
                for c in range(4):
                    for s in range(2):
                        name = ("out", c, s)
                        wait_full(dve, l, name)
                        part = X[:, 2 * s:2 * s + 2, 256 * c:256 * c + 256]
                        nc.vector.scalar_tensor_tensor(out=part, in0=part, scalar=ALPHA,
                                                       in1=bank_of(l, name).rearrange("p (t f) -> p t f", t=2),
                                                       op0=ALU.mult, op1=ALU.add).then_inc(dve_drained[l], 1)
                wait_drained(dve, l, ("out", 3, 1))
                norm(l, ln1_params(l), ln_in, var_ready, sd_ready, scaled)
                for k in range(1, KT, 2):
                    drain(l, ("x1T", k), XT[:, k, :])
                dve.wait_ge(route_in[l], 64)
                routing(l)
                dve.sem_inc(y_ready[l], 1)
                with dve.Fori(0, NE) as e:
                    expert(l, e)
                combine(l)
                norm(l, ln2_p, ln2_in, var2_ready, sd2_ready, scaled2)

        @block.gpsimd
        def _(pool):
            pool.wait_ge(zero_set, 1)
            zi = zrow[:, 0:CAP].bitcast(I32)
            pool.dma_start(rpb_pad[0:RPB_PAD].rearrange("(a n) -> a n", a=1), zrow[:]).then_inc(pads_in, 16)
            pool.dma_start(rpb_pad[RPB_PAD + NA_HEADS * RPB_HEAD:].rearrange("(a n) -> a n", a=1), zrow[:])\
                .then_inc(pads_in, 16)
            pool.dma_start(rpb_pad[RPB_PAD:RPB_PAD + NA_HEADS * RPB_HEAD].rearrange("(h n) -> h n", h=NA_HEADS),
                           na_rpb[0].rearrange("h r c -> h (r c)")).then_inc(pads_in, 16)
            for b in range(MAX_BLOCKS):
                pool.dma_start(slot_token[b * CAP:(b + 1) * CAP, :].rearrange("s o -> o s"), zi)\
                    .then_inc(slots_zeroed, 16)
            nc.gpsimd.memset(zeros, 0.0).then_inc(zeros_set, 1)
            pool.wait_ge(zeros_set, 1)
            for r in range(NE * CAP, MAX_BLOCKS * CAP, P):
                pool.dma_start(y_rows[r:r + P, :], zeros).then_inc(y_zeroed, 16)
            pool.wait_ge(y_zeroed, 16 * ((MAX_BLOCKS - NE) * CAP // P))
            pool.wait_ge(rpb_in, 16 * ROWS)
            pool.wait_ge(const_in, 32)
            for v, shift in enumerate((SHIFT[0], SHIFT[1], SHIFT[3])):
                for h in range(NA_HEADS):
                    run = rpb_tab[:, h, shift:shift + 1]
                    src = bass.AP(tensor=run.tensor, offset=run.offset, ap=[list(run.ap[0]), [RPB_ROW, ROWS], [1, KC]])
                    ins = nc.gpsimd.tensor_tensor(bias_tab[:, v, h, :].rearrange("p (r c) -> p r c", c=KC), src,
                                                  na_mask[:, v:v + 1, :].to_broadcast([P, ROWS, KC]), ALU.add)
                ins.then_inc(bias_built, 1)

            for l in range(DEPTH):
                if l == 1:
                    wait_drained(pool, 1, ("o", 2, 1))
                    pool.wait_ge(mlp_in, 16 * 8)
                    nc.gpsimd.tensor_tensor(o_gate, o_gate, norm_g.unsqueeze(1).to_broadcast([P, TT, TOKEN_W]),
                                            ALU.mult).then_inc(o_scaled, 1)
                for t in range(TT):
                    pool.wait_ge(scaled[l], t + 1)
                    nc.gpsimd.tensor_tensor(X[:, t, :], X[:, t, :], ln1_params(l)[:, 1, :], ALU.add)\
                        .then_inc(x1_ready[l], 1)
                pool.wait_ge(dest_ready[l], 1)
                if l == 0:
                    pool.wait_ge(slots_zeroed, 16 * MAX_BLOCKS)
                for t in range(TT):
                    for k in range(2):
                        pool.indirect_dma_start(out=slot_token, out_offset=bass.IndirectOffsetOnAxis(
                            ap=dest[:, t, k:k + 1].bitcast(U32), axis=0), in_=ctok[:, t:t + 1], in_offset=None)\
                            .then_inc(slots_set[l], 16)
                pool.wait_ge(slots_set[l], 16 * 2 * TT)
                pool.dma_start(slot_tab[:], slot_token.rearrange("(b s) o -> s (b o)", s=CAP)).then_inc(slots_in[l], 16)
                pool.wait_ge(slots_in[l], 16)
                pool.wait_ge(x_stored[l], 16 * TT)
                pool.wait_ge(blocks_ready[l], 1)
                total = pool.value_load(blk_i[0:1, 2 * NE:2 * NE + 1], min_val=NE, max_val=MAX_BLOCKS)

                def gather(g, first):
                    if not first:
                        pool.wait_ge(xgT_full[l], g)
                    nc.gpsimd.tensor_copy(idx_now[:], slot_tab[:, bass.ds(g, 1)]).then_inc(idx_set[l], 1)
                    this = g + 1 if isinstance(g, int) else pool.to_reg(g + 1)
                    settle(pool)
                    pool.wait_ge(idx_set[l], this)
                    pool.indirect_dma_start(out=xg, out_offset=None, in_=x_rows, in_offset=bass.IndirectOffsetOnAxis(
                        ap=idx_now[:].bitcast(U32), axis=0)).then_inc(x_gathered[l], 16)
                    pool.wait_ge(x_gathered[l], 16 * (g + 1))

                gather(0, True)
                with pool.Fori(1, total) as g:
                    gather(g, False)
                stored = pool.to_reg(16 * (total + 1))
                settle(pool)
                pool.wait_ge(y_stored[l], stored)
                for t in range(TT):
                    for k in range(2):
                        pool.indirect_dma_start(out=y_got[:, 2 * t + k, :], out_offset=None,
                                                in_=y_rows[0:MAX_BLOCKS * CAP, :],
                                                in_offset=bass.IndirectOffsetOnAxis(
                                                    ap=dest[:, t, k:k + 1].bitcast(U32), axis=0))\
                            .then_inc(y_got_in[l][t], 16)
                for t in range(TT):
                    pool.wait_ge(scaled2[l], t + 1)
                    nc.gpsimd.tensor_tensor(X[:, t, :], X[:, t, :], ln2_p[:, 1, :], ALU.add).then_inc(x2_ready[l], 1)


_INS = ['x', 'mem', 'w_mem_kv', 'na_w_in', 'na_rpb', 'ml_w_in', 'ml_conv_w', 'ml_conv_b', 'ml_gate_b', 'ml_norm_g',
        'w_out', 'ln1_g', 'ln1_b', 'ln2_g', 'ln2_b', 'moe_wg', 'moe_bg', 'moe_we', 'moe_be', 'moe_w1', 'moe_w3',
        'moe_w2']


def kernel(**inputs):
    import numpy as _np
    import concourse.bacc as _bacc
    from concourse import mybir as _mybir
    from concourse.bass_utils import run_bass_kernel_spmd as _run

    nc = _bacc.Bacc("TRN2", target_bir_lowering=False, num_devices=1)
    const_f, const_tok = constants()
    arrays = {f"in_{name}": _np.ascontiguousarray(inputs[name]) for name in _INS}
    arrays["const_f"], arrays["const_tok"] = const_f, const_tok
    args = [nc.dram_tensor(name, a.shape, _mybir.dt.from_np(a.dtype), kind="ExternalInput").ap()
            for name, a in arrays.items()]
    out = nc.dram_tensor("out_0", (1, T, D), F32, kind="ExternalOutput").ap()
    encoder(nc, *args, out)
    r = _run(nc, [arrays], core_ids=[0])
    return r.results[0]["out_0"]
```

```python
from contextlib import ExitStack

import concourse.bass as bass
from concourse import mybir
import numpy as np

F32 = mybir.dt.float32
I32 = mybir.dt.int32
F16 = mybir.dt.float16
U32 = mybir.dt.uint32
ALU = mybir.AluOpType
ACT = mybir.ActivationFunctionType
AX = mybir.AxisListType.X

P = 128
D = 1024
T = 512
TT = T // P
KT = D // P
DEPTH = 2
NMEM = 256
GRID_W = 64
ROWS = T // GRID_W
WIN_H, WIN_W = 8, 16
TOKEN_W = 768
MEM_W = 256
HD = 64
NA_HEADS = 12
ML_HEADS = 4
ML_DH = 192
VW = ML_DH + 1
CONV_K = 5
NG, EPG = 4, 8
NE = NG * EPG
FE = 512
FT = FE // P
CAP = 64
MAX_BLOCKS = NE + (2 * T - 1) // CAP + 1
LN_EPS = 1e-5
ALPHA = (2 * DEPTH) ** 0.25
NEG = -1e30

QC = 16
KC = 32
NBLK = GRID_W // QC
KEY0 = [min(max(QC * b - WIN_W // 2, 0), GRID_W - KC) for b in range(NBLK)]
SHIFT = [KEY0[b] - QC * b + 16 for b in range(NBLK)]
VARIANT = [0, 1, 1, 2]
RPB_ROW = 2 * WIN_W - 1
RPB_HEAD = (2 * WIN_H - 1) * RPB_ROW
RPB_RUN = (ROWS - 1) * RPB_ROW + 48
RPB_PAD = 64

W_SCALE = 256.0
X_SCALE = 16.0
H_SCALE = 8.0

DVE_COLS = 1024
ACT_RUNS = [[(DVE_COLS, 2048), (2048, 4096)], [(0, 2048), (2048, 4096)], [(0, 2048), (2048, 4096)]]
N_RUNS = sum(len(runs) for runs in ACT_RUNS)

CHUNK = 2176


def constants():
    p = np.arange(P)
    ident = np.eye(P)
    anti = ident[::-1]
    earlier = (p[:, None] < p[None, :]) * 1.0
    ones = np.ones((P, P))
    na = np.zeros((P, 3, KC))
    for b in (0, 1, 3):
        c = QC * b + 15 - p % QC
        start = np.clip(c - WIN_W // 2, 0, GRID_W - WIN_W)[:, None]
        kc = KEY0[b] + np.arange(KC)[None, :]
        na[:, VARIANT[b], :] = np.where((kc >= start) & (kc < start + WIN_W), 0.0, NEG)
    fwd = np.where(p[None, :] >= p[:, None], 0.0, NEG)
    bwd = np.where(p[None, :] <= p[:, None], 0.0, NEG)
    count = np.tile(np.arange(NE), (P, 1)) * 1.0
    f = np.concatenate([ident, anti, earlier, ones, na.reshape(P, -1), fwd, bwd, count], axis=1).astype(np.float32)
    tokens = (np.arange(TT)[None, :] * P + p[:, None]).astype(np.int32)
    return f, tokens


class Jobs:

    def __init__(self, order):
        self.number, self.engine, self.ordinal = {}, {}, {}
        self.by = []
        seen = {"act": 0, "dve": 0}
        for n, (name, engine) in enumerate(order):
            seen[engine] += 1
            self.number[name], self.engine[name], self.ordinal[name] = n, engine, seen[engine]
            self.by.append(name)


def chunk_list(layer):
    if layer == 0:
        return ([("v", c, 2 * TOKEN_W + 256 * c, 256) for c in range(3)]
                + [("q", c, 256 * c, 256) for c in range(3)]
                + [("k", c, TOKEN_W + 256 * c, 256) for c in range(3)] + [("m", 0, 3 * TOKEN_W, 256)])
    return ([("q", c, 256 * c, 256) for c in range(3)] + [("k", c, TOKEN_W + 256 * c, 256) for c in range(3)]
            + [("m", 0, 4 * TOKEN_W, 16 + 256)]
            + [("v", c, 2 * TOKEN_W + 256 * c, 256) for c in range(3)]
            + [("o", c, 3 * TOKEN_W + 256 * c, 256) for c in range(3)])


def job_order(layer):
    order = [(("xT", k), ("act", "dve")[k % 2]) for k in range(KT)]
    if layer == 0:
        order += [(("memT", k), ("act", "dve")[k % 2]) for k in range(4)]
        order += [(("memk", 0), "act"), (("memv", 0), "dve")]
    for kind, c, _, _ in chunk_list(layer):
        if layer == 1 and kind == "m":
            order.append((("gates", 0), "dve"))
        for s in range(2):
            drain = ("act", "dve")[s] if layer == 0 else "act"
            order.append(((kind, c, s), drain))
    if layer == 1:
        order += [(("rows", 0), "dve"), (("rows", 1), "dve"), (("cols", 0), "dve")]
        order += [(("hT", i), ("act", "dve")[i % 2]) for i in range(6)]
    order += [(("out", c, s), "dve") for c in range(4) for s in range(2)]
    order += [(("x1T", k), ("act", "dve")[k % 2]) for k in range(KT)]
    order += [(("logitsT", 0), "dve"), (("logits", 0), "dve"), (("rank", 0), "dve")]
    return order


def attention_units(layer):
    units = []
    if layer == 0:
        units += [(b, par, i, False) for b in range(NBLK) for par in range(2) for i in range(3)]
    units += [(t, par, 0, True) for t in range(TT) for par in range(2)]
    return units


def encoder(nc, x, mem, w_mem_kv, na_w_in, na_rpb, ml_w_in, ml_conv_w, ml_conv_b, ml_gate_b, ml_norm_g, w_out,
            ln1_g, ln1_b, ln2_g, ln2_b, moe_wg, moe_bg, moe_we, moe_be, moe_w1, moe_w3, moe_w2,
            const_f, const_tok, out):
    ctx = ExitStack()
    with ctx:
        ctx.enter_context(nc.allow_non_contiguous_dma("small parameters"))

        def sb(name, shape, dt=F32):
            return ctx.enter_context(nc.sbuf_tensor(name, shape, dt))

        def sem(name):
            return ctx.enter_context(nc.semaphore(name))

        def sems(name, n=DEPTH):
            return [sem(f"{name}{i}") for i in range(n)]

        def dram(name, shape, dt=F32):
            return nc.dram_tensor(name, shape, dt, kind="Internal").ap()

        rpb_pad = dram("rpb_pad", [RPB_PAD * 2 + NA_HEADS * RPB_HEAD])
        v_rows = dram("v_rows", [T, TOKEN_W])
        x_rows = dram("x_rows", [T, 2 * D], F16)
        slot_token = dram("slot_token", [(MAX_BLOCKS + 2) * CAP, 1], I32)
        y_rows = dram("y_rows", [(MAX_BLOCKS + 1 + T // CAP) * CAP, D])

        X = sb("X", [P, TT, D])
        XT = sb("XT", [P, KT, T])
        RING = sb("RING", [P, 3 * 12288])
        AREA = sb("AREA", [P, 4864])
        CF = sb("CF", [P, 128 * 4 + 96 + 256 + 32])
        ctok = sb("ctok", [P, TT], I32)
        memk = sb("memk", [P, 2, NMEM])
        memv = sb("memv", [P, 2, MEM_W])
        wr = sb("wr", [P, KT, NG + NE])
        rbias = sb("rbias", [P, NG + NE])
        gates = sb("gates", [P, TT, 2])
        dest = sb("dest", [P, TT, 2], I32)
        blk_i = sb("blk_i", [1, 2 * NE + 1], I32)
        slot_tab = sb("slot_tab", [CAP, MAX_BLOCKS + 2], I32)
        const16 = sb("const16", [P, 3, P], F16)
        ident16, earlier16, ones16 = (const16[:, i, :] for i in range(3))
        idx_now = sb("idx_now", [CAP, 1], I32)
        zrow = sb("zrow", [1, 64])
        small = sb("small", [P, 192])
        PS = ctx.enter_context(nc.psum_tensor("PS", [P, 8, 512], F32))

        ident = CF[:, 0:128]
        anti = CF[:, 128:256]
        earlier = CF[:, 256:384]
        ones = CF[:, 384:512]
        na_mask = CF[:, 512:608].rearrange("p (v k) -> p v k", v=3)
        ml_mask = CF[:, 608:864].rearrange("p (d k) -> p d k", d=2)
        count = CF[:, 864:896]

        def ring(off, *dims):
            n = int(np.prod(dims))
            assert off + n <= 3 * 12288
            v = RING[:, off:off + n]
            if len(dims) == 2:
                v = v.rearrange("p (a b) -> p a b", b=dims[1])
            elif len(dims) == 3:
                v = v.rearrange("p (a b c) -> p a b c", b=dims[1], c=dims[2])
            return v

        qT = ring(0, 6, T)
        kT = ring(3072, 6, T)
        v_win = ring(6144, 2 * NBLK, TOKEN_W)
        bias_tab = ring(12288, 3, NA_HEADS, ROWS * KC)
        rpb_tab = ring(21504, NA_HEADS, RPB_RUN)
        v_nat = ring(24704, TT, TOKEN_W)
        o_na = ring(27776, NBLK, TOKEN_W)
        o_mem0 = ring(30848, TT, MEM_W)
        qm0 = ring(31872, 2, T)
        sneg = ring(32896, 3, 512)
        prob0 = ring(34432, 3, 512)
        probT0 = ring(24704, 2, 512)
        memT = ring(27776, KT, NMEM)
        w_kv = ring(6144, KT, 2 * MEM_W)
        zeros = ring(12288, D)
        mem_in = ring(30848, 2, D)
        qk = ring(0, 12, T)
        pre = ring(6144, 4, T + 4)
        v_ml = ring(8208, TT, ML_HEADS, VW)
        o_gate = ring(11296, TT, TOKEN_W)
        H = ring(14368, TT, TOKEN_W)
        W = ring(17440, 2, TT, T)
        E = ring(21536, 2, TT, T)
        qm1 = ring(25632, 2, T)
        Rd = ring(26656, 2, 512)
        r_F = ring(27680, T)
        r_a = ring(28192, T)
        r_M = ring(28704, T)
        r_m = ring(29216, T)
        prob1 = ring(29728, 3, 512)
        probT1 = ring(31264, 2, 512)
        o_mem1 = ring(32288, TT, MEM_W)
        norm_g = ring(33312, TOKEN_W)
        conv_w = ring(34080, 12, CONV_K)
        conv_b = ring(34140, 12)
        g_in = ring(34160, TT, 64)
        g_fo = ring(34416, TT, 64)
        g_tok = ring(34672, TT, 16)
        g_abs = ring(34736, TT, 8)
        g_ln = ring(34768, TT, 8)
        g_bias = ring(34800, 16)
        ml_st = ring(34816, 16, 6)
        ml_mv = ring(34912, 16, 2)
        ml_rstd = ring(34944, 16)
        acol = ring(34960, TT, 8)
        mcol = ring(34992, TT, 8)
        em = ring(35024, TT, 8)
        den = ring(35056, 16, 2)
        rden = ring(35088, 16, 2)
        qm, prob, probT, o_mem = [qm0, qm1], [prob0, prob1], [probT0, probT1], [o_mem0, o_mem1]
        mixT = XT

        staged = [RING[:, 24576 + 4096 * i:24576 + 4096 * (i + 1)] for i in range(3)]
        parts = [[RING[:, 4096 * (3 * q + i):4096 * (3 * q + i + 1)].bitcast(F16).rearrange("p (a n) -> p a n", a=2)
                  for i in range(3)] for q in range(2)]
        y_got = ring(24576, 2 * TT, D)
        ln2_p = ring(24576 + 8192, 2, D)

        chunk_buf = [AREA[:, CHUNK * i:CHUNK * (i + 1)] for i in range(2)]
        xg = AREA[0:CAP, 0:1024].bitcast(F16)
        xgT = AREA[:, 1024:1536].bitcast(F16).rearrange("p (k s) -> p k s", s=P)
        hs = AREA[0:CAP, 1536:2048]
        h3 = AREA[0:CAP, 2048:2560]
        h_parts = AREA[0:CAP, 2560:3072].bitcast(F16).rearrange("p (a f) -> p a f", a=2)
        hT = AREA[:, 3072:3328].bitcast(F16).rearrange("p (k s) -> p k s", s=P)
        y_blk = AREA[0:CAP, 3328:4352]
        logitsT = AREA[0:NG + NE, 4352:4864]

        msum = sb("msum", [P, 40, 2])
        mneg = sb("mneg", [P, 40, 2])
        mraw = sb("mraw", [P, 8, 2])
        rsum = small[:, 0:16].rearrange("p (a b) -> p a b", b=8)
        ln_st = small[:, 16:112].rearrange("p (t a s) -> p t a s", t=TT, a=4)
        ln_mv = small[:, 112:120].rearrange("p (t s) -> p t s", s=2)
        ln_ve = small[:, 120:124]
        ln_sd = small[:, 124:128]
        ln_rs = small[:, 128:132]
        ln_nm = small[:, 132:136]
        warm = small[0:1, 136:137]

        const_in, x_in, mem_in_s, kv_in = sem("const_in"), sem("x_in"), sem("mem_in_s"), sem("kv_in")
        zero_set, pads_in, rpb_in, mlp_in = sem("zero_set"), sem("pads_in"), sem("rpb_in"), sem("mlp_in")
        slots_zeroed, zeros_set, y_zeroed = sem("slots_zeroed"), sem("zeros_set"), sem("y_zeroed")
        v_out, v_in, bias_built = sem("v_out"), sem("v_in"), sem("bias_built")
        chunk_in = [sems(f"chunk_in_l{l}_", 2) for l in range(DEPTH)]
        ln_in, ln2_in, route_in = sem("ln_in"), sem("ln2_in"), sem("route_in")
        bank_full = sems("bank_full")
        act_drained, dve_drained = sems("act_drained"), sems("dve_drained")
        scores_full, max_ready, probs_ready = sems("scores_full"), sems("max_ready"), sems("probs_ready")
        probsT_full, probsT_ready, values_summed = sems("probsT_full"), sems("probsT_ready"), sems("values_summed")
        heads_ready, mix_full, mix_ready = sems("heads_ready"), sems("mix_full"), sems("mix_ready")
        dve_step, pool_step = sem("dve_step"), sem("pool_step")
        pads_zero = sem("pads_zero")
        conv_done, silu_done, o_scaled = sem("conv_done"), sem("silu_done"), sem("o_scaled")
        lf_abs, lf_ln, gates_set = sem("lf_abs"), sem("lf_ln"), sem("gates_set")
        rows_set, mcol_set, em_set = sem("rows_set"), sem("mcol_set"), sem("em_set")
        r_full, r_masked, e_ready = sem("r_full"), sem("r_masked"), sem("e_ready")
        s_full, w_ready, num_full, h_added = sem("s_full"), sem("w_ready"), sem("num_full"), sem("h_added")
        ml_var, ml_sd, h_ready = sem("ml_var"), sem("ml_sd"), sem("h_ready")
        var_ready, sd_ready, x1_dve, x1_pool = sem("var_ready"), sem("sd_ready"), sem("x1_dve"), sem("x1_pool")
        moments, normed, x_alpha = sem("moments"), sem("normed"), sem("x_alpha")
        var2_ready, sd2_ready, x2_dve, x2_pool = sem("var2_ready"), sem("sd2_ready"), sem("x2_dve"), sem("x2_pool")
        moments2, normed2 = sem("moments2"), sem("normed2")
        gdiff, gexp, ediff, eexp = sem("gdiff"), sem("gexp"), sem("ediff"), sem("eexp")
        picks_ready, blocks_ready, dest_ready = sem("picks_ready"), sem("blocks_ready"), sem("dest_ready")
        x_stored, slots_set, slots_in = sem("x_stored"), sem("slots_set"), sem("slots_in")
        idx_set, x_gathered = sems("idx_set"), sems("x_gathered")
        xgT_full, xgT_ready = sems("xgT_full"), sems("xgT_ready")
        h1_full, h3_full, h1_summed, h3_summed = sems("h1_full"), sems("h3_full"), sems("h1_summed"), sems("h3_summed")
        silu_ready, h_ready_e, h_high, h_low = sems("silu_ready"), sems("h_ready_e"), sems("h_high"), sems("h_low")
        hT_full, hT_ready = sems("hT_full"), sems("hT_ready")
        h1_upper, h3_upper, y_upper = sems("h1_upper"), sems("h3_upper"), sems("y_upper")
        w_high, w_low, x_high, x_low = sems("w_high"), sems("w_low"), sem("x_high"), sem("x_low")
        const16_set, w_first = sem("const16_set"), sem("w_first")
        y_full, y_ready, y_stored = sems("y_full"), sems("y_ready"), sems("y_stored")
        w_in = [sems(f"w_in_l{l}_", 3) for l in range(DEPTH)]
        y_got_in = sems("y_got_in", TT)
        out_done = sem("out_done")

        jobs = [Jobs(job_order(l)) for l in range(DEPTH)]
        units = [attention_units(l) for l in range(DEPTH)]
        chunks = [chunk_list(l) for l in range(DEPTH)]
        n_proj = [len(c) for c in chunks]

        def bank_of(l, name):
            return PS[:, jobs[l].number[name] % 8, :]

        def wait_drained(eng, l, name):
            s = act_drained if jobs[l].engine[name] == "act" else dve_drained
            eng.wait_ge(s[l], jobs[l].ordinal[name])

        def wait_full(eng, l, name):
            eng.wait_ge(bank_full[l], jobs[l].number[name] + 1)

        NORM1_SHARED, NORM2_SHARED = (3,), (0, 2)
        NORM2_ACT = (("root", 0), ("root", 1), ("norm", 0), ("root", 2), ("root", 3), ("norm", 2))
        EARLY = [(0, 0), (0, 1), (0, 2), (1, 0), (1, 1)]

        def wait_x(eng, l, t, after_experts=False):
            shared, by_pool, by_dve = ((NORM2_SHARED, x2_pool, x2_dve) if after_experts
                                       else (NORM1_SHARED, x1_pool, x1_dve))
            mine = t in shared
            per_layer = len(shared) if mine else TT - len(shared)
            eng.wait_ge(by_pool if mine else by_dve,
                        per_layer * l + sum((u in shared) == mine for u in range(t + 1)))

        def wait_x_all(eng, l):
            for t in (TT - 2, TT - 1):
                wait_x(eng, l, t, True)

        def last_mix_round(l, blk_index):
            return sum(1 if m else 2 for m in block_kinds(l)[:blk_index + 1])

        def block_kinds(l):
            return ([False] * NBLK if l == 0 else []) + [True] * TT

        def block_no(l, unit):
            b, _, _, is_mem = unit
            return b + (NBLK if l == 0 and is_mem else 0)

        def steps(l):
            us = units[l]
            for i in range(len(us) + 6):
                at = lambda lag: us[i - lag] if 0 <= i - lag < len(us) else None
                yield i, at

        def ends_group(u):
            return u is not None and (u[3] or u[2] == 2)

        def group_no(l, u):
            return 2 * block_no(l, u) + u[1]

        def blocks_of(eng, e):
            n = eng.value_load(blk_i[0:1, bass.ds(e, 1)], min_val=1, max_val=T // CAP)
            g0 = eng.value_load(blk_i[0:1, bass.ds(e + NE, 1)], min_val=1, max_val=MAX_BLOCKS)
            return n, g0

        def blocks_end(eng):
            return eng.value_load(blk_i[0:1, 2 * NE:2 * NE + 1], min_val=NE + 1, max_val=MAX_BLOCKS + 1)

        def x_parts(t):
            return parts[1][2].rearrange("p a (b n) -> p (a b n)", b=2)[:, 2 * D * t:2 * D * (t + 1)]\
                .rearrange("p (a k f) -> p a k f", a=2, k=KT)

        def by_tile(row):
            return row.rearrange("p (f k) -> p k f", k=KT)

        def routing_views(l):
            base = chunk_buf[(n_proj[l] + 3) % 2]
            views, at = {}, 0
            for name, dims in (("lg", (TT, 36)), ("gp", (TT, 8)), ("gm", (TT, 8)), ("gi", (TT, 8)), ("gd", (TT, 4)),
                               ("ge", (TT, 4)), ("z", (TT, 1)), ("gif", (TT, 1)), ("oh", (TT, 4)),
                               ("prod", (TT, NG, EPG)), ("es", (TT, 8)), ("e8", (TT, 8)), ("ei", (TT, 8)),
                               ("ed", (TT, 1)), ("e2", (TT, 1)), ("dn", (TT, 1)), ("eif", (TT, 2)), ("eid", (TT, 2)),
                               ("pick", (TT, 2, NE)), ("picks", (TT, NE)), ("ci", (NE,)), ("cs", (NE,)),
                               ("nb", (NE,)), ("inc", (NE,)), ("ex", (NE,)), ("slot", (TT, NE)), ("ps", (TT, 2, NE)),
                               ("df", (TT, 2))):
                n = int(np.prod(dims))
                v = base[:, at:at + n]
                if name in ("gi", "ei"):
                    v = v.bitcast(U32)
                if name == "picks":
                    v = v.bitcast(F16)[:, 0:n]
                if name in ("ci", "cs"):
                    v = v.bitcast(I32)
                if len(dims) == 2:
                    v = v.rearrange("p (a b) -> p a b", b=dims[1])
                elif len(dims) == 3:
                    v = v.rearrange("p (a b c) -> p a b c", b=dims[1], c=dims[2])
                views[name] = v
                at += n
            assert at <= CHUNK
            return views

        def ln1_params(l):
            return chunk_buf[(n_proj[l] + 2) % 2][:, 0:2 * D].rearrange("p (a d) -> p a d", d=D)

        def settle(eng):
            eng.wait_ge(const_in, 32)

        block = ctx.enter_context(nc.Block())

        @block.tensor
        def _(pe):
            def begin(l, name):
                n = jobs[l].number[name]
                if n >= 8:
                    wait_drained(pe, l, jobs[l].by[n - 8])
                return bank_of(l, name)

            def keep_busy(n):
                for _ in range(n):
                    nc.tensor.matmul(PS[:, 6, :], ident, XT[:, 0, :], start=True, stop=True)

            def transposed_x(l, kind):
                for t in range(TT):
                    if kind == "x1T" or l > 0:
                        wait_x(pe, l if kind == "x1T" else l - 1, t, kind == "xT")
                    for k in range(KT):
                        bank = begin(l, (kind, k)) if t == 0 else bank_of(l, (kind, k))
                        mm = nc.tensor.transpose(bank[:, t * P:(t + 1) * P], X[:, t, k * P:(k + 1) * P], ident)
                        if t == TT - 1:
                            mm.then_inc(bank_full[l], 1)

            def memory_kv():
                pe.wait_ge(mem_in_s, 16)
                for k2 in range(4):
                    bank = begin(0, ("memT", k2))
                    for kk in range(2):
                        for m in range(2):
                            k = 2 * k2 + kk
                            mm = nc.tensor.transpose(bank[:, kk * NMEM + m * P:kk * NMEM + (m + 1) * P],
                                                     mem_in[:, m, k * P:(k + 1) * P], ident)
                    mm.then_inc(bank_full[0], 1)
                pe.wait_ge(kv_in, 16)
                wait_drained(pe, 0, ("memT", 2))
                wait_drained(pe, 0, ("memT", 3))
                bank = begin(0, ("memk", 0))
                for i in range(2):
                    for k in range(KT):
                        mm = nc.tensor.matmul(bank[:, i * NMEM:(i + 1) * NMEM], w_kv[:, k, i * P:(i + 1) * P],
                                              memT[:, k, :], start=(k == 0), stop=(k == KT - 1))
                mm.then_inc(bank_full[0], 1)
                bank = begin(0, ("memv", 0))
                for m in range(2):
                    for k in range(KT):
                        mm = nc.tensor.matmul(bank[:, m * MEM_W:(m + 1) * MEM_W], memT[:, k, m * P:(m + 1) * P],
                                              w_kv[:, k, MEM_W:2 * MEM_W], start=(k == 0), stop=(k == KT - 1))
                mm.then_inc(bank_full[0], 1)

            def projection(l):
                wait_drained(pe, l, ("xT", KT - 2))
                wait_drained(pe, l, ("xT", KT - 1))
                for c, (kind, i, _, width) in enumerate(chunks[l]):
                    pe.wait_ge(chunk_in[l][c % 2], 16 * (c // 2 + 1))
                    w = chunk_buf[c % 2][:, 0:KT * width].rearrange("p (k f) -> p k f", f=width)
                    first = width - 256
                    if first:
                        bank = begin(l, ("gates", 0))
                        for t in range(TT):
                            for k in range(KT):
                                mm = nc.tensor.matmul(bank[:, 16 * t:16 * t + 16], XT[:, k, t * P:(t + 1) * P],
                                                      w[:, k, 0:16], start=(k == 0), stop=(k == KT - 1))
                        mm.then_inc(bank_full[l], 1)
                    for s in range(2):
                        bank = begin(l, (kind, i, s))
                        if kind in "qkm":
                            for k in range(KT):
                                mm = nc.tensor.matmul(bank, w[:, k, first + s * P:first + (s + 1) * P], XT[:, k, :],
                                                      start=(k == 0), stop=(k == KT - 1))
                        else:
                            for j in range(2):
                                t = 2 * s + j
                                for k in range(KT):
                                    mm = nc.tensor.matmul(bank[:, 256 * j:256 * j + 256],
                                                          XT[:, k, t * P:(t + 1) * P], w[:, k, 0:256],
                                                          start=(k == 0), stop=(k == KT - 1))
                        mm.then_inc(bank_full[l], 1)

            def attention(l):
                def scores(n, u):
                    b, par, i, is_mem = u
                    lo = HD * par
                    if n >= 3:
                        pe.wait_ge(probs_ready[l], 2 * (n - 2))
                    bank = PS[:, (0, 1, 7)[n % 3], :]
                    if l == 0 and n == 0:
                        wait_drained(pe, 0, ("k", 2, 0)), wait_drained(pe, 0, ("k", 2, 1))
                    if is_mem:
                        wait_drained(pe, l, ("m", 0, 0)), wait_drained(pe, l, ("m", 0, 1))
                    for j in range(2):
                        if is_mem:
                            mm = nc.tensor.matmul(bank[:, 256 * j:256 * j + 256],
                                                  qm[l][lo:lo + HD, j, b * P:(b + 1) * P],
                                                  memk[lo:lo + HD, j, :], start=True, stop=True)
                        else:
                            tile = 2 * i + j
                            keys = kT[lo:lo + HD, tile, :].rearrange("p (r c) -> p r c", c=GRID_W)
                            mm = nc.tensor.matmul(bank[:, 256 * j:256 * j + 256],
                                                  qT[lo:lo + HD, tile, b * P:(b + 1) * P],
                                                  keys[:, :, KEY0[b]:KEY0[b] + KC], start=True, stop=True)
                    mm.then_inc(scores_full[l], 1)

                def turn(n, u):
                    pe.wait_ge(probs_ready[l], 2 * (n + 1))
                    if n >= 2:
                        pe.wait_ge(probsT_ready[l], n - 1)
                    for j in range(4):
                        mm = nc.tensor.transpose(PS[:, 2 + n % 2, j * P:(j + 1) * P],
                                                 prob[l][:, n % 3, j * P:(j + 1) * P], ident)
                    mm.then_inc(probsT_full[l], 1)

                def values(n, u):
                    b, par, i, is_mem = u
                    pe.wait_ge(probsT_ready[l], n + 1)
                    if (is_mem or i == 0) and group_no(l, u) >= 2:
                        pe.wait_ge(heads_ready[l], group_no(l, u) - 1)
                    if l == 0 and n == 0:
                        pe.wait_ge(v_in, 16 * 2 * NBLK)
                    for j in range(2):
                        dst = PS[:, 4 + par, (2 * i + j) * HD:(2 * i + j + 1) * HD]
                        h = 2 * (2 * i + j) + par
                        for kt in range(2):
                            vals = (memv[:, kt, h * HD:(h + 1) * HD] if is_mem
                                    else v_win[:, 2 * b + kt, h * HD:(h + 1) * HD])
                            mm = nc.tensor.matmul(dst, probT[l][:, n % 2, (2 * j + kt) * P:(2 * j + kt + 1) * P], vals,
                                                  start=(kt == 0), stop=(kt == 1))
                    mm.then_inc(values_summed[l], 1)

                def mix(u):
                    b, par, _, is_mem = u
                    pe.wait_ge(heads_ready[l], group_no(l, u) + 1)
                    done = last_mix_round(l, block_no(l, u) - 1) if block_no(l, u) else 0
                    for r in range(1 if is_mem else 2):
                        if done + r:
                            pe.wait_ge(mix_ready[l], done + r)
                        for i in range(2 if is_mem else 3):
                            f = (3 * r + i) * P
                            src = o_mem[l][:, b, f:f + P] if is_mem else o_na[:, b, f:f + P]
                            mm = nc.tensor.matmul(PS[:, 6, i * P:(i + 1) * P], src, ident if is_mem else anti,
                                                  start=True, stop=True)
                        mm.then_inc(mix_full[l], 1)

                for s, at in steps(l):
                    if at(0):
                        scores(s, at(0))
                    if s in (1, 2):
                        keep_busy(2)
                    if at(2):
                        turn(s - 2, at(2))
                    if at(3):
                        values(s - 3, at(3))
                    if ends_group(at(5)) and at(5)[1] == 1:
                        mix(at(5))

            def mlstm():
                j = jobs[1]
                for r, src in enumerate((g_in, g_fo)):
                    if r == 0:
                        pe.wait_ge(gates_set, 3)
                    bank = begin(1, ("rows", r))
                    for t in range(TT):
                        mm = nc.tensor.transpose(bank[0:64, t * P:(t + 1) * P], src[:, t, :], ident)
                    mm.then_inc(bank_full[1], 1)
                pe.wait_ge(rows_set, 1)
                bank = begin(1, ("cols", 0))
                for g, src in enumerate((r_a, r_m)):
                    for t in range(TT):
                        mm = nc.tensor.transpose(bank[:, g * 256 + t * 64:g * 256 + (t + 1) * 64],
                                                 src[0:64, t * P:(t + 1) * P], ident[0:64, 0:64])
                mm.then_inc(bank_full[1], 1)
                wait_drained(pe, 1, ("cols", 0))
                pe.wait_ge(silu_done, 12)
                parts = [[(0, 0, 128), (1, 0, 64)], [(1, 64, 128), (2, 0, 128)],
                         [(3, 0, 128), (4, 0, 64)], [(4, 64, 128), (5, 0, 128)]]
                for h in range(ML_HEADS + 1):
                    if h < ML_HEADS:
                        for d in range(2):
                            n = 2 * h + d
                            if n >= 2:
                                pe.wait_ge(e_ready, n - 1)
                            row = 32 * d + h
                            nc.tensor.matmul(PS[:, (0, 7)[d], :], ident[0:64, row:row + 1].to_broadcast([64, P]),
                                             r_M[0:64, :], start=True, stop=True).then_inc(r_full, 1)
                        for i in range(TT):
                            if h:
                                pe.wait_ge(w_ready, TT * (h - 1) + i + 1)
                            for a, (tile, lo, hi) in enumerate(parts[h]):
                                mm = nc.tensor.matmul(PS[:, 1 + i, :], qk[lo:hi, 6 + tile, i * P:(i + 1) * P],
                                                      qk[lo:hi, tile, :], start=(a == 0), stop=(a == 1))
                            mm.then_inc(s_full, 1)
                    if h >= 1:
                        g = h - 1
                        pe.wait_ge(w_ready, TT * (g + 1))
                        for t in range(TT):
                            n = TT * g + t
                            if n >= 2:
                                pe.wait_ge(h_added, n - 1)
                            bank = PS[:, 5 + n % 2, :]
                            for d in range(2):
                                tiles = range(0, t + 1) if d == 0 else range(t, TT)
                                for i in tiles:
                                    mm = nc.tensor.matmul(bank[:, 256 * d:256 * d + VW], W[:, d, i, t * P:(t + 1) * P],
                                                          v_ml[:, i, g, :], start=(i == tiles[0]), stop=(i == tiles[-1]))
                            mm.then_inc(num_full, 1)
                pe.wait_ge(h_ready, TT)
                for i in range(6):
                    bank = begin(1, ("hT", i))
                    for t in range(TT):
                        mm = nc.tensor.transpose(bank[:, t * P:(t + 1) * P], H[:, t, i * P:(i + 1) * P], ident)
                    mm.then_inc(bank_full[1], 1)
                wait_drained(pe, 1, ("hT", 4))
                wait_drained(pe, 1, ("hT", 5))

            def output_projection(l):
                for c in range(4):
                    n = n_proj[l] + c
                    pe.wait_ge(chunk_in[l][n % 2], 16 * (n // 2 + 1))
                    w = chunk_buf[n % 2][:, 0:KT * 256].rearrange("p (k f) -> p k f", f=256)
                    for s in range(2):
                        bank = begin(l, ("out", c, s))
                        for j in range(2):
                            t = 2 * s + j
                            for k in range(KT):
                                mm = nc.tensor.matmul(bank[:, 256 * j:256 * j + 256], mixT[:, k, t * P:(t + 1) * P],
                                                      w[:, k, :], start=(k == 0), stop=(k == KT - 1))
                        mm.then_inc(bank_full[l], 1)

            def routing(l, picks):
                pe.wait_ge(route_in, 64 * l + 64)
                bank = begin(l, ("logitsT", 0))
                for k in range(KT):
                    wait_drained(pe, l, ("x1T", k))
                    mm = nc.tensor.matmul(bank[0:NG + NE, :], wr[:, k, :], XT[:, k, :],
                                          start=(k == 0), stop=(k == KT - 1))
                mm.then_inc(bank_full[l], 1)
                wait_drained(pe, l, ("logitsT", 0))
                bank = begin(l, ("logits", 0))
                for t in range(TT):
                    mm = nc.tensor.transpose(bank[:, 36 * t:36 * t + 36], logitsT[:, t * P:(t + 1) * P],
                                             ident[0:NG + NE, 0:NG + NE])
                mm.then_inc(bank_full[l], 1)
                if l == 0:
                    pe.wait_ge(const16_set, 1)
                pe.wait_ge(picks_ready, l + 1)
                bank = begin(l, ("rank", 0))
                for t in range(TT):
                    for t2 in range(t + 1):
                        nc.tensor.matmul(bank[:, NE * t:NE * t + NE], earlier16 if t2 == t else ones16, picks[:, t2, :],
                                         start=(t2 == 0), stop=(t2 == t))
                for t in range(TT):
                    mm = nc.tensor.matmul(bank[:, NE * TT:NE * TT + NE], ones16, picks[:, t, :],
                                          start=(t == 0), stop=(t == TT - 1))
                mm.then_inc(bank_full[l], 1)

            def turn_rows(l, g):
                bank = PS[:, 0, :].bitcast(F16)
                for k in range(KT):
                    for a in range(2):
                        mm = nc.tensor.transpose(bank[:, k * P + a * CAP:k * P + (a + 1) * CAP],
                                                 xg[:, a * D + k * P:a * D + (k + 1) * P], ident16[0:CAP, 0:CAP])
                mm.then_inc(xgT_full[l], 1)

            def expert(l, e, q):
                n, g0 = blocks_of(pe, e)
                split = pe.to_reg(3 * e + 3)
                settle(pe)
                pe.wait_ge(w_low[l], split)
                with pe.Fori(0, n) as i:
                    g = g0 + i
                    now, gathered = pe.to_reg(g), pe.to_reg(16 * (g + 1))
                    settle(pe)
                    pe.wait_ge(xgT_ready[l], now)
                    for bank, piece, full in ((1, 0, h1_full), (2, 1, h3_full)):
                        for k in range(KT):
                            for a in range(2):
                                mm = nc.tensor.matmul(PS[:, bank, :], xgT[:, k, :],
                                                      parts[q][piece][:, a, k * FE:(k + 1) * FE],
                                                      start=(k == 0 and a == 0), stop=(k == KT - 1 and a == 1))
                        mm.then_inc(full[l], 1)
                    settle(pe)
                    pe.wait_ge(x_gathered[l], gathered)
                    turn_rows(l, g + 1)
                    settle(pe)
                    pe.wait_ge(h_low[l], now)
                    bank = PS[:, 3, :].bitcast(F16)
                    for k in range(FT):
                        for a in range(2):
                            mm = nc.tensor.transpose(bank[:, k * P + a * CAP:k * P + (a + 1) * CAP],
                                                     h_parts[:, a, k * P:(k + 1) * P], ident16[0:CAP, 0:CAP])
                    mm.then_inc(hT_full[l], 1)
                    settle(pe)
                    pe.wait_ge(hT_ready[l], now)
                    pe.wait_ge(y_ready[l], now)
                    for c in range(2):
                        for k in range(FT):
                            for a in range(2):
                                mm = nc.tensor.matmul(PS[:, 4 + c, :], hT[:, k, :],
                                                      parts[q][2][:, a, k * D + c * FE:k * D + (c + 1) * FE],
                                                      start=(k == 0 and a == 0), stop=(k == FT - 1 and a == 1))
                    mm.then_inc(y_full[l], 1)

            pe.wait_ge(const_in, 32)
            for l in range(DEPTH):
                if l == 0:
                    pe.wait_ge(x_in, 16)
                transposed_x(l, "xT")
                if l == 0:
                    memory_kv()
                projection(l)
                tail = jobs[l].by[:jobs[l].number[("out", 0, 0) if l == 0 else ("rows", 0)]][-8:]
                for name in sorted(tail, key=lambda name: jobs[l].number[name] % 8 != 6):
                    wait_drained(pe, l, name)
                    if jobs[l].number[name] % 8 == 6:
                        keep_busy(2)
                attention(l)
                pe.wait_ge(mix_ready[l], last_mix_round(l, len(block_kinds(l)) - 1))
                if l == 1:
                    mlstm()
                output_projection(l)
                transposed_x(l, "x1T")
                routing(l, routing_views(l)["picks"])
                pe.wait_ge(blocks_ready, l + 1)
                wait_drained(pe, l, ("rank", 0))
                pe.wait_ge(x_gathered[l], 16)
                turn_rows(l, 1)
                with pe.Fori(0, NE, 2) as e:
                    for q in range(2):
                        expert(l, e + q, q)

        w13_v = [w.rearrange("l e (p k) f -> (l e) p (k f)", k=KT) for w in (moe_w1, moe_w3)]
        w2_v = moe_w2.rearrange("l e (k p) f -> (l e) p k f", p=P)

        @block.sync
        def _(sp):
            def load_chunk(l, n):
                if n >= 2:
                    if n - 2 < n_proj[l]:
                        kind, c = chunks[l][n - 2][:2]
                        wait_full(sp, l, (kind, c, 1))
                    else:
                        wait_full(sp, l, ("out", n - 2 - n_proj[l], 1))
                elif l == 1:
                    pass
                if n < n_proj[l]:
                    _, _, col, width = chunks[l][n]
                    src = (na_w_in, ml_w_in)[l][0].rearrange("(k p) f -> p k f", p=P)[:, :, col:col + width]
                else:
                    c, width = n - n_proj[l], 256
                    src = w_out[l].rearrange("(k p) f -> p k f", p=P)[:, :, 256 * c:256 * c + 256]
                dst = chunk_buf[n % 2][:, 0:KT * width].rearrange("p (k f) -> p k f", f=width)
                sp.dma_start(dst, src).then_inc(chunk_in[l][n % 2], 16)

            def load_piece(l, e, piece):
                if isinstance(e, int):
                    if e:
                        sp.wait_ge(w_low[l], 3 * (e - 1) + piece + 1)
                else:
                    sp.wait_ge(w_low[l], sp.to_reg(3 * (e - 1) + piece + 1))
                if piece < 2:
                    src = w13_v[piece][bass.ds(l * NE + e, 1)].rearrange("a p n -> (a p) n")
                    sp.dma_start(staged[piece], src).then_inc(w_in[l][piece], 16)
                else:
                    src = w2_v[bass.ds(l * NE + e, 1)].rearrange("a p k f -> (a p) k f")
                    sp.dma_start(staged[2].rearrange("p (k f) -> p k f", k=FT), src).then_inc(w_in[l][2], 16)

            def store_blocks(l, e):
                n, g0 = blocks_of(sp, e)
                with sp.Fori(0, n) as i:
                    g = g0 + i
                    sp.wait_ge(y_ready[l], g)
                    sp.dma_start(y_rows[bass.ds((g - 1) * CAP, CAP), :], y_blk).then_inc(y_stored[l], 16)

            sp.dma_start(X[:], x[0].rearrange("(t p) d -> p t d", p=P)).then_inc(x_in, 16)
            sp.dma_start(CF[:], const_f).then_inc(const_in, 16)
            sp.dma_start(ctok[:], const_tok).then_inc(const_in, 16)
            sp.dma_start(mem_in, mem[0].rearrange("(m p) d -> p m d", p=P)).then_inc(mem_in_s, 16)
            sp.dma_start(w_kv, w_mem_kv.rearrange("(k p) f -> p k f", p=P)).then_inc(kv_in, 16)
            for l in range(DEPTH):
                if l == 1:
                    wait_x_all(sp, 0)
                    sp.dma_start(norm_g, ml_norm_g[0:1, :].partition_broadcast(P)).then_inc(mlp_in, 16)
                    sp.dma_start(g_bias, ml_gate_b.rearrange("a j h -> a (j h)")[0:1, :].partition_broadcast(P))\
                        .then_inc(mlp_in, 16)
                    for j in range(CONV_K):
                        sp.dma_start(conv_w[:, :, j], ml_conv_w[0, j].rearrange("(m p) -> p m", p=P)).then_inc(mlp_in, 16)
                    sp.dma_start(conv_b, ml_conv_b[0].rearrange("(m p) -> p m", p=P)).then_inc(mlp_in, 16)
                for n in range(n_proj[l]):
                    load_chunk(l, n)
                    if l == 0 and n == 2:
                        sp.wait_ge(pads_in, 48)
                        for r in range(ROWS):
                            src = bass.AP(tensor=rpb_pad.tensor, offset=RPB_PAD - 16 + RPB_ROW * r,
                                          ap=[[1, QC], [RPB_HEAD, NA_HEADS], [1, RPB_RUN]])
                            sp.dma_start(rpb_tab[QC * r:QC * r + QC], src).then_inc(rpb_in, 16)
                    if l == 0 and n == 5:
                        wait_drained(sp, 0, ("v", 2, 0)), wait_drained(sp, 0, ("v", 2, 1))
                        sp.dma_start(v_rows.rearrange("(t p) f -> p t f", p=P), v_nat).then_inc(v_out, 16)
                        wait_drained(sp, 0, ("memk", 0)), wait_drained(sp, 0, ("memv", 0))
                        sp.wait_ge(v_out, 16)
                        rows = v_rows.rearrange("(r c) f -> r c f", c=GRID_W)
                        for b in range(NBLK):
                            for j in range(2):
                                sp.dma_start(v_win[:, 2 * b + j, :],
                                             rows[4 * j:4 * j + 4, KEY0[b]:KEY0[b] + KC, :]).then_inc(v_in, 16)
                load_chunk(l, n_proj[l])
                load_chunk(l, n_proj[l] + 1)
                sp.dma_start(wr[:, :, 0:NG], moe_wg[l].rearrange("(k p) g -> p k g", p=P)).then_inc(route_in, 16)
                sp.dma_start(wr[:, :, NG:], moe_we[l].rearrange("(k p) g -> p k g", p=P)).then_inc(route_in, 16)
                sp.dma_start(rbias[:, 0:NG], moe_bg[l:l + 1, :].partition_broadcast(P)).then_inc(route_in, 16)
                sp.dma_start(rbias[:, NG:], moe_be[l:l + 1, :].partition_broadcast(P)).then_inc(route_in, 16)
                if l == 0:
                    sp.wait_ge(mix_ready[l], last_mix_round(l, len(block_kinds(l)) - 1))
                else:
                    wait_full(sp, l, ("hT", 5))
                for piece in range(3):
                    load_piece(l, 0, piece)
                    if piece == 0:
                        load_chunk(l, n_proj[l] + 2)
                load_chunk(l, n_proj[l] + 3)
                for piece in range(3):
                    load_piece(l, 1, piece)
                wait_full(sp, l, ("out", 2, 1))
                params = ln1_params(l)
                sp.dma_start(params[:, 0, :], ln1_g[l:l + 1, :].partition_broadcast(P)).then_inc(ln_in, 16)
                sp.dma_start(params[:, 1, :], ln1_b[l:l + 1, :].partition_broadcast(P)).then_inc(ln_in, 16)
                for piece in range(3):
                    load_piece(l, 2, piece)
                sp.sem_inc(y_stored[l], 16)
                sp.wait_ge(blocks_ready, l + 1)
                with sp.Fori(0, NE - 3) as e:
                    store_blocks(l, e)
                    for piece in range(3):
                        load_piece(l, e + 3, piece)
                for e in range(NE - 3, NE):
                    store_blocks(l, e)
                    if e == NE - 3:
                        sp.wait_ge(w_low[l], 3 * NE)
                        sp.dma_start(ln2_p[:, 0, :], ln2_g[l:l + 1, :].partition_broadcast(P)).then_inc(ln2_in, 16)
                        sp.dma_start(ln2_p[:, 1, :], ln2_b[l:l + 1, :].partition_broadcast(P)).then_inc(ln2_in, 16)
                end = blocks_end(sp)
                sp.wait_ge(y_ready[l], end)
                sp.dma_start(y_rows[bass.ds((end - 1) * CAP, CAP), :], y_blk).then_inc(y_stored[l], 16)
            for t in range(TT):
                wait_x(sp, 1, t, True)
                sp.dma_start(out[0, t * P:(t + 1) * P, :], X[:, t, :]).then_inc(out_done, 16)
            sp.wait_ge(out_done, 16 * TT)

        @block.scalar
        def _(act):
            def drain(l, name, dst, func=ACT.Copy):
                wait_full(act, l, name)
                nc.scalar.activation(dst, bank_of(l, name), func).then_inc(act_drained[l], 1)

            def blocked(dst):
                return dst.rearrange("p (b r c) -> p b r c", r=ROWS, c=QC)

            def attention(l):
                for s, at in steps(l):
                    u = at(0)
                    if u:
                        if s >= 3:
                            act.wait_ge(probsT_full[l], s - 2)
                        act.wait_ge(max_ready[l], s + 1)
                        for j in range(2):
                            src = PS[:, (0, 1, 7)[s % 3], 256 * j:256 * j + 256] if u[3] \
                                else sneg[:, s % 3, 256 * j:256 * j + 256]
                            nc.scalar.activation(prob[l][:, s % 3, 256 * j:256 * j + 256], src, ACT.Exp,
                                                 bias=mneg[:, s, j:j + 1], scale=HD ** -0.5 if u[3] else -1.0,
                                                 accum_out=msum[:, s, j:j + 1]).then_inc(probs_ready[l], 1)
                    if at(2):
                        n = s - 2
                        act.wait_ge(probsT_full[l], n + 1)
                        if n >= 2:
                            act.wait_ge(values_summed[l], n - 1)
                        nc.scalar.activation(probT[l][:, n % 2, :], PS[:, 2 + n % 2, :], ACT.Copy)\
                            .then_inc(probsT_ready[l], 1)

            def high_part(l, e, piece, q):
                act.wait_ge(w_in[l][piece], 16 * (e + 1) if isinstance(e, int) else act.to_reg(16 * (e + 1)))
                for lo, hi in ACT_RUNS[piece]:
                    nc.scalar.activation(parts[q][piece][:, 0, lo:hi], staged[piece][:, lo:hi], ACT.Copy,
                                         scale=W_SCALE).then_inc(w_high[l], 1)

            def square_root(var, sd, ready, done, count):
                act.wait_ge(ready, count)
                nc.scalar.activation(sd, var, ACT.Sqrt).then_inc(done, 1)

            for l in range(DEPTH):
                for k in range(0, KT, 2):
                    drain(l, ("xT", k), XT[:, k, :])
                if l == 0:
                    for k2 in (0, 2):
                        drain(0, ("memT", k2), memT[:, 2 * k2:2 * k2 + 2, :].rearrange("p a b -> p (a b)"))
                    drain(0, ("memk", 0), memk[:].rearrange("p a b -> p (a b)"))
                    for kind, c, _, _ in chunks[0]:
                        name = (kind, c, 0)
                        wait_full(act, 0, name)
                        bank = bank_of(0, name)
                        if kind == "v":
                            ins = nc.scalar.activation(v_nat[:, 0:2, 256 * c:256 * c + 256],
                                                       bank.rearrange("p (t f) -> p t f", t=2), ACT.Copy)
                        elif kind == "q":
                            ins = nc.scalar.activation(
                                blocked(qT[:, 2 * c, :]),
                                bank.rearrange("p (r b c) -> p b r c", b=NBLK, c=QC)[:, :, ::-1, ::-1], ACT.Copy)
                        elif kind == "k":
                            ins = nc.scalar.activation(kT[:, 2 * c, :], bank, ACT.Copy)
                        else:
                            ins = nc.scalar.activation(qm0[:, 0, :], bank, ACT.Copy)
                        ins.then_inc(act_drained[0], 1)
                else:
                    def silu(m):
                        act.wait_ge(conv_done, m + 1)
                        nc.scalar.activation(qk[:, m, :], qk[:, m, :], ACT.Silu).then_inc(silu_done, 1)

                    act.wait_ge(pads_zero, 1)
                    for m in range(12):
                        if m >= 4:
                            act.wait_ge(conv_done, m - 3)
                        kind, c, s = "qk"[m // 6], (m % 6) // 2, m % 2
                        drain(1, (kind, c, s), pre[:, m % 4, 2:T + 2])
                        if m >= 2:
                            silu(m - 2)
                    for s in range(2):
                        drain(1, ("m", 0, s), qm1[:, s, :])
                    silu(10)
                    silu(11)
                    for c in range(3):
                        for s in range(2):
                            name = ("v", c, s)
                            wait_full(act, 1, name)
                            bank = bank_of(1, name).rearrange("p (t f) -> p t f", t=2)
                            lo = 256 * c
                            while lo < 256 * c + 256:
                                h = lo // ML_DH
                                hi = min(256 * c + 256, ML_DH * (h + 1))
                                ins = nc.scalar.activation(
                                    v_ml[:, 2 * s:2 * s + 2, h, lo - ML_DH * h:hi - ML_DH * h],
                                    bank[:, :, lo - 256 * c:hi - 256 * c], ACT.Copy)
                                lo = hi
                            ins.then_inc(act_drained[1], 1)
                    for c in range(3):
                        for s in range(2):
                            name = ("o", c, s)
                            wait_full(act, 1, name)
                            nc.scalar.activation(o_gate[:, 2 * s:2 * s + 2, 256 * c:256 * c + 256],
                                                 bank_of(1, name).rearrange("p (t f) -> p t f", t=2), ACT.Sigmoid)\
                                .then_inc(act_drained[1], 1)
                    act.wait_ge(lf_abs, 1)
                    nc.scalar.activation(g_abs, g_abs, ACT.Exp, scale=-1.0).then_inc(lf_ln, 1)
                    act.wait_ge(lf_abs, 2)
                    nc.scalar.activation(g_ln, g_abs, ACT.Ln).then_inc(lf_ln, 1)
                attention(l)
                if l == 1:
                    act.wait_ge(mcol_set, 1)
                    nc.scalar.activation(em, mcol, ACT.Exp, scale=-1.0).then_inc(em_set, 1)
                    for h in range(ML_HEADS):
                        for d in range(2):
                            n = 2 * h + d
                            act.wait_ge(r_masked, n + 1)
                            if h:
                                act.wait_ge(w_ready, TT * h)
                            for i in range(TT):
                                col = acol[:, i, 4 * d + h:4 * d + h + 1]
                                lo, hi = (i + 1, TT) if d == 0 else (0, i)
                                if hi > lo:
                                    nc.scalar.activation(E[:, d, i, lo * P:hi * P], PS[:, (0, 7)[d], lo * P:hi * P],
                                                         ACT.Exp, bias=col)
                                ins = nc.scalar.activation(E[:, d, i, i * P:(i + 1) * P], Rd[:, d, i * P:(i + 1) * P],
                                                           ACT.Exp, bias=col)
                            ins.then_inc(e_ready, 1)
                    square_root(ml_rstd, ml_rstd, ml_var, ml_sd, 1)
                    for i in range(0, 6, 2):
                        drain(1, ("hT", i), mixT[:, i, :])
                for e, piece in EARLY:
                    high_part(l, e, piece, e)
                square_root(ln_ve, ln_sd, var_ready, sd_ready, l + 1)
                for t in range(TT):
                    if t in NORM1_SHARED:
                        act.wait_ge(moments, l + 1)
                        nc.scalar.activation(X[:, t, :], X[:, t, :], ACT.Identity, scale=ln_rs[:, t:t + 1],
                                             bias=ln_nm[:, t:t + 1]).then_inc(normed, 1)
                for t in range(TT):
                    if t == TT - 1:
                        for k in range(0, KT, 2):
                            drain(l, ("x1T", k), XT[:, k, :])
                    wait_x(act, l, t)
                    nc.scalar.activation(x_parts(t)[:, 0], by_tile(X[:, t, :]), ACT.Copy, scale=X_SCALE)\
                        .then_inc(x_high, 1)
                rv = routing_views(l)
                act.wait_ge(gdiff, l + 1)
                nc.scalar.activation(rv["ge"], rv["gd"], ACT.Exp).then_inc(gexp, 1)
                act.wait_ge(ediff, l + 1)
                nc.scalar.activation(rv["e2"], rv["ed"], ACT.Exp).then_inc(eexp, 1)

                act.wait_ge(x_stored, 16 * (l + 1))
                high_part(l, 1, 2, 1)

                def rows_out(g):
                    act.wait_ge(xgT_full[l], g)
                    nc.scalar.activation(xgT.rearrange("p k s -> p (k s)"), PS[:, 0, :].bitcast(F16), ACT.Copy)\
                        .then_inc(xgT_ready[l], 1)

                def outputs_up(g, stored):
                    act.wait_ge(y_full[l], g)
                    act.wait_ge(y_stored[l], stored)
                    nc.scalar.activation(y_blk.rearrange("p (a b) -> p a b", b=512), PS[CAP:P, 4:6, :], ACT.Copy)\
                        .then_inc(y_upper[l], 1)

                def expert(e):
                    n, g0 = blocks_of(act, e)
                    with act.Fori(0, n) as i:
                        g = g0 + i
                        nc.scalar.activation(warm, ones[0:1, 0:1], ACT.Silu)
                        outputs_up(g, g * 16)
                        for full, bank, dst, upper in ((h1_full, 1, hs, h1_upper), (h3_full, 2, h3, h3_upper)):
                            act.wait_ge(full[l], g)
                            nc.scalar.activation(dst, PS[CAP:P, bank, :], ACT.Copy).then_inc(upper[l], 1)
                        act.wait_ge(h1_summed[l], g)
                        nc.scalar.activation(hs, hs, ACT.Silu, scale=1 / (X_SCALE * W_SCALE))\
                            .then_inc(silu_ready[l], 1)
                        rows_out(g + 1)
                        act.wait_ge(h_ready_e[l], g)
                        nc.scalar.activation(h_parts[:, 0, :], h3, ACT.Copy).then_inc(h_high[l], 1)
                        act.wait_ge(hT_full[l], g)
                        nc.scalar.activation(hT.rearrange("p k s -> p (k s)"), PS[:, 3, 0:256].bitcast(F16), ACT.Copy)\
                            .then_inc(hT_ready[l], 1)
                    return g0 + n

                act.wait_ge(blocks_ready, l + 1)
                rows_out(1)
                with act.Fori(0, NE - 2, 2) as e:
                    for q in range(2):
                        after = expert(e + q)
                        for piece in range(3):
                            if piece == 2:
                                act.wait_ge(y_full[l], act.to_reg(after))
                            high_part(l, e + q + 2, piece, q)
                expert(NE - 2)
                expert(NE - 1)
                end = blocks_end(act)
                outputs_up(end, end * 16)
                for t in range(TT):
                    nc.scalar.activation(X[:, t, :], X[:, t, :], ACT.Copy, scale=ALPHA).then_inc(x_alpha, 1)
                for step, t in NORM2_ACT:
                    if step == "root":
                        act.wait_ge(var2_ready, TT * l + t + 1)
                        nc.scalar.activation(ln_sd[:, t:t + 1], ln_ve[:, t:t + 1], ACT.Sqrt).then_inc(sd2_ready, 1)
                    else:
                        act.wait_ge(moments2, len(NORM2_SHARED) * l + NORM2_SHARED.index(t) + 1)
                        nc.scalar.activation(X[:, t, :], X[:, t, :], ACT.Identity, scale=ln_rs[:, t:t + 1],
                                             bias=ln_nm[:, t:t + 1]).then_inc(normed2, 1)

        @block.vector
        def _(dve):
            done = [0]

            def link(ins):
                done[0] += 1
                ins.then_inc(dve_step, 1)
                dve.wait_ge(dve_step, done[0])

            def drain(l, name, dst):
                wait_full(dve, l, name)
                nc.vector.tensor_copy(dst, bank_of(l, name)).then_inc(dve_drained[l], 1)

            def softmax_front(l, n, u):
                b, par, i, is_mem = u
                dve.wait_ge(scores_full[l], n + 1)
                bank = PS[:, (0, 1, 7)[n % 3], :].rearrange("p (j k) -> p j k", j=2)
                if is_mem:
                    m = n % 8
                    link(nc.vector.tensor_reduce(mraw[:, m, :], bank, AX, ALU.max))
                    nc.vector.tensor_scalar(mneg[:, n, :], mraw[:, m, :], -(HD ** -0.5), None, ALU.mult)\
                        .then_inc(max_ready[l], 1)
                    return
                if n >= 3:
                    dve.wait_ge(probs_ready[l], 2 * (n - 2))
                if n == 0:
                    dve.wait_ge(bias_built, 3)
                h = 4 * i + par
                dst = sneg[:, n % 3, :].rearrange("p (j k) -> p j k", j=2)
                link(nc.vector.scalar_tensor_tensor(
                    out=dst, in0=bank, scalar=-(HD ** -0.5), in1=bias_tab[:, VARIANT[b], h:h + 3:2, :],
                    op0=ALU.mult, op1=ALU.subtract))
                nc.vector.tensor_reduce(mneg[:, n, :], dst, AX, ALU.min).then_inc(max_ready[l], 1)

            def heads_out(l, n, u):
                b, par, i, is_mem = u
                k = 2 if is_mem else 6
                first = n - (0 if is_mem else 2)
                dve.wait_ge(probs_ready[l], 2 * (n + 1))
                r = rsum[:, group_no(l, u) % 2, 0:k]
                link(nc.vector.reciprocal(r, msum[:, first:n + 1, :].rearrange("p a b -> p (a b)")))
                dve.wait_ge(values_summed[l], n + 1)
                dst = (o_mem[l][:, b, :] if is_mem else o_na[:, b, :]).rearrange("p (s q d) -> p s q d", q=2, d=HD)
                src = PS[:, 4 + par, 0:k * HD].rearrange("p (s d) -> p s d", d=HD)
                nc.vector.tensor_tensor(dst[:, :, par, :], src, r.unsqueeze(2).to_broadcast([P, k, HD]), ALU.mult)\
                    .then_inc(heads_ready[l], 1)

            def mix_out(l, u):
                b, _, _, is_mem = u
                done_ = last_mix_round(l, block_no(l, u) - 1) if block_no(l, u) else 0
                for r in range(1 if is_mem else 2):
                    dve.wait_ge(mix_full[l], done_ + r + 1)
                    if is_mem:
                        ins = nc.vector.tensor_copy(mixT[:, 6:8, b * P:(b + 1) * P],
                                                    PS[:, 6, 0:256].rearrange("p (i c) -> p i c", i=2))
                    else:
                        for i in range(3):
                            dst = mixT[:, 3 * r + i, :].rearrange("p (r c) -> p r c", c=GRID_W)[:, :, QC * b:QC * b + QC]
                            ins = nc.vector.tensor_copy(dst, PS[:, 6, i * P:(i + 1) * P].rearrange("p (r c) -> p r c", c=QC))
                    ins.then_inc(mix_ready[l], 1)

            def attention(l):
                for s, at in steps(l):
                    if at(0):
                        softmax_front(l, s, at(0))
                    if ends_group(at(4)):
                        heads_out(l, s - 4, at(4))
                    if ends_group(at(5)) and at(5)[1] == 1:
                        mix_out(l, at(5))

            def low_part(l, e, piece, q):
                count = (lambda v: v) if isinstance(e, int) else dve.to_reg
                high, low = parts[q][piece][:, 0, :], parts[q][piece][:, 1, :]
                if piece == 0:
                    dve.wait_ge(w_in[l][0], count(16 * (e + 1)))
                    nc.vector.tensor_scalar(high[:, 0:DVE_COLS], staged[0][:, 0:DVE_COLS], W_SCALE, None, ALU.mult)\
                        .then_inc(w_first, 1)
                    dve.wait_ge(w_first, count(l * NE + e + 1))
                    nc.vector.scalar_tensor_tensor(out=low[:, 0:DVE_COLS], in0=staged[0][:, 0:DVE_COLS],
                                                   scalar=W_SCALE, in1=high[:, 0:DVE_COLS],
                                                   op0=ALU.mult, op1=ALU.subtract)
                for j, (lo, hi) in enumerate(ACT_RUNS[piece]):
                    dve.wait_ge(w_high[l], count(N_RUNS * e + sum(len(r) for r in ACT_RUNS[:piece]) + j + 1))
                    ins = nc.vector.scalar_tensor_tensor(out=low[:, lo:hi], in0=staged[piece][:, lo:hi],
                                                         scalar=W_SCALE, in1=high[:, lo:hi],
                                                         op0=ALU.mult, op1=ALU.subtract)
                ins.then_inc(w_low[l], 1)

            def finish(l, t, params):
                link(nc.vector.scalar_tensor_tensor(out=X[:, t, :], in0=X[:, t, :], scalar=ln_mv[:, t, 0:1],
                                                    in1=params[:, 0, :], op0=ALU.subtract, op1=ALU.mult))
                return nc.vector.scalar_tensor_tensor(out=X[:, t, :], in0=X[:, t, :], scalar=ln_rs[:, t:t + 1],
                                                      in1=params[:, 1, :], op0=ALU.mult, op1=ALU.add)

            def norm1(l):
                for t in range(TT):
                    ins = nc.vector.bn_aggr(ln_mv[:, t, :], ln_st[:, t, :, :].rearrange("p a s -> p (a s)"))
                link(ins)
                nc.vector.tensor_scalar(ln_ve, ln_mv[:, :, 1], LN_EPS, None, ALU.add).then_inc(var_ready, 1)
                dve.wait_ge(sd_ready, l + 1)
                link(nc.vector.reciprocal(ln_rs, ln_sd))
                nc.vector.scalar_tensor_tensor(out=ln_nm, in0=ln_mv[:, :, 0], scalar=-1.0, in1=ln_rs,
                                               op0=ALU.mult, op1=ALU.mult).then_inc(moments, 1)
                dve.wait_ge(ln_in, 32 * (l + 1))
                for t in range(TT):
                    if t not in NORM1_SHARED:
                        finish(l, t, ln1_params(l)).then_inc(x1_dve, 1)

            def combine_and_norm2(l):
                def front(t):
                    dve.wait_ge(y_got_in[t], 32 * l + 32)
                    dve.wait_ge(x_alpha, TT * l + t + 1)
                    for k in range(2):
                        link(nc.vector.scalar_tensor_tensor(out=X[:, t, :], in0=y_got[:, 2 * t + k, :],
                                                            scalar=gates[:, t, k:k + 1], in1=X[:, t, :],
                                                            op0=ALU.mult, op1=ALU.add))
                    for a in range(2):
                        ins = nc.vector.bn_stats(ln_st[:, t, a, :], X[:, t, 512 * a:512 * a + 512])
                    link(ins)
                    link(nc.vector.bn_aggr(ln_mv[:, t, :], ln_st[:, t, 0:2, :].rearrange("p a s -> p (a s)")))
                    nc.vector.tensor_scalar(ln_ve[:, t:t + 1], ln_mv[:, t, 1:2], LN_EPS, None, ALU.add)\
                        .then_inc(var2_ready, 1)

                def back(t):
                    dve.wait_ge(sd2_ready, TT * l + t + 1)
                    link(nc.vector.reciprocal(ln_rs[:, t:t + 1], ln_sd[:, t:t + 1]))
                    if t in NORM2_SHARED:
                        nc.vector.scalar_tensor_tensor(out=ln_nm[:, t:t + 1], in0=ln_mv[:, t, 0:1], scalar=-1.0,
                                                       in1=ln_rs[:, t:t + 1], op0=ALU.mult, op1=ALU.mult)\
                            .then_inc(moments2, 1)
                    else:
                        finish(l, t, ln2_p).then_inc(x2_dve, 1)

                dve.wait_ge(ln2_in, 32 * (l + 1))
                for t in range(TT):
                    front(t)
                    if t >= 1:
                        back(t - 1)
                back(TT - 1)

            def gate_rows():
                wait_full(dve, 1, ("gates", 0))
                dve.wait_ge(mlp_in, 16 * 8)
                done[0] += 1
                nc.vector.tensor_tensor(g_tok, bank_of(1, ("gates", 0))[:, 0:64].rearrange("p (t g) -> p t g", t=TT),
                                        g_bias.unsqueeze(1).to_broadcast([P, TT, 16]), ALU.add)\
                    .then_inc(dve_drained[1], 1)
                done[0] -= 1
                wait_drained(dve, 1, ("gates", 0))
                nc.vector.scalar_tensor_tensor(out=g_abs, in0=g_tok[:, :, 8:16], scalar=-1.0, in1=g_tok[:, :, 8:16],
                                               op0=ALU.mult, op1=ALU.max).then_inc(lf_abs, 1)
                split = lambda v: v.rearrange("p t (a b) -> p t a b", b=32)[:, :, :, 0:4]
                dve.wait_ge(gates_set, 2)
                for dd in range(2):
                    link(nc.vector.tensor_copy(g_in[:, :, 32 * dd:32 * dd + 4], g_tok[:, :, 4 * dd:4 * dd + 4]))

            def forget_rows():
                dve.wait_ge(lf_ln, 1)
                nc.vector.tensor_scalar(g_abs, g_abs, 1.0, None, ALU.add).then_inc(lf_abs, 1)
                dve.wait_ge(lf_ln, 2)
                for dd in range(2):
                    ins = nc.vector.scalar_tensor_tensor(
                        out=g_fo[:, :, 32 * dd:32 * dd + 4], in0=g_tok[:, :, 8 + 4 * dd:12 + 4 * dd], scalar=0.0,
                        in1=g_ln[:, :, 4 * dd:4 * dd + 4], op0=ALU.min, op1=ALU.subtract)
                ins.then_inc(gates_set, 1)

            def convolve(m):
                kind, c, s = "qk"[m // 6], (m % 6) // 2, m % 2
                wait_drained(dve, 1, (kind, c, s))
                src = pre[:, m % 4, :]
                dst = qk[:, m, :]
                link(nc.vector.tensor_scalar(dst, src[:, 0:T], conv_w[:, m, 0:1], conv_b[:, m:m + 1], ALU.mult, ALU.add))
                for j in range(1, CONV_K):
                    ins = nc.vector.scalar_tensor_tensor(out=dst, in0=src[:, j:j + T], scalar=conv_w[:, m, j:j + 1],
                                                         in1=dst, op0=ALU.mult, op1=ALU.add)
                    if j < CONV_K - 1:
                        link(ins)
                ins.then_inc(conv_done, 1)

            def mlstm():
                wait_full(dve, 1, ("rows", 1))
                li, lf = bank_of(1, ("rows", 0)), bank_of(1, ("rows", 1))
                one = ones[:, 0:1]
                for lo, step in ((0, 1), (32, -1)):
                    hi = lo + 32
                    ins = nc.vector.tensor_tensor_scan(r_F[lo:hi, ::step], one[lo:hi].to_broadcast([32, T]),
                                                       lf[lo:hi, ::step], 0.0, ALU.mult, ALU.add)
                    link(ins)
                link(nc.vector.tensor_tensor(r_a[0:64, :], li[0:64, :], r_F[0:64, :], ALU.subtract))
                for lo, step in ((0, 1), (32, -1)):
                    hi = lo + 32
                    link(nc.vector.tensor_tensor_scan(r_M[lo:hi, ::step], r_a[lo:hi, ::step], r_a[lo:hi, ::step], 0.0,
                                                      ALU.max, ALU.max))
                link(nc.vector.tensor_tensor(r_m[0:64, :], r_F[0:64, :], r_M[0:64, :], ALU.add))
                nc.vector.tensor_scalar(r_M[0:64, :], r_M[0:64, :], -1.0, None, ALU.mult).then_inc(rows_set, 1)
                dve.wait_ge(rows_set, 1)
                dve.sem_inc(dve_drained[1], 2)
                wait_full(dve, 1, ("cols", 0))
                view = bank_of(1, ("cols", 0)).rearrange("p (g t a b) -> p g t a b", g=2, t=TT, b=32)
                for dd in range(2):
                    nc.vector.tensor_copy(mcol[:, :, 4 * dd:4 * dd + 4], view[:, 1, :, dd, 0:4])
                    ins = nc.vector.tensor_copy(acol[:, :, 4 * dd:4 * dd + 4], view[:, 0, :, dd, 0:4])
                ins.then_inc(dve_drained[1], 1)
                wait_drained(dve, 1, ("cols", 0))
                dve.sem_inc(mcol_set, 1)
                dve.wait_ge(em_set, 1)
                for h in range(ML_HEADS + 1):
                    if h < ML_HEADS:
                        for d in range(2):
                            n = 2 * h + d
                            dve.wait_ge(r_full, n + 1)
                            if n >= 2:
                                dve.wait_ge(e_ready, n - 1)
                            nc.vector.tensor_tensor(Rd[:, d, :].rearrange("p (t c) -> p t c", c=P),
                                                    PS[:, (0, 7)[d], :].rearrange("p (t c) -> p t c", c=P),
                                                    ml_mask[:, d:d + 1, :].to_broadcast([P, TT, P]), ALU.add)\
                                .then_inc(r_masked, 1)
                    if h >= 1:
                        g = h - 1
                        for t in range(TT):
                            n = TT * g + t
                            dve.wait_ge(num_full, n + 1)
                            bank = PS[:, 5 + n % 2, :].rearrange("p (d f) -> p d f", d=2)
                            link(nc.vector.tensor_copy(den[:, n, :], bank[:, :, ML_DH]))
                            link(nc.vector.scalar_tensor_tensor(out=den[:, n, :], in0=den[:, n, :], scalar=-1.0,
                                                                in1=den[:, n, :], op0=ALU.mult, op1=ALU.max))
                            link(nc.vector.tensor_tensor(den[:, n, :], den[:, n, :], em[:, t, g:8:4], ALU.max))
                            link(nc.vector.reciprocal(rden[:, n, :], den[:, n, :]))
                            dst = H[:, t, ML_DH * g:ML_DH * (g + 1)]
                            link(nc.vector.tensor_scalar(dst, bank[:, 0, 0:ML_DH], rden[:, n, 0:1], None, ALU.mult))
                            nc.vector.scalar_tensor_tensor(out=dst, in0=bank[:, 1, 0:ML_DH], scalar=rden[:, n, 1:2],
                                                           in1=dst, op0=ALU.mult, op1=ALU.add).then_inc(h_added, 1)
                    if h < ML_HEADS:
                        dve.wait_ge(e_ready, 2 * h + 2)
                        for i in range(TT):
                            dve.wait_ge(s_full, TT * h + i + 1)
                            for d in range(2):
                                lo, hi = (i, TT) if d == 0 else (0, i + 1)
                                ins = nc.vector.scalar_tensor_tensor(
                                    out=W[:, d, i, lo * P:hi * P], in0=PS[:, 1 + i, lo * P:hi * P],
                                    scalar=ML_DH ** -0.5, in1=E[:, d, i, lo * P:hi * P], op0=ALU.mult, op1=ALU.mult)
                            ins.then_inc(w_ready, 1)
                dve.wait_ge(h_added, 16)
                Hh = H.rearrange("p t (h f) -> p (t h) f", f=ML_DH)
                for n in range(16):
                    ins = nc.vector.bn_stats(ml_st[:, n, :], Hh[:, n, :])
                link(ins)
                for n in range(16):
                    ins = nc.vector.bn_aggr(ml_mv[:, n, :], ml_st[:, n, :])
                link(ins)
                nc.vector.tensor_scalar(ml_rstd, ml_mv[:, :, 1], LN_EPS, None, ALU.add).then_inc(ml_var, 1)
                dve.wait_ge(ml_sd, 1)
                link(nc.vector.reciprocal(ml_rstd, ml_rstd))
                for n in range(16):
                    ins = nc.vector.tensor_scalar(Hh[:, n, :], Hh[:, n, :], ml_mv[:, n, 0:1], ml_rstd[:, n:n + 1],
                                                  ALU.subtract, ALU.mult)
                link(ins)
                dve.wait_ge(o_scaled, 1)
                for t in range(TT):
                    nc.vector.tensor_tensor(H[:, t, :], H[:, t, :], o_gate[:, t, :], ALU.mult).then_inc(h_ready, 1)
                for i in range(1, 6, 2):
                    drain(1, ("hT", i), mixT[:, i, :])

            def routing(l):
                v = routing_views(l)
                nc.vector.memset(v["gp"], -3e38)
                wait_full(dve, l, ("logits", 0))
                nc.vector.tensor_tensor(v["lg"], bank_of(l, ("logits", 0))[:, 0:144].rearrange("p (t g) -> p t g", t=TT),
                                        rbias[:].unsqueeze(1).to_broadcast([P, TT, 36]), ALU.add)\
                    .then_inc(dve_drained[l], 1)
                wait_drained(dve, l, ("logits", 0))
                link(nc.vector.tensor_copy(v["gp"][:, :, 0:NG], v["lg"][:, :, 0:NG]))
                for t in range(TT):
                    ins = nc.vector.max(v["gm"][:, t, :], v["gp"][:, t, :])
                link(ins)
                for t in range(TT):
                    ins = nc.vector.max_index(v["gi"][:, t, :], v["gm"][:, t, :], v["gp"][:, t, :])
                nc.vector.tensor_tensor(v["gd"], v["lg"][:, :, 0:NG], v["gm"][:, :, 0:1].to_broadcast([P, TT, NG]),
                                        ALU.subtract).then_inc(gdiff, 1)
                dve.wait_ge(gdiff, l + 1)
                link(nc.vector.tensor_copy(v["gif"], v["gi"][:, :, 0:1]))
                link(nc.vector.tensor_tensor(v["oh"], count[:, 0:NG].unsqueeze(1).to_broadcast([P, TT, NG]),
                                             v["gif"].to_broadcast([P, TT, NG]), ALU.is_equal))
                link(nc.vector.tensor_tensor(v["prod"], v["lg"][:, :, NG:].rearrange("p t (g e) -> p t g e", g=NG),
                                             v["oh"].unsqueeze(3).to_broadcast([P, TT, NG, EPG]), ALU.mult))
                link(nc.vector.tensor_reduce(v["es"], v["prod"].rearrange("p t g e -> p t e g"), AX, ALU.add))
                for t in range(TT):
                    ins = nc.vector.max(v["e8"][:, t, :], v["es"][:, t, :])
                link(ins)
                for t in range(TT):
                    ins = nc.vector.max_index(v["ei"][:, t, :], v["e8"][:, t, :], v["es"][:, t, :])
                link(ins)
                nc.vector.tensor_tensor(v["ed"], v["e8"][:, :, 1:2], v["e8"][:, :, 0:1], ALU.subtract)\
                    .then_inc(ediff, 1)
                link(nc.vector.tensor_copy(v["eif"], v["ei"][:, :, 0:2]))
                link(nc.vector.scalar_tensor_tensor(out=v["eid"], in0=v["gif"].to_broadcast([P, TT, 2]),
                                                    scalar=float(EPG), in1=v["eif"], op0=ALU.mult, op1=ALU.add))
                link(nc.vector.tensor_tensor(v["pick"],
                                             count.unsqueeze(1).unsqueeze(1).to_broadcast([P, TT, 2, NE]),
                                             v["eid"].unsqueeze(3).to_broadcast([P, TT, 2, NE]), ALU.is_equal))
                nc.vector.tensor_tensor(v["picks"], v["pick"][:, :, 0, :], v["pick"][:, :, 1, :], ALU.add)\
                    .then_inc(picks_ready, 1)
                dve.wait_ge(gexp, l + 1)
                link(nc.vector.tensor_reduce(v["z"], v["ge"], AX, ALU.add))
                dve.wait_ge(eexp, l + 1)
                link(nc.vector.scalar_tensor_tensor(out=v["dn"], in0=v["e2"], scalar=1.0, in1=v["z"],
                                                    op0=ALU.add, op1=ALU.mult))
                link(nc.vector.tensor_scalar(v["dn"], v["dn"], H_SCALE * W_SCALE, None, ALU.mult))
                link(nc.vector.reciprocal(gates[:, :, 0:1], v["dn"]))
                link(nc.vector.tensor_tensor(gates[:, :, 1:2], gates[:, :, 0:1], v["e2"], ALU.mult))
                wait_full(dve, l, ("rank", 0))
                bank = bank_of(l, ("rank", 0))
                link(nc.vector.tensor_scalar(v["ci"], bank[:, NE * TT:NE * TT + NE], float(CAP - 1), None, ALU.add))
                link(nc.vector.tensor_scalar(v["cs"], v["ci"], CAP.bit_length() - 1, None, ALU.logical_shift_right))
                link(nc.vector.tensor_scalar(v["nb"], v["cs"], 1.0, None, ALU.max))
                link(nc.vector.tensor_tensor_scan(v["inc"], ones[:, 0:NE], v["nb"], 1.0, ALU.mult, ALU.add))
                link(nc.vector.tensor_tensor(v["ex"], v["inc"], v["nb"], ALU.subtract))
                nc.vector.tensor_copy(blk_i[:, 0:NE], v["nb"][0:1])
                nc.vector.tensor_copy(blk_i[:, NE:2 * NE], v["ex"][0:1])
                nc.vector.tensor_copy(blk_i[:, 2 * NE:], v["inc"][0:1, NE - 1:NE]).then_inc(blocks_ready, 1)
                nc.vector.scalar_tensor_tensor(
                    out=v["slot"], in0=v["ex"].unsqueeze(1).to_broadcast([P, TT, NE]), scalar=float(CAP),
                    in1=bank[:, 0:NE * TT].rearrange("p (t e) -> p t e", t=TT), op0=ALU.mult, op1=ALU.add)\
                    .then_inc(dve_drained[l], 1)
                wait_drained(dve, l, ("rank", 0))
                link(nc.vector.tensor_tensor(v["ps"], v["pick"], v["slot"].unsqueeze(2).to_broadcast([P, TT, 2, NE]),
                                             ALU.mult))
                link(nc.vector.tensor_reduce(v["df"], v["ps"], AX, ALU.add))
                nc.vector.tensor_copy(dest[:], v["df"]).then_inc(dest_ready, 1)

            def outputs_out(l, g):
                dve.wait_ge(y_upper[l], g)
                y_v = y_blk.rearrange("p (a b) -> p a b", b=512)
                nc.vector.tensor_tensor(y_v, PS[0:CAP, 4:6, :], y_v, ALU.add).then_inc(y_ready[l], 1)

            def expert(l, e):
                n, g0 = blocks_of(dve, e)
                with dve.Fori(0, n) as i:
                    g = g0 + i
                    dve.wait_ge(h1_upper[l], g)
                    nc.vector.tensor_tensor(hs, PS[0:CAP, 1, :], hs, ALU.add).then_inc(h1_summed[l], 1)
                    dve.wait_ge(h3_upper[l], g)
                    nc.vector.tensor_tensor(h3, PS[0:CAP, 2, :], h3, ALU.add).then_inc(h3_summed[l], 1)
                    dve.wait_ge(h3_summed[l], g)
                    dve.wait_ge(silu_ready[l], g)
                    nc.vector.scalar_tensor_tensor(out=h3, in0=h3, scalar=H_SCALE / (X_SCALE * W_SCALE), in1=hs,
                                                   op0=ALU.mult, op1=ALU.mult).then_inc(h_ready_e[l], 1)
                    outputs_out(l, g)
                    dve.wait_ge(h_high[l], g)
                    nc.vector.tensor_tensor(h_parts[:, 1, :], h3, h_parts[:, 0, :], ALU.subtract).then_inc(h_low[l], 1)

            nc.vector.memset(zrow[:], 0.0).then_inc(zero_set, 1)
            dve.wait_ge(const_in, 32)
            for part, src in ((ident16, ident), (earlier16, earlier), (ones16, ones)):
                ins = nc.vector.tensor_copy(part, src)
            ins.then_inc(const16_set, 1)
            for l in range(DEPTH):
                if l == 1:
                    wait_x_all(dve, 0)
                    for i in range(4):
                        nc.vector.memset(pre[:, i, 0:2], 0.0)
                        ins = nc.vector.memset(pre[:, i, T + 2:T + 4], 0.0)
                    ins.then_inc(pads_zero, 1)
                    nc.vector.memset(v_ml[:, :, :, ML_DH:VW], 1.0)
                    nc.vector.memset(g_in, 0.0).then_inc(gates_set, 1)
                    nc.vector.memset(g_fo, 0.0).then_inc(gates_set, 1)
                for k in range(1, KT, 2):
                    drain(l, ("xT", k), XT[:, k, :])
                if l == 0:
                    for k2 in (1, 3):
                        drain(0, ("memT", k2), memT[:, 2 * k2:2 * k2 + 2, :].rearrange("p a b -> p (a b)"))
                    drain(0, ("memv", 0), memv[:].rearrange("p a b -> p (a b)"))
                    for kind, c, _, _ in chunks[0]:
                        name = (kind, c, 1)
                        wait_full(dve, 0, name)
                        bank = bank_of(0, name)
                        if kind == "v":
                            ins = nc.vector.tensor_copy(v_nat[:, 2:4, 256 * c:256 * c + 256],
                                                        bank.rearrange("p (t f) -> p t f", t=2))
                        elif kind == "q":
                            ins = nc.vector.tensor_copy(
                                qT[:, 2 * c + 1, :].rearrange("p (b r c) -> p b r c", r=ROWS, c=QC),
                                bank.rearrange("p (r b c) -> p b r c", b=NBLK, c=QC)[:, :, ::-1, ::-1])
                        elif kind == "k":
                            ins = nc.vector.tensor_copy(kT[:, 2 * c + 1, :], bank)
                        else:
                            ins = nc.vector.tensor_copy(qm0[:, 1, :], bank)
                        ins.then_inc(dve_drained[0], 1)
                else:
                    dve.wait_ge(mlp_in, 16 * 8)
                    for m in range(12):
                        convolve(m)
                    gate_rows()
                    forget_rows()
                attention(l)
                if l == 1:
                    mlstm()
                for c in range(4):
                    for s in range(2):
                        name = ("out", c, s)
                        wait_full(dve, l, name)
                        part = X[:, 2 * s:2 * s + 2, 256 * c:256 * c + 256]
                        nc.vector.scalar_tensor_tensor(out=part, in0=part, scalar=ALPHA,
                                                       in1=bank_of(l, name).rearrange("p (t f) -> p t f", t=2),
                                                       op0=ALU.mult, op1=ALU.add).then_inc(dve_drained[l], 1)
                        wait_drained(dve, l, name)
                        for t in (2 * s, 2 * s + 1):
                            ins = nc.vector.bn_stats(ln_st[:, t, c, :], X[:, t, 256 * c:256 * c + 256])
                        if 2 * c + s < len(EARLY):
                            e, piece = EARLY[2 * c + s]
                            low_part(l, e, piece, e)
                link(ins)
                norm1(l)

                def x_low_part(t):
                    dve.wait_ge(x_high, TT * l + t + 1)
                    xp = x_parts(t)
                    nc.vector.scalar_tensor_tensor(out=xp[:, 1], in0=by_tile(X[:, t, :]), scalar=X_SCALE, in1=xp[:, 0],
                                                   op0=ALU.mult, op1=ALU.subtract).then_inc(x_low, 1)

                x_low_part(0)
                for k in range(1, KT, 2):
                    drain(l, ("x1T", k), XT[:, k, :])
                for t in range(1, TT):
                    x_low_part(t)
                dve.wait_ge(route_in, 64 * l + 64)
                wait_full(dve, l, ("logitsT", 0))
                nc.vector.tensor_copy(logitsT, bank_of(l, ("logitsT", 0))[0:NG + NE, :]).then_inc(dve_drained[l], 1)
                routing(l)
                dve.wait_ge(x_stored, 16 * (l + 1))
                low_part(l, 1, 2, 1)
                dve.sem_inc(y_full[l], 1)
                with dve.Fori(0, NE - 2, 2) as e:
                    for q in range(2):
                        expert(l, e + q)
                        for piece in range(3):
                            low_part(l, e + q + 2, piece, q)
                expert(l, NE - 2)
                expert(l, NE - 1)
                end = blocks_end(dve)
                outputs_out(l, end)
                combine_and_norm2(l)

        @block.gpsimd
        def _(pool):
            steps_done = [0]
            pool.wait_ge(zero_set, 1)
            pool.dma_start(rpb_pad[0:RPB_PAD].rearrange("(a n) -> a n", a=1), zrow[:]).then_inc(pads_in, 16)
            pool.dma_start(rpb_pad[RPB_PAD + NA_HEADS * RPB_HEAD:].rearrange("(a n) -> a n", a=1), zrow[:])\
                .then_inc(pads_in, 16)
            pool.dma_start(rpb_pad[RPB_PAD:RPB_PAD + NA_HEADS * RPB_HEAD].rearrange("(h n) -> h n", h=NA_HEADS),
                           na_rpb[0].rearrange("h r c -> h (r c)")).then_inc(pads_in, 16)
            nc.gpsimd.memset(zeros, 0.0).then_inc(zeros_set, 1)
            pool.wait_ge(zeros_set, 1)
            pool.dma_start(slot_token.rearrange("(b s) o -> b (s o)", s=CAP), zeros[0:MAX_BLOCKS + 2, 0:CAP].bitcast(I32))\
                .then_inc(slots_zeroed, 16)
            for r in range((NE + 1) * CAP, (MAX_BLOCKS + 1) * CAP, P):
                pool.dma_start(y_rows[r:r + P, :], zeros).then_inc(y_zeroed, 16)
            pool.wait_ge(y_zeroed, 16 * ((MAX_BLOCKS - NE) * CAP // P))
            pool.wait_ge(slots_zeroed, 16)
            pool.wait_ge(rpb_in, 16 * ROWS)
            pool.wait_ge(const_in, 32)
            for v, shift in enumerate((SHIFT[0], SHIFT[1], SHIFT[3])):
                for h in range(NA_HEADS):
                    run = rpb_tab[:, h, shift:shift + 1]
                    src = bass.AP(tensor=run.tensor, offset=run.offset, ap=[list(run.ap[0]), [RPB_ROW, ROWS], [1, KC]])
                    ins = nc.gpsimd.tensor_tensor(bias_tab[:, v, h, :].rearrange("p (r c) -> p r c", c=KC), src,
                                                  na_mask[:, v:v + 1, :].to_broadcast([P, ROWS, KC]), ALU.add)
                ins.then_inc(bias_built, 1)

            for l in range(DEPTH):
                if l == 1:
                    wait_drained(pool, 1, ("o", 2, 1))
                    pool.wait_ge(mlp_in, 16 * 8)
                    nc.gpsimd.tensor_tensor(o_gate, o_gate, norm_g.unsqueeze(1).to_broadcast([P, TT, TOKEN_W]),
                                            ALU.mult).then_inc(o_scaled, 1)
                def scale_and_shift(t, params, ready):
                    steps_done[0] += 1
                    nc.gpsimd.tensor_tensor(X[:, t, :], X[:, t, :], params[:, 0, :], ALU.mult).then_inc(pool_step, 1)
                    pool.wait_ge(pool_step, steps_done[0])
                    nc.gpsimd.tensor_tensor(X[:, t, :], X[:, t, :], params[:, 1, :], ALU.add).then_inc(ready, 1)

                pool.wait_ge(ln_in, 32 * (l + 1))
                for n, t in enumerate(NORM1_SHARED):
                    pool.wait_ge(normed, len(NORM1_SHARED) * l + n + 1)
                    scale_and_shift(t, ln1_params(l), x1_pool)
                pool.wait_ge(x_low, TT * (l + 1))
                pool.dma_start(x_rows.rearrange("(t p) d -> p t d", p=P),
                               parts[1][2].rearrange("p a (b n) -> p (a b) n", b=2)).then_inc(x_stored, 16)
                pool.wait_ge(dest_ready, l + 1)
                for t in range(TT):
                    for k in range(2):
                        pool.indirect_dma_start(out=slot_token, out_offset=bass.IndirectOffsetOnAxis(
                            ap=dest[:, t, k:k + 1].bitcast(U32), axis=0), in_=ctok[:, t:t + 1], in_offset=None)\
                            .then_inc(slots_set, 16)
                pool.wait_ge(slots_set, 32 * TT * (l + 1))
                pool.dma_start(slot_tab[:], slot_token.rearrange("(b s) o -> s (b o)", s=CAP)).then_inc(slots_in, 16)
                pool.wait_ge(slots_in, 16 * l + 16)
                pool.wait_ge(x_stored, 16 * (l + 1))
                pool.wait_ge(blocks_ready, l + 1)
                end = blocks_end(pool)

                def gather(g, first):
                    if not first:
                        pool.wait_ge(xgT_full[l], g - 1)
                    nc.gpsimd.tensor_copy(idx_now[:], slot_tab[:, bass.ds(g, 1)]).then_inc(idx_set[l], 1)
                    this = g if isinstance(g, int) else pool.to_reg(g)
                    settle(pool)
                    pool.wait_ge(idx_set[l], this)
                    pool.indirect_dma_start(out=xg, out_offset=None, in_=x_rows, in_offset=bass.IndirectOffsetOnAxis(
                        ap=idx_now[:].bitcast(U32), axis=0)).then_inc(x_gathered[l], 16)
                    pool.wait_ge(x_gathered[l], 16 * g)

                gather(1, True)
                with pool.Fori(2, end + 1) as g:
                    gather(g, False)
                stored = pool.to_reg(16 * (end + 1))
                settle(pool)
                pool.wait_ge(y_stored[l], stored)
                for t in range(TT):
                    for k in range(2):
                        pool.indirect_dma_start(out=y_got[:, 2 * t + k, :], out_offset=None,
                                                in_=y_rows[0:(MAX_BLOCKS + 1) * CAP, :],
                                                in_offset=bass.IndirectOffsetOnAxis(
                                                    ap=dest[:, t, k:k + 1].bitcast(U32), axis=0))\
                            .then_inc(y_got_in[t], 16)
                pool.wait_ge(ln2_in, 32 * (l + 1))
                for n, t in enumerate(NORM2_SHARED):
                    pool.wait_ge(normed2, len(NORM2_SHARED) * l + n + 1)
                    scale_and_shift(t, ln2_p, x2_pool)


_INS = ['x', 'mem', 'w_mem_kv', 'na_w_in', 'na_rpb', 'ml_w_in', 'ml_conv_w', 'ml_conv_b', 'ml_gate_b', 'ml_norm_g',
        'w_out', 'ln1_g', 'ln1_b', 'ln2_g', 'ln2_b', 'moe_wg', 'moe_bg', 'moe_we', 'moe_be', 'moe_w1', 'moe_w3',
        'moe_w2']


def kernel(**inputs):
    import numpy as _np
    import concourse.bacc as _bacc
    from concourse import mybir as _mybir
    from concourse.bass_utils import run_bass_kernel_spmd as _run

    nc = _bacc.Bacc("TRN2", target_bir_lowering=False, num_devices=1)
    const_f, const_tok = constants()
    arrays = {f"in_{name}": _np.ascontiguousarray(inputs[name]) for name in _INS}
    arrays["const_f"], arrays["const_tok"] = const_f, const_tok
    args = [nc.dram_tensor(name, a.shape, _mybir.dt.from_np(a.dtype), kind="ExternalInput").ap()
            for name, a in arrays.items()]
    out = nc.dram_tensor("out_0", (1, T, D), F32, kind="ExternalOutput").ap()
    encoder(nc, *args, out)
    r = _run(nc, [arrays], core_ids=[0])
    return r.results[0]["out_0"]
```

```python
from contextlib import ExitStack

import concourse.bass as bass
from concourse import mybir
import numpy as np

F32 = mybir.dt.float32
I32 = mybir.dt.int32
F16 = mybir.dt.float16
U32 = mybir.dt.uint32
ALU = mybir.AluOpType
ACT = mybir.ActivationFunctionType
AX = mybir.AxisListType.X

P = 128
D = 1024
T = 512
TT = T // P
KT = D // P
DEPTH = 2
NMEM = 256
GRID_W = 64
ROWS = T // GRID_W
WIN_H, WIN_W = 8, 16
TOKEN_W = 768
MEM_W = 256
HD = 64
NA_HEADS = 12
ML_HEADS = 4
ML_DH = 192
VW = ML_DH + 1
CONV_K = 5
NG, EPG = 4, 8
NE = NG * EPG
FE = 512
FT = FE // P
CAP = 64
MAX_BLOCKS = NE + (2 * T - 1) // CAP + 1
LN_EPS = 1e-5
ALPHA = (2 * DEPTH) ** 0.25
NEG = -1e30

QC = 16
KC = 32
NBLK = GRID_W // QC
KEY0 = [min(max(QC * b - WIN_W // 2, 0), GRID_W - KC) for b in range(NBLK)]
SHIFT = [KEY0[b] - QC * b + 16 for b in range(NBLK)]
VARIANT = [0, 1, 1, 2]
RPB_ROW = 2 * WIN_W - 1
RPB_HEAD = (2 * WIN_H - 1) * RPB_ROW
RPB_RUN = (ROWS - 1) * RPB_ROW + 48
RPB_PAD = 64

W_SCALE = 256.0
X_SCALE = 16.0
H_SCALE = 8.0
XW_SCALE = X_SCALE * W_SCALE

DVE_COLS = 1024
ACT_RUNS = [[(DVE_COLS, 2048), (2048, 4096)], [(0, 2048), (2048, 4096)], [(0, 2048), (2048, 4096)]]
N_RUNS = sum(len(runs) for runs in ACT_RUNS)

CHUNK = 2176


def constants():
    p = np.arange(P)
    ident = np.eye(P)
    anti = ident[::-1]
    earlier = (p[:, None] < p[None, :]) * 1.0
    ones = np.ones((P, P))
    na = np.zeros((P, 3, KC))
    for b in (0, 1, 3):
        c = QC * b + 15 - p % QC
        start = np.clip(c - WIN_W // 2, 0, GRID_W - WIN_W)[:, None]
        kc = KEY0[b] + np.arange(KC)[None, :]
        na[:, VARIANT[b], :] = np.where((kc >= start) & (kc < start + WIN_W), 0.0, NEG)
    fwd = np.where(p[None, :] >= p[:, None], 0.0, NEG)
    bwd = np.where(p[None, :] <= p[:, None], 0.0, NEG)
    count = np.tile(np.arange(NE), (P, 1)) * 1.0
    f = np.concatenate([ident, anti, earlier, ones, na.reshape(P, -1), fwd, bwd, count], axis=1).astype(np.float32)
    tokens = (np.arange(TT)[None, :] * P + p[:, None]).astype(np.int32)
    return f, tokens


class Jobs:

    def __init__(self, order):
        self.number, self.engine, self.ordinal = {}, {}, {}
        self.by = []
        seen = {"act": 0, "dve": 0}
        for n, (name, engine) in enumerate(order):
            seen[engine] += 1
            self.number[name], self.engine[name], self.ordinal[name] = n, engine, seen[engine]
            self.by.append(name)


def chunk_list(layer):
    if layer == 0:
        return ([("v", c, 2 * TOKEN_W + 256 * c, 256) for c in range(3)]
                + [("q", c, 256 * c, 256) for c in range(3)]
                + [("k", c, TOKEN_W + 256 * c, 256) for c in range(3)] + [("m", 0, 3 * TOKEN_W, 256)])
    return ([("q", c, 256 * c, 256) for c in range(3)] + [("k", c, TOKEN_W + 256 * c, 256) for c in range(3)]
            + [("m", 0, 4 * TOKEN_W, 16 + 256)]
            + [("v", c, 2 * TOKEN_W + 256 * c, 256) for c in range(3)]
            + [("o", c, 3 * TOKEN_W + 256 * c, 256) for c in range(3)])


def job_order(layer):
    order = [(("xT", k), "dve") for k in range(KT)]
    if layer == 0:
        order += [(("memT", k), ("act", "dve")[k % 2]) for k in range(4)]
    for kind, c, _, _ in chunk_list(layer):
        if layer == 1 and kind == "m":
            order.append((("gates", 0), "dve"))
        for s in range(2):
            drain = ("dve" if kind == "v" else ("act", "dve")[s]) if layer == 0 else "act"
            order.append(((kind, c, s), drain))
        if layer == 0 and (kind, c) == ("v", 0):
            order += [(("memk", 0), "act"), (("memv", 0), "dve")]
    if layer == 1:
        order += [(("rows", 0), "dve"), (("rows", 1), "dve"), (("cols", 0), "dve")]
        order += [(("hT", i), "dve") for i in range(6)]
    order += [(("out", c, s), "dve") for c in range(4) for s in range(2)]
    order += [(("x1T", k), ("act", "dve")[k % 2]) for k in range(KT)]
    order += [(("logitsT", 0), "dve"), (("logits", 0), "dve"), (("rank", 0), "dve")]
    return order


def attention_units(layer):
    units = []
    if layer == 0:
        units += [(b, par, i, False) for b in range(NBLK) for par in range(2) for i in range(3)]
    units += [(t, par, 0, True) for t in range(TT) for par in range(2)]
    return units


def encoder(nc, x, mem, w_mem_kv, na_w_in, na_rpb, ml_w_in, ml_conv_w, ml_conv_b, ml_gate_b, ml_norm_g, w_out,
            ln1_g, ln1_b, ln2_g, ln2_b, moe_wg, moe_bg, moe_we, moe_be, moe_w1, moe_w3, moe_w2,
            const_f, const_tok, out):
    ctx = ExitStack()
    with ctx:
        ctx.enter_context(nc.allow_non_contiguous_dma("small parameters"))

        def sb(name, shape, dt=F32):
            return ctx.enter_context(nc.sbuf_tensor(name, shape, dt))

        def sem(name):
            return ctx.enter_context(nc.semaphore(name))

        def sems(name, n=DEPTH):
            return [sem(f"{name}{i}") for i in range(n)]

        def dram(name, shape, dt=F32):
            return nc.dram_tensor(name, shape, dt, kind="Internal").ap()

        rpb_pad = dram("rpb_pad", [RPB_PAD * 2 + NA_HEADS * RPB_HEAD])
        v_rows = dram("v_rows", [T, 2 * TOKEN_W], F16)
        x_rows = dram("x_rows", [T, 2 * D], F16)
        slot_token = dram("slot_token", [(MAX_BLOCKS + 2) * CAP, 1], I32)
        y_rows = dram("y_rows", [(MAX_BLOCKS + 1 + T // CAP) * CAP, D])

        X = sb("X", [P, TT, D])
        XT = sb("XT", [P, KT, T])
        RING = sb("RING", [P, 3 * 12288])
        AREA = sb("AREA", [P, 4864])
        CF = sb("CF", [P, 128 * 4 + 96 + 256 + 32])
        ctok = sb("ctok", [P, TT], I32)
        memk = sb("memk", [P, 2, NMEM])
        memv = sb("memv", [P, 2, 2, MEM_W], F16)
        wr = sb("wr", [P, KT, NG + NE])
        rbias = sb("rbias", [P, NG + NE])
        gates = sb("gates", [P, TT, 2])
        dest = sb("dest", [P, TT, 2], I32)
        blk_i = sb("blk_i", [1, 2 * NE + 1], I32)
        slot_tab = sb("slot_tab", [CAP, MAX_BLOCKS + 2], I32)
        const16 = sb("const16", [P, 3, P], F16)
        ident16, earlier16, ones16 = (const16[:, i, :] for i in range(3))
        idx_now = sb("idx_now", [CAP, 1], I32)
        zrow = sb("zrow", [1, 64])
        small = sb("small", [P, 192])
        PS = ctx.enter_context(nc.psum_tensor("PS", [P, 8, 512], F32))

        ident = CF[:, 0:128]
        anti = CF[:, 128:256]
        earlier = CF[:, 256:384]
        ones = CF[:, 384:512]
        na_mask = CF[:, 512:608].rearrange("p (v k) -> p v k", v=3)
        ml_mask = CF[:, 608:864].rearrange("p (d k) -> p d k", d=2)
        count = CF[:, 864:896]

        def ring(off, *dims):
            n = int(np.prod(dims))
            assert off + n <= 3 * 12288
            v = RING[:, off:off + n]
            if len(dims) == 2:
                v = v.rearrange("p (a b) -> p a b", b=dims[1])
            elif len(dims) == 3:
                v = v.rearrange("p (a b c) -> p a b c", b=dims[1], c=dims[2])
            return v

        qT = ring(0, 6, T)
        kT = ring(3072, 6, T)
        v_win = ring(6144, 2 * NBLK * TOKEN_W).bitcast(F16).rearrange("p (b a f) -> p b a f", b=2 * NBLK, a=2)
        bias_tab = ring(12288, 3, NA_HEADS, ROWS * KC)
        rpb_tab = ring(21504, NA_HEADS, RPB_RUN)
        v_nat = ring(24704, TT * TOKEN_W).bitcast(F16).rearrange("p (t a f) -> p t a f", t=TT, a=2)
        o_na = ring(27776, NBLK, TOKEN_W)
        o_mem0 = ring(30848, TT, MEM_W)
        qm0 = ring(31872, 2, T)
        sneg = ring(32896, 3, 512)
        prob0 = ring(34432, 3, 512)
        probT0 = ring(24704, 2, 512)
        memT = ring(13312, KT, NMEM)
        w_kv = ring(6144, KT, 2 * MEM_W)
        zeros = ring(12288, D)
        mem_in = ring(30848, 2, D)
        qk = ring(0, 12, T)
        pre = ring(6144, 4, T + 4)
        v_ml = ring(8208, TT, ML_HEADS, VW)
        o_gate = ring(11296, TT, TOKEN_W)
        H = ring(14368, TT, TOKEN_W)
        W = ring(17440, 2, TT, T)
        E = ring(21536, 2, TT, T)
        qm1 = ring(25632, 2, T)
        Rd = ring(26656, 2, 512)
        r_F = ring(27680, T)
        r_a = ring(28192, T)
        r_M = ring(28704, T)
        r_m = ring(29216, T)
        prob1 = ring(29728, 3, 512)
        probT1 = ring(31264, 2, 512)
        o_mem1 = ring(32288, TT, MEM_W)
        norm_g = ring(33312, TOKEN_W)
        conv_w = ring(34080, 12, CONV_K)
        conv_b = ring(34140, 12)
        g_in = ring(34160, TT, 64)
        g_fo = ring(34416, TT, 64)
        g_tok = ring(34672, TT, 16)
        g_abs = ring(34736, TT, 8)
        g_ln = ring(34768, TT, 8)
        g_bias = ring(34800, 16)
        ml_st = ring(34816, 16, 6)
        ml_mv = ring(34912, 16, 2)
        ml_rstd = ring(34944, 16)
        ml_nm = ring(35120, 16)
        acol = ring(34960, TT, 8)
        mcol = ring(34992, TT, 8)
        em = ring(35024, TT, 8)
        den = ring(35056, 16, 2)
        rden = ring(35088, 16, 2)
        qm, prob, o_mem = [qm0, qm1], [prob0, prob1], [o_mem0, o_mem1]
        probT = [v.rearrange("p b n -> p (b n)").bitcast(F16).rearrange("p (b a n) -> p b a n", b=2, a=2)
                 for v in (probT0, probT1)]
        XT16 = XT[:].rearrange("p k t -> p (k t)").bitcast(F16).rearrange("p (a k t) -> p a k t", a=2, k=KT)

        staged = [RING[:, 24576 + 4096 * i:24576 + 4096 * (i + 1)] for i in range(3)]
        parts = [[RING[:, 4096 * (3 * q + i):4096 * (3 * q + i + 1)].bitcast(F16).rearrange("p (a n) -> p a n", a=2)
                  for i in range(3)] for q in range(2)]
        y_got = ring(24576, 2 * TT, D)
        ln2_p = ring(24576 + 8192, 2, D)

        chunk_buf = [AREA[:, CHUNK * i:CHUNK * (i + 1)] for i in range(2)]
        xg = AREA[0:CAP, 0:1024].bitcast(F16)
        xgT = AREA[:, 1024:1536].bitcast(F16).rearrange("p (k s) -> p k s", s=P)
        hs = AREA[0:CAP, 1536:2048]
        h3 = AREA[0:CAP, 2048:2560]
        h_parts = AREA[0:CAP, 2560:3072].bitcast(F16).rearrange("p (a f) -> p a f", a=2)
        hT = AREA[:, 3072:3328].bitcast(F16).rearrange("p (k s) -> p k s", s=P)
        y_blk = AREA[0:CAP, 3328:4352]
        logitsT = AREA[0:NG + NE, 4352:4864]

        def chunk_parts(l, n):
            width = chunks[l][n][3] if n < n_proj[l] else 256
            if n < n_proj[l]:
                at = (27776, 17440)[l] + (2048, CHUNK)[l] * (n % 2)
            else:
                at = ((22528, 6144)[l], 20480, 22528, 20480)[n - n_proj[l]]
            return RING[:, at:at + KT * width].bitcast(F16).rearrange("p (a k f) -> p a k f", a=2, k=KT)

        def chunk_staged(l, n):
            width = chunks[l][n][3] if n < n_proj[l] else 256
            return chunk_buf[n % 2][:, 0:KT * width].rearrange("p (k f) -> p k f", f=width)

        def chunk_number(l, n):
            return n + 1 + (n_proj[0] + 4 if l else 0)

        msum = sb("msum", [P, 40, 2])
        mneg = sb("mneg", [P, 40, 2])
        mraw = sb("mraw", [P, 8, 2])
        rsum = small[:, 0:16].rearrange("p (a b) -> p a b", b=8)
        ln_st = small[:, 16:112].rearrange("p (t a s) -> p t a s", t=TT, a=4)
        ln_mv = small[:, 112:120].rearrange("p (t s) -> p t s", s=2)
        ln_ve = small[:, 120:124]
        ln_sd = small[:, 124:128]
        ln_rs = small[:, 128:132]
        ln_nm = small[:, 132:136]
        warm = small[0:1, 136:137]

        const_in, x_in, mem_in_s, kv_in = sem("const_in"), sems("x_in", TT), sem("mem_in_s"), sem("kv_in")
        zero_set, pads_in, rpb_in, mlp_in = sem("zero_set"), sem("pads_in"), sem("rpb_in"), sem("mlp_in")
        zeros_stored = sem("zeros_stored")
        v_out, v_in, bias_built = sem("v_out"), sem("v_in"), sem("bias_built")
        chunk_high, chunk_low, t_high = sem("chunk_high"), sem("chunk_low"), sem("t_high")
        chunk_in = [sems(f"chunk_in_l{l}_", 2) for l in range(DEPTH)]
        ln_in, ln2_in, route_in = sem("ln_in"), sem("ln2_in"), sem("route_in")
        bank_full = sems("bank_full")
        act_drained, dve_drained = sems("act_drained"), sems("dve_drained")
        scores_full, max_ready, probs_ready = sems("scores_full"), sems("max_ready"), sems("probs_ready")
        probsT_high, v_high = sem("probsT_high"), sem("v_high")
        probsT_full, probsT_ready, values_summed = sems("probsT_full"), sems("probsT_ready"), sems("values_summed")
        heads_ready, mix_full, mix_ready = sems("heads_ready"), sems("mix_full"), sems("mix_ready")
        dve_step, pool_step = sem("dve_step"), sem("pool_step")
        pads_zero = sem("pads_zero")
        conv_done, silu_done, o_scaled = sem("conv_done"), sem("silu_done"), sem("o_scaled")
        lf_abs, lf_ln, gates_set = sem("lf_abs"), sem("lf_ln"), sem("gates_set")
        rows_set, mcol_set, em_set = sem("rows_set"), sem("mcol_set"), sem("em_set")
        r_full, r_masked, e_ready = sem("r_full"), sem("r_masked"), sem("e_ready")
        s_full, w_ready, num_full, h_added = sem("s_full"), sem("w_ready"), sem("num_full"), sem("h_added")
        ml_var, ml_sd, h_ready = sem("ml_var"), sem("ml_sd"), sem("h_ready")
        ml_moments, h_normed = sem("ml_moments"), sem("h_normed")
        var_ready, sd_ready, x1_dve, x1_pool = sem("var_ready"), sem("sd_ready"), sem("x1_dve"), sem("x1_pool")
        moments, normed, x_alpha = sem("moments"), sem("normed"), sem("x_alpha")
        var2_ready, sd2_ready, x2_dve, x2_pool = sem("var2_ready"), sem("sd2_ready"), sem("x2_dve"), sem("x2_pool")
        moments2, normed2 = sem("moments2"), sem("normed2")
        gdiff, gexp, ediff, eexp = sem("gdiff"), sem("gexp"), sem("ediff"), sem("eexp")
        picks_ready, blocks_ready, dest_ready = sem("picks_ready"), sem("blocks_ready"), sem("dest_ready")
        x_stored, slots_set, slots_in = sem("x_stored"), sem("slots_set"), sem("slots_in")
        idx_set, x_gathered = sems("idx_set"), sems("x_gathered")
        xgT_full, xgT_ready = sems("xgT_full"), sems("xgT_ready")
        h1_full, h3_full, h1_summed, h3_summed = sems("h1_full"), sems("h3_full"), sems("h1_summed"), sems("h3_summed")
        silu_ready, h_ready_e, h_high, h_low = sems("silu_ready"), sems("h_ready_e"), sems("h_high"), sems("h_low")
        hT_full, hT_ready = sems("hT_full"), sems("hT_ready")
        h1_upper, h3_upper, y_upper = sems("h1_upper"), sems("h3_upper"), sems("y_upper")
        w_high, w_low, x_high, x_low = sems("w_high"), sems("w_low"), sem("x_high"), sem("x_low")
        const16_set, w_first = sem("const16_set"), sem("w_first")
        y_full, y_ready, y_stored = sems("y_full"), sems("y_ready"), sems("y_stored")
        w_in = [sems(f"w_in_l{l}_", 3) for l in range(DEPTH)]
        y_got_in = sems("y_got_in", TT)
        out_done = sem("out_done")

        jobs = [Jobs(job_order(l)) for l in range(DEPTH)]
        units = [attention_units(l) for l in range(DEPTH)]
        chunks = [chunk_list(l) for l in range(DEPTH)]
        n_proj = [len(c) for c in chunks]

        def bank_of(l, name):
            return PS[:, jobs[l].number[name] % 8, :]

        def wait_drained(eng, l, name):
            s = act_drained if jobs[l].engine[name] == "act" else dve_drained
            eng.wait_ge(s[l], jobs[l].ordinal[name])

        def wait_full(eng, l, name):
            eng.wait_ge(bank_full[l], jobs[l].number[name] + 1)

        NORM1_SHARED, NORM2_SHARED = (3,), (0, 1)
        NORM2_ACT = (("root", 0), ("root", 1), ("norm", 0), ("root", 2), ("norm", 1), ("root", 3))
        EARLY = [(0, 0), (0, 1), (0, 2), (1, 0), (1, 1)]

        def wait_x(eng, l, t, after_experts=False):
            shared, by_pool, by_dve = ((NORM2_SHARED, x2_pool, x2_dve) if after_experts
                                       else (NORM1_SHARED, x1_pool, x1_dve))
            mine = t in shared
            per_layer = len(shared) if mine else TT - len(shared)
            eng.wait_ge(by_pool if mine else by_dve,
                        per_layer * l + sum((u in shared) == mine for u in range(t + 1)))

        def wait_x_all(eng, l):
            for t in (NORM2_SHARED[-1], TT - 1):
                wait_x(eng, l, t, True)

        def wait_chunk_place(eng, l, n):
            c = n - n_proj[l]
            if l == 0 and n == 1:
                wait_full(eng, 0, ("memT", 3))
            if c == 0:
                if l == 0:
                    eng.wait_ge(bias_built, 3)
                else:
                    eng.wait_ge(conv_done, 12)
            elif c == 1:
                if l == 0:
                    eng.wait_ge(mix_ready[0], last_mix_round(0, len(block_kinds(0)) - 1))
                else:
                    eng.wait_ge(num_full, 16)
            elif c >= 2:
                wait_full(eng, l, ("out", c - 2, 1))
            elif n >= 2:
                kind, i = chunks[l][n - 2][:2]
                wait_full(eng, l, (kind, i, 1))

        def last_mix_round(l, blk_index):
            return sum(1 if m else 2 for m in block_kinds(l)[:blk_index + 1])

        def block_kinds(l):
            return ([False] * NBLK if l == 0 else []) + [True] * TT

        def block_no(l, unit):
            b, _, _, is_mem = unit
            return b + (NBLK if l == 0 and is_mem else 0)

        def steps(l):
            us = units[l]
            for i in range(len(us) + 7):
                at = lambda lag: us[i - lag] if 0 <= i - lag < len(us) else None
                yield i, at

        def mix_rounds(at):
            for lag in (6, 5):
                u = at(lag)
                if ends_group(u) and u[1] == 1 and (lag == 5 or not u[3]):
                    yield u, lag - 5

        def ends_group(u):
            return u is not None and (u[3] or u[2] == 2)

        def group_no(l, u):
            return 2 * block_no(l, u) + u[1]

        def blocks_of(eng, e):
            n = eng.value_load(blk_i[0:1, bass.ds(e, 1)], min_val=1, max_val=T // CAP)
            g0 = eng.value_load(blk_i[0:1, bass.ds(e + NE, 1)], min_val=1, max_val=MAX_BLOCKS)
            return n, g0

        def blocks_end(eng):
            return eng.value_load(blk_i[0:1, 2 * NE:2 * NE + 1], min_val=NE + 1, max_val=MAX_BLOCKS + 1)

        def x_parts(t):
            return parts[1][2].rearrange("p a (b n) -> p (a b n)", b=2)[:, 2 * D * t:2 * D * (t + 1)]\
                .rearrange("p (a k f) -> p a k f", a=2, k=KT)

        def by_tile(row):
            return row.rearrange("p (f k) -> p k f", k=KT)

        def routing_views(l):
            base = chunk_buf[(n_proj[l] + 3) % 2]
            views, at = {}, 0
            for name, dims in (("lg", (TT, 36)), ("gp", (TT, 8)), ("gm", (TT, 8)), ("gi", (TT, 8)), ("gd", (TT, 4)),
                               ("ge", (TT, 4)), ("z", (TT, 1)), ("gif", (TT, 1)), ("oh", (TT, 4)),
                               ("prod", (TT, NG, EPG)), ("es", (TT, 8)), ("e8", (TT, 8)), ("ei", (TT, 8)),
                               ("ed", (TT, 1)), ("e2", (TT, 1)), ("dn", (TT, 1)), ("eif", (TT, 2)), ("eid", (TT, 2)),
                               ("pick", (TT, 2, NE)), ("picks", (TT, NE)), ("ci", (NE,)), ("cs", (NE,)),
                               ("nb", (NE,)), ("inc", (NE,)), ("ex", (NE,)), ("slot", (TT, NE)), ("ps", (TT, 2, NE)),
                               ("df", (TT, 2))):
                n = int(np.prod(dims))
                v = base[:, at:at + n]
                if name in ("gi", "ei"):
                    v = v.bitcast(U32)
                if name == "picks":
                    v = v.bitcast(F16)[:, 0:n]
                if name in ("ci", "cs"):
                    v = v.bitcast(I32)
                if len(dims) == 2:
                    v = v.rearrange("p (a b) -> p a b", b=dims[1])
                elif len(dims) == 3:
                    v = v.rearrange("p (a b c) -> p a b c", b=dims[1], c=dims[2])
                views[name] = v
                at += n
            assert at <= CHUNK
            return views

        def ln1_params(l):
            return chunk_buf[(n_proj[l] + 2) % 2][:, 0:2 * D].rearrange("p (a d) -> p a d", d=D)

        def settle(eng):
            eng.wait_ge(const_in, 32)

        block = ctx.enter_context(nc.Block())

        @block.tensor
        def _(pe):
            def begin(l, name):
                n = jobs[l].number[name]
                if n >= 8:
                    wait_drained(pe, l, jobs[l].by[n - 8])
                return bank_of(l, name)

            def keep_busy(n, out=PS[:, 6, :]):
                for _ in range(n):
                    nc.tensor.matmul(out, ident, CF[:, 0:out.shape[-1]], start=True, stop=True)

            def transposed_x(l, kind):
                for t in range(TT):
                    if kind == "x1T" and t == 0:
                        begin(l, (kind, 0))
                        keep_busy(7, bank_of(l, (kind, 0)))
                    elif kind == "x1T" or l > 0:
                        keep_busy(3, bank_of(l, (kind, 0))[:, t * P:])
                    if l == 0 and kind == "xT":
                        pe.wait_ge(x_in[t], 16)
                    else:
                        wait_x(pe, l if kind == "x1T" else l - 1, t, kind == "xT")
                    for k in range(KT):
                        bank = begin(l, (kind, k)) if t == 0 else bank_of(l, (kind, k))
                        mm = nc.tensor.transpose(bank[:, t * P:(t + 1) * P], X[:, t, k * P:(k + 1) * P], ident)
                        if t == TT - 1:
                            mm.then_inc(bank_full[l], 1)

            def turn_memory():
                pe.wait_ge(mem_in_s, 16)
                for k2 in range(4):
                    bank = begin(0, ("memT", k2))
                    for kk in range(2):
                        for m in range(2):
                            k = 2 * k2 + kk
                            mm = nc.tensor.transpose(bank[:, kk * NMEM + m * P:kk * NMEM + (m + 1) * P],
                                                     mem_in[:, m, k * P:(k + 1) * P], ident)
                    mm.then_inc(bank_full[0], 1)

            def memory_products():
                pe.wait_ge(kv_in, 16)
                wait_drained(pe, 0, ("memT", 2))
                wait_drained(pe, 0, ("memT", 3))
                bank = begin(0, ("memk", 0))
                for i in range(2):
                    for k in range(KT):
                        mm = nc.tensor.matmul(bank[:, i * NMEM:(i + 1) * NMEM], w_kv[:, k, i * P:(i + 1) * P],
                                              memT[:, k, :], start=(k == 0), stop=(k == KT - 1))
                mm.then_inc(bank_full[0], 1)
                bank = begin(0, ("memv", 0))
                for m in range(2):
                    for k in range(KT):
                        mm = nc.tensor.matmul(bank[:, m * MEM_W:(m + 1) * MEM_W], memT[:, k, m * P:(m + 1) * P],
                                              w_kv[:, k, MEM_W:2 * MEM_W], start=(k == 0), stop=(k == KT - 1))
                mm.then_inc(bank_full[0], 1)

            def products(out, x, w, before=None):
                for k in range(KT):
                    if before:
                        before(k)
                    for n, (a, b) in enumerate(((0, 0), (0, 1), (1, 0))):
                        mm = nc.tensor.matmul(out, x[:, a, k, :], w[:, b, k, :], start=(k == 0 and n == 0),
                                              stop=(k == KT - 1 and n == 2))
                return mm

            def projection(l):
                for c, (kind, i, _, width) in enumerate(chunks[l]):
                    pe.wait_ge(chunk_low, chunk_number(l, c))
                    w = chunk_parts(l, c)
                    first = width - 256
                    if first:
                        bank = begin(l, ("gates", 0))
                        for t in range(TT):
                            mm = products(bank[:, 16 * t:16 * t + 16], XT16[:, :, :, t * P:(t + 1) * P], w[:, :, :, 0:16])
                        mm.then_inc(bank_full[l], 1)
                    for s in range(2):
                        bank = begin(l, (kind, i, s))
                        x_there = (lambda k: wait_drained(pe, l, ("xT", k))) if (c, s) == (0, 0) else None
                        if kind in "qkm":
                            mm = products(bank, w[:, :, :, first + s * P:first + (s + 1) * P], XT16, x_there)
                        else:
                            for j in range(2):
                                t = 2 * s + j
                                mm = products(bank[:, 256 * j:256 * j + 256], XT16[:, :, :, t * P:(t + 1) * P], w,
                                              x_there if j == 0 else None)
                        mm.then_inc(bank_full[l], 1)
                    if l == 0 and c == 0:
                        memory_products()

            def attention(l):
                def scores(n, u):
                    b, par, i, is_mem = u
                    lo = HD * par
                    if n >= 3:
                        pe.wait_ge(probs_ready[l], 2 * (n - 2))
                    bank = PS[:, (0, 1, 7)[n % 3], :]
                    if l == 0 and n == 0:
                        wait_drained(pe, 0, ("k", 2, 0)), wait_drained(pe, 0, ("k", 2, 1))
                    if is_mem:
                        wait_drained(pe, l, ("m", 0, 0)), wait_drained(pe, l, ("m", 0, 1))
                    for j in range(2):
                        if is_mem:
                            mm = nc.tensor.matmul(bank[:, 256 * j:256 * j + 256],
                                                  qm[l][lo:lo + HD, j, b * P:(b + 1) * P],
                                                  memk[lo:lo + HD, j, :], start=True, stop=True)
                        else:
                            tile = 2 * i + j
                            keys = kT[lo:lo + HD, tile, :].rearrange("p (r c) -> p r c", c=GRID_W)
                            mm = nc.tensor.matmul(bank[:, 256 * j:256 * j + 256],
                                                  qT[lo:lo + HD, tile, b * P:(b + 1) * P],
                                                  keys[:, :, KEY0[b]:KEY0[b] + KC], start=True, stop=True)
                    mm.then_inc(scores_full[l], 1)

                def turn(n, u):
                    pe.wait_ge(probs_ready[l], 2 * (n + 1))
                    if n >= 2:
                        pe.wait_ge(probsT_ready[l], n - 1)
                    for j in range(4):
                        mm = nc.tensor.transpose(PS[:, 2 + n % 2, j * P:(j + 1) * P],
                                                 prob[l][:, n % 3, j * P:(j + 1) * P], ident)
                    mm.then_inc(probsT_full[l], 1)

                def values(n, u):
                    b, par, i, is_mem = u
                    pe.wait_ge(probsT_ready[l], n + 1)
                    if (is_mem or i == 0) and group_no(l, u) >= 2:
                        pe.wait_ge(heads_ready[l], group_no(l, u) - 1)
                    if l == 0 and n == 0:
                        pe.wait_ge(v_in, 16 * 2 * NBLK)
                    for j in range(2):
                        dst = PS[:, 4 + par, (2 * i + j) * HD:(2 * i + j + 1) * HD]
                        h = 2 * (2 * i + j) + par
                        for kt in range(2):
                            for x, (a, b_) in enumerate(((0, 0), (0, 1), (1, 0))):
                                vals = (memv[:, b_, kt, h * HD:(h + 1) * HD] if is_mem
                                        else v_win[:, 2 * b + kt, b_, h * HD:(h + 1) * HD])
                                mm = nc.tensor.matmul(
                                    dst, probT[l][:, n % 2, a, (2 * j + kt) * P:(2 * j + kt + 1) * P], vals,
                                    start=(kt == 0 and x == 0), stop=(kt == 1 and x == 2))
                    mm.then_inc(values_summed[l], 1)

                def mix(u, r):
                    b, par, _, is_mem = u
                    pe.wait_ge(heads_ready[l], group_no(l, u) + 1)
                    done = last_mix_round(l, block_no(l, u) - 1) if block_no(l, u) else 0
                    if done + r:
                        pe.wait_ge(mix_ready[l], done + r)
                    for i in range(2 if is_mem else 3):
                        f = (3 * r + i) * P
                        src = o_mem[l][:, b, f:f + P] if is_mem else o_na[:, b, f:f + P]
                        mm = nc.tensor.matmul(PS[:, 6, i * P:(i + 1) * P], src, ident if is_mem else anti,
                                              start=True, stop=True)
                    mm.then_inc(mix_full[l], 1)

                for s, at in steps(l):
                    if at(0):
                        scores(s, at(0))
                    if s in (1, 2):
                        keep_busy(2)
                    if at(2):
                        turn(s - 2, at(2))
                    if at(3):
                        values(s - 3, at(3))
                    for u, r in mix_rounds(at):
                        mix(u, r)

            def mlstm():
                j = jobs[1]
                for r, src in enumerate((g_in, g_fo)):
                    if r == 0:
                        pe.wait_ge(gates_set, 3)
                    bank = begin(1, ("rows", r))
                    for t in range(TT):
                        mm = nc.tensor.transpose(bank[0:64, t * P:(t + 1) * P], src[:, t, :], ident)
                    mm.then_inc(bank_full[1], 1)
                pe.wait_ge(rows_set, 1)
                bank = begin(1, ("cols", 0))
                for g, src in enumerate((r_a, r_m)):
                    for t in range(TT):
                        mm = nc.tensor.transpose(bank[:, g * 256 + t * 64:g * 256 + (t + 1) * 64],
                                                 src[0:64, t * P:(t + 1) * P], ident[0:64, 0:64])
                mm.then_inc(bank_full[1], 1)
                wait_drained(pe, 1, ("cols", 0))
                pe.wait_ge(silu_done, 12)
                parts = [[(0, 0, 128), (1, 0, 64)], [(1, 64, 128), (2, 0, 128)],
                         [(3, 0, 128), (4, 0, 64)], [(4, 64, 128), (5, 0, 128)]]
                for h in range(ML_HEADS + 1):
                    if h < ML_HEADS:
                        for d in range(2):
                            n = 2 * h + d
                            if n >= 2:
                                pe.wait_ge(e_ready, n - 1)
                            row = 32 * d + h
                            nc.tensor.matmul(PS[:, (0, 7)[d], :], ident[0:64, row:row + 1].to_broadcast([64, P]),
                                             r_M[0:64, :], start=True, stop=True).then_inc(r_full, 1)
                        for i in range(TT):
                            if h:
                                pe.wait_ge(w_ready, TT * (h - 1) + i + 1)
                            for a, (tile, lo, hi) in enumerate(parts[h]):
                                mm = nc.tensor.matmul(PS[:, 1 + i, :], qk[lo:hi, 6 + tile, i * P:(i + 1) * P],
                                                      qk[lo:hi, tile, :], start=(a == 0), stop=(a == 1))
                            mm.then_inc(s_full, 1)
                    if h >= 1:
                        g = h - 1
                        pe.wait_ge(w_ready, TT * (g + 1))
                        for t in range(TT):
                            n = TT * g + t
                            if n >= 2:
                                pe.wait_ge(h_added, n - 1)
                            bank = PS[:, 5 + n % 2, :]
                            for d in range(2):
                                tiles = range(0, t + 1) if d == 0 else range(t, TT)
                                for i in tiles:
                                    mm = nc.tensor.matmul(bank[:, 256 * d:256 * d + VW], W[:, d, i, t * P:(t + 1) * P],
                                                          v_ml[:, i, g, :], start=(i == tiles[0]), stop=(i == tiles[-1]))
                            mm.then_inc(num_full, 1)
                keep_busy(8, PS[:, 1, :])
                for t in range(TT):
                    pe.wait_ge(h_ready, t + 1)
                    for i in range(6):
                        bank = begin(1, ("hT", i)) if t == 0 else bank_of(1, ("hT", i))
                        mm = nc.tensor.transpose(bank[:, t * P:(t + 1) * P], H[:, t, i * P:(i + 1) * P], ident)
                        if t == TT - 1:
                            mm.then_inc(bank_full[1], 1)

            def output_projection(l):
                for c in range(4):
                    pe.wait_ge(chunk_low, chunk_number(l, n_proj[l] + c))
                    w = chunk_parts(l, n_proj[l] + c)
                    for s in range(2):
                        bank = begin(l, ("out", c, s))
                        for j in range(2):
                            t = 2 * s + j
                            there = ((lambda k: wait_drained(pe, 1, ("hT", min(k, 5))))
                                     if l == 1 and (c, s, j) == (0, 0, 0) else None)
                            mm = products(bank[:, 256 * j:256 * j + 256], XT16[:, :, :, t * P:(t + 1) * P], w, there)
                        mm.then_inc(bank_full[l], 1)

            def routing(l, picks):
                pe.wait_ge(route_in, 64 * l + 64)
                bank = begin(l, ("logitsT", 0))
                for k in range(KT):
                    wait_drained(pe, l, ("x1T", k))
                    mm = nc.tensor.matmul(bank[0:NG + NE, :], wr[:, k, :], XT[:, k, :],
                                          start=(k == 0), stop=(k == KT - 1))
                mm.then_inc(bank_full[l], 1)
                wait_drained(pe, l, ("logitsT", 0))
                bank = begin(l, ("logits", 0))
                for t in range(TT):
                    mm = nc.tensor.transpose(bank[:, 36 * t:36 * t + 36], logitsT[:, t * P:(t + 1) * P],
                                             ident[0:NG + NE, 0:NG + NE])
                mm.then_inc(bank_full[l], 1)
                if l == 0:
                    pe.wait_ge(const16_set, 1)
                pe.wait_ge(picks_ready, l + 1)
                bank = begin(l, ("rank", 0))
                for t in range(TT):
                    for t2 in range(t + 1):
                        nc.tensor.matmul(bank[:, NE * t:NE * t + NE], earlier16 if t2 == t else ones16, picks[:, t2, :],
                                         start=(t2 == 0), stop=(t2 == t))
                for t in range(TT):
                    mm = nc.tensor.matmul(bank[:, NE * TT:NE * TT + NE], ones16, picks[:, t, :],
                                          start=(t == 0), stop=(t == TT - 1))
                mm.then_inc(bank_full[l], 1)

            def turn_rows(l, g):
                bank = PS[:, 0, :].bitcast(F16)
                for k in range(KT):
                    for a in range(2):
                        mm = nc.tensor.transpose(bank[:, k * P + a * CAP:k * P + (a + 1) * CAP],
                                                 xg[:, a * D + k * P:a * D + (k + 1) * P], ident16[0:CAP, 0:CAP])
                mm.then_inc(xgT_full[l], 1)

            def expert(l, e, q):
                n, g0 = blocks_of(pe, e)
                split = pe.to_reg(3 * e + 3)
                settle(pe)
                pe.wait_ge(w_low[l], split)
                with pe.Fori(0, n) as i:
                    g = g0 + i
                    now, gathered = pe.to_reg(g), pe.to_reg(16 * (g + 1))
                    settle(pe)
                    pe.wait_ge(xgT_ready[l], now)
                    for bank, piece, full in ((1, 0, h1_full), (2, 1, h3_full)):
                        for k in range(KT):
                            for a in range(2):
                                mm = nc.tensor.matmul(PS[:, bank, :], xgT[:, k, :],
                                                      parts[q][piece][:, a, k * FE:(k + 1) * FE],
                                                      start=(k == 0 and a == 0), stop=(k == KT - 1 and a == 1))
                        mm.then_inc(full[l], 1)
                    settle(pe)
                    pe.wait_ge(x_gathered[l], gathered)
                    turn_rows(l, g + 1)
                    settle(pe)
                    pe.wait_ge(h_low[l], now)
                    bank = PS[:, 3, :].bitcast(F16)
                    for k in range(FT):
                        for a in range(2):
                            mm = nc.tensor.transpose(bank[:, k * P + a * CAP:k * P + (a + 1) * CAP],
                                                     h_parts[:, a, k * P:(k + 1) * P], ident16[0:CAP, 0:CAP])
                    mm.then_inc(hT_full[l], 1)
                    settle(pe)
                    pe.wait_ge(hT_ready[l], now)
                    pe.wait_ge(y_ready[l], now)
                    for c in range(2):
                        for k in range(FT):
                            for a in range(2):
                                mm = nc.tensor.matmul(PS[:, 4 + c, :], hT[:, k, :],
                                                      parts[q][2][:, a, k * D + c * FE:k * D + (c + 1) * FE],
                                                      start=(k == 0 and a == 0), stop=(k == FT - 1 and a == 1))
                    mm.then_inc(y_full[l], 1)

            pe.wait_ge(const_in, 32)
            for l in range(DEPTH):
                transposed_x(l, "xT")
                if l == 0:
                    turn_memory()
                projection(l)
                tail = jobs[l].by[:jobs[l].number[("out", 0, 0) if l == 0 else ("rows", 0)]][-8:]
                for name in sorted(tail, key=lambda name: jobs[l].number[name] % 8 != 6):
                    wait_drained(pe, l, name)
                    if jobs[l].number[name] % 8 == 6:
                        keep_busy(2)
                attention(l)
                pe.wait_ge(mix_ready[l], last_mix_round(l, len(block_kinds(l)) - 1))
                if l == 1:
                    mlstm()
                output_projection(l)
                transposed_x(l, "x1T")
                routing(l, routing_views(l)["picks"])
                pe.wait_ge(blocks_ready, l + 1)
                wait_drained(pe, l, ("rank", 0))
                pe.wait_ge(x_gathered[l], 16)
                turn_rows(l, 1)
                with pe.Fori(0, NE, 2) as e:
                    for q in range(2):
                        expert(l, e + q, q)

        w13_v = [w.rearrange("l e (p k) f -> (l e) p (k f)", k=KT) for w in (moe_w1, moe_w3)]
        w2_v = moe_w2.rearrange("l e (k p) f -> (l e) p k f", p=P)

        @block.sync
        def _(sp):
            def load_chunk(l, n):
                if n >= 2:
                    sp.wait_ge(chunk_low, chunk_number(l, n - 2))
                if n < n_proj[l]:
                    _, _, col, width = chunks[l][n]
                    src = (na_w_in, ml_w_in)[l][0].rearrange("(k p) f -> p k f", p=P)[:, :, col:col + width]
                else:
                    c, width = n - n_proj[l], 256
                    src = w_out[l].rearrange("(k p) f -> p k f", p=P)[:, :, 256 * c:256 * c + 256]
                sp.dma_start(chunk_staged(l, n), src).then_inc(chunk_in[l][n % 2], 16)

            def load_piece(l, e, piece):
                if isinstance(e, int):
                    if e:
                        sp.wait_ge(w_low[l], 3 * (e - 1) + piece + 1)
                else:
                    sp.wait_ge(w_low[l], sp.to_reg(3 * (e - 1) + piece + 1))
                if piece < 2:
                    src = w13_v[piece][bass.ds(l * NE + e, 1)].rearrange("a p n -> (a p) n")
                    sp.dma_start(staged[piece], src).then_inc(w_in[l][piece], 16)
                else:
                    src = w2_v[bass.ds(l * NE + e, 1)].rearrange("a p k f -> (a p) k f")
                    sp.dma_start(staged[2].rearrange("p (k f) -> p k f", k=FT), src).then_inc(w_in[l][2], 16)

            def store_blocks(l, e):
                n, g0 = blocks_of(sp, e)
                with sp.Fori(0, n) as i:
                    g = g0 + i
                    sp.wait_ge(y_ready[l], g)
                    sp.dma_start(y_rows[bass.ds((g - 1) * CAP, CAP), :], y_blk).then_inc(y_stored[l], 16)

            sp.dma_start(CF[:], const_f).then_inc(const_in, 16)
            sp.dma_start(ctok[:], const_tok).then_inc(const_in, 16)
            for t in range(TT):
                sp.dma_start(X[:, t, :], x[0, t * P:(t + 1) * P, :]).then_inc(x_in[t], 16)
            sp.dma_start(mem_in, mem[0].rearrange("(m p) d -> p m d", p=P)).then_inc(mem_in_s, 16)
            load_chunk(0, 0)
            sp.dma_start(w_kv, w_mem_kv.rearrange("(k p) f -> p k f", p=P)).then_inc(kv_in, 16)
            for l in range(DEPTH):
                if l == 1:
                    wait_x_all(sp, 0)
                    sp.dma_start(norm_g, ml_norm_g[0:1, :].partition_broadcast(P)).then_inc(mlp_in, 16)
                    sp.dma_start(g_bias, ml_gate_b.rearrange("a j h -> a (j h)")[0:1, :].partition_broadcast(P))\
                        .then_inc(mlp_in, 16)
                    for j in range(CONV_K):
                        sp.dma_start(conv_w[:, :, j], ml_conv_w[0, j].rearrange("(m p) -> p m", p=P)).then_inc(mlp_in, 16)
                    sp.dma_start(conv_b, ml_conv_b[0].rearrange("(m p) -> p m", p=P)).then_inc(mlp_in, 16)
                for n in range(n_proj[l]):
                    if n >= 2 or l == 0 and n == 1:
                        load_chunk(l, n)
                    if l == 0 and n == 2:
                        sp.wait_ge(pads_in, 48)
                        for r in range(ROWS):
                            src = bass.AP(tensor=rpb_pad.tensor, offset=RPB_PAD - 16 + RPB_ROW * r,
                                          ap=[[1, QC], [RPB_HEAD, NA_HEADS], [1, RPB_RUN]])
                            sp.dma_start(rpb_tab[QC * r:QC * r + QC], src).then_inc(rpb_in, 16)
                    if l == 0 and n == 5:
                        wait_drained(sp, 0, ("v", 2, 0)), wait_drained(sp, 0, ("v", 2, 1))
                        sp.dma_start(v_rows.rearrange("(t p) f -> p t f", p=P), v_nat.rearrange("p t a f -> p t (a f)")).then_inc(v_out, 16)
                        wait_drained(sp, 0, ("memk", 0)), wait_drained(sp, 0, ("memv", 0))
                        sp.wait_ge(v_out, 16)
                        rows = v_rows.rearrange("(r c) f -> r c f", c=GRID_W)
                        for b in range(NBLK):
                            for j in range(2):
                                sp.dma_start(v_win[:, 2 * b + j].rearrange("p a f -> p (a f)"),
                                             rows[4 * j:4 * j + 4, KEY0[b]:KEY0[b] + KC, :]).then_inc(v_in, 16)
                load_chunk(l, n_proj[l])
                load_chunk(l, n_proj[l] + 1)
                sp.dma_start(wr[:, :, 0:NG], moe_wg[l].rearrange("(k p) g -> p k g", p=P)).then_inc(route_in, 16)
                sp.dma_start(wr[:, :, NG:], moe_we[l].rearrange("(k p) g -> p k g", p=P)).then_inc(route_in, 16)
                sp.dma_start(rbias[:, 0:NG], moe_bg[l:l + 1, :].partition_broadcast(P)).then_inc(route_in, 16)
                sp.dma_start(rbias[:, NG:], moe_be[l:l + 1, :].partition_broadcast(P)).then_inc(route_in, 16)
                if l == 0:
                    sp.wait_ge(mix_ready[l], last_mix_round(l, len(block_kinds(l)) - 1))
                else:
                    wait_full(sp, l, ("hT", 5))
                for piece in range(3):
                    load_piece(l, 0, piece)
                    if piece == 0:
                        load_chunk(l, n_proj[l] + 2)
                load_chunk(l, n_proj[l] + 3)
                for piece in range(3):
                    load_piece(l, 1, piece)
                wait_full(sp, l, ("out", 2, 1))
                sp.wait_ge(chunk_low, chunk_number(l, n_proj[l] + 2))
                params = ln1_params(l)
                sp.dma_start(params[:, 0, :], ln1_g[l:l + 1, :].partition_broadcast(P)).then_inc(ln_in, 16)
                sp.dma_start(params[:, 1, :], ln1_b[l:l + 1, :].partition_broadcast(P)).then_inc(ln_in, 16)
                for piece in range(3):
                    if piece == 2:
                        sp.wait_ge(x_gathered[l], 16)
                    load_piece(l, 2, piece)
                sp.sem_inc(y_stored[l], 16)
                sp.wait_ge(blocks_ready, l + 1)
                with sp.Fori(0, NE - 3) as e:
                    store_blocks(l, e)
                    for piece in range(3):
                        load_piece(l, e + 3, piece)
                for e in range(NE - 3, NE):
                    store_blocks(l, e)
                    if e == NE - 3:
                        sp.wait_ge(w_low[l], 3 * NE)
                        sp.dma_start(ln2_p[:, 0, :], ln2_g[l:l + 1, :].partition_broadcast(P)).then_inc(ln2_in, 16)
                        sp.dma_start(ln2_p[:, 1, :], ln2_b[l:l + 1, :].partition_broadcast(P)).then_inc(ln2_in, 16)
                end = blocks_end(sp)
                sp.wait_ge(y_ready[l], end)
                sp.dma_start(y_rows[bass.ds((end - 1) * CAP, CAP), :], y_blk).then_inc(y_stored[l], 16)
                if l + 1 < DEPTH:
                    sp.wait_ge(y_stored[l], (end + 1) * 16)
                    for n in range(2):
                        sp.wait_ge(y_got_in[2 * n], 32 * (l + 1))
                        load_chunk(l + 1, n)
            for t in range(TT):
                wait_x(sp, 1, t, True)
                sp.dma_start(out[0, t * P:(t + 1) * P, :], X[:, t, :]).then_inc(out_done, 16)
            sp.wait_ge(out_done, 16 * TT)

        @block.scalar
        def _(act):
            def drain(l, name, dst, scale=1.0):
                wait_full(act, l, name)
                nc.scalar.activation(dst, bank_of(l, name), ACT.Copy, scale=scale).then_inc(act_drained[l], 1)

            def high_out(l, name, k):
                wait_full(act, l, name)
                nc.scalar.activation(XT16[:, 0, k, :], bank_of(l, name), ACT.Copy, scale=X_SCALE).then_inc(t_high, 1)

            def chunk_high_part(l, n):
                act.wait_ge(chunk_in[l][n % 2], 16 * (n // 2 + 1))
                wait_chunk_place(act, l, n)
                nc.scalar.activation(chunk_parts(l, n)[:, 0], chunk_staged(l, n), ACT.Copy, scale=W_SCALE)\
                    .then_inc(chunk_high, 1)

            def blocked(dst):
                return dst.rearrange("p (b r c) -> p b r c", r=ROWS, c=QC)

            def attention(l):
                for s, at in steps(l):
                    if at(2):
                        n = s - 2
                        act.wait_ge(probsT_full[l], n + 1)
                        if n >= 2:
                            act.wait_ge(values_summed[l], n - 1)
                        nc.scalar.activation(probT[l][:, n % 2, 0, :], PS[:, 2 + n % 2, :], ACT.Copy)\
                            .then_inc(probsT_high, 1)
                    u = at(0)
                    if u:
                        if s >= 3:
                            act.wait_ge(probsT_full[l], s - 2)
                        act.wait_ge(max_ready[l], s + 1)
                        for j in range(2):
                            src = PS[:, (0, 1, 7)[s % 3], 256 * j:256 * j + 256] if u[3] \
                                else sneg[:, s % 3, 256 * j:256 * j + 256]
                            nc.scalar.activation(prob[l][:, s % 3, 256 * j:256 * j + 256], src, ACT.Exp,
                                                 bias=mneg[:, s, j:j + 1], scale=HD ** -0.5 if u[3] else -1.0,
                                                 accum_out=msum[:, s, j:j + 1]).then_inc(probs_ready[l], 1)
            def high_part(l, e, piece, q):
                act.wait_ge(w_in[l][piece], 16 * (e + 1) if isinstance(e, int) else act.to_reg(16 * (e + 1)))
                for lo, hi in ACT_RUNS[piece]:
                    nc.scalar.activation(parts[q][piece][:, 0, lo:hi], staged[piece][:, lo:hi], ACT.Copy,
                                         scale=W_SCALE).then_inc(w_high[l], 1)

            def square_root(var, sd, ready, done, count):
                act.wait_ge(ready, count)
                nc.scalar.activation(sd, var, ACT.Sqrt).then_inc(done, 1)

            for l in range(DEPTH):
                if l == 1:
                    chunk_high_part(1, 0)
                for k in range(KT):
                    high_out(l, ("xT", k), k)
                if l == 0:
                    chunk_high_part(0, 0)
                    for k2 in (0, 2):
                        drain(0, ("memT", k2), memT[:, 2 * k2:2 * k2 + 2, :].rearrange("p a b -> p (a b)"))
                    for n, (kind, c, _, _) in enumerate(chunks[0]):
                        if n + 1 < n_proj[0]:
                            chunk_high_part(0, n + 1)
                        if kind == "v":
                            for half in range(2):
                                wait_full(act, 0, (kind, c, half))
                                nc.scalar.activation(
                                    v_nat[:, 2 * half:2 * half + 2, 0, 256 * c:256 * c + 256],
                                    bank_of(0, (kind, c, half)).rearrange("p (t f) -> p t f", t=2), ACT.Copy,
                                    scale=X_SCALE / XW_SCALE).then_inc(v_high, 1)
                            if n == 0:
                                drain(0, ("memk", 0), memk[:].rearrange("p a b -> p (a b)"))
                                wait_full(act, 0, ("memv", 0))
                                nc.scalar.activation(memv[:, 0].rearrange("p a b -> p (a b)"), bank_of(0, ("memv", 0)),
                                                     ACT.Copy, scale=X_SCALE).then_inc(v_high, 1)
                            continue
                        name = (kind, c, 0)
                        wait_full(act, 0, name)
                        bank = bank_of(0, name)
                        if kind == "q":
                            ins = nc.scalar.activation(
                                blocked(qT[:, 2 * c, :]),
                                bank.rearrange("p (r b c) -> p b r c", b=NBLK, c=QC)[:, :, ::-1, ::-1], ACT.Copy,
                                scale=1 / XW_SCALE)
                        elif kind == "k":
                            ins = nc.scalar.activation(kT[:, 2 * c, :], bank, ACT.Copy, scale=1 / XW_SCALE)
                        else:
                            ins = nc.scalar.activation(qm0[:, 0, :], bank, ACT.Copy, scale=1 / XW_SCALE)
                        ins.then_inc(act_drained[0], 1)
                else:
                    def silu(m):
                        act.wait_ge(conv_done, m + 1)
                        nc.scalar.activation(qk[:, m, :], qk[:, m, :], ACT.Silu).then_inc(silu_done, 1)

                    act.wait_ge(pads_zero, 1)
                    for m in range(12):
                        if m % 2 == 0:
                            chunk_high_part(1, m // 2 + 1)
                        if m >= 4:
                            act.wait_ge(conv_done, m - 3)
                        kind, c, s = "qk"[m // 6], (m % 6) // 2, m % 2
                        drain(1, (kind, c, s), pre[:, m % 4, 2:T + 2], 1 / XW_SCALE)
                        if m >= 2:
                            silu(m - 2)
                    chunk_high_part(1, 7)
                    for s in range(2):
                        drain(1, ("m", 0, s), qm1[:, s, :], 1 / XW_SCALE)
                    silu(10)
                    silu(11)
                    for c in range(3):
                        chunk_high_part(1, 8 + c)
                        for s in range(2):
                            name = ("v", c, s)
                            wait_full(act, 1, name)
                            bank = bank_of(1, name).rearrange("p (t f) -> p t f", t=2)
                            lo = 256 * c
                            while lo < 256 * c + 256:
                                h = lo // ML_DH
                                hi = min(256 * c + 256, ML_DH * (h + 1))
                                ins = nc.scalar.activation(
                                    v_ml[:, 2 * s:2 * s + 2, h, lo - ML_DH * h:hi - ML_DH * h],
                                    bank[:, :, lo - 256 * c:hi - 256 * c], ACT.Copy, scale=1 / XW_SCALE)
                                lo = hi
                            ins.then_inc(act_drained[1], 1)
                    for c in range(3):
                        if c < 2:
                            chunk_high_part(1, 11 + c)
                        for s in range(2):
                            name = ("o", c, s)
                            wait_full(act, 1, name)
                            nc.scalar.activation(o_gate[:, 2 * s:2 * s + 2, 256 * c:256 * c + 256],
                                                 bank_of(1, name).rearrange("p (t f) -> p t f", t=2), ACT.Sigmoid,
                                                 scale=1 / XW_SCALE)\
                                .then_inc(act_drained[1], 1)
                    act.wait_ge(lf_abs, 1)
                    nc.scalar.activation(g_abs, g_abs, ACT.Exp, scale=-1.0).then_inc(lf_ln, 1)
                    act.wait_ge(lf_abs, 2)
                    nc.scalar.activation(g_ln, g_abs, ACT.Ln).then_inc(lf_ln, 1)
                chunk_high_part(l, n_proj[l])
                attention(l)
                if l == 1:
                    act.wait_ge(mcol_set, 1)
                    nc.scalar.activation(em, mcol, ACT.Exp, scale=-1.0).then_inc(em_set, 1)
                    for h in range(ML_HEADS):
                        for d in range(2):
                            n = 2 * h + d
                            act.wait_ge(r_masked, n + 1)
                            if h:
                                act.wait_ge(w_ready, TT * h)
                            for i in range(TT):
                                col = acol[:, i, 4 * d + h:4 * d + h + 1]
                                lo, hi = (i + 1, TT) if d == 0 else (0, i)
                                if hi > lo:
                                    nc.scalar.activation(E[:, d, i, lo * P:hi * P], PS[:, (0, 7)[d], lo * P:hi * P],
                                                         ACT.Exp, bias=col)
                                ins = nc.scalar.activation(E[:, d, i, i * P:(i + 1) * P], Rd[:, d, i * P:(i + 1) * P],
                                                           ACT.Exp, bias=col)
                            ins.then_inc(e_ready, 1)
                    square_root(ml_rstd, ml_rstd, ml_var, ml_sd, 1)
                    act.wait_ge(ml_moments, 1)
                    for n in range(8, 16):
                        Hn = H[:, n // ML_HEADS, ML_DH * (n % ML_HEADS):ML_DH * (n % ML_HEADS + 1)]
                        ins = nc.scalar.activation(Hn, Hn, ACT.Identity, scale=ml_rstd[:, n:n + 1],
                                                   bias=ml_nm[:, n:n + 1])
                        if n % ML_HEADS == ML_HEADS - 1:
                            ins.then_inc(h_normed, 1)
                    chunk_high_part(1, n_proj[1] + 1)
                    for i in range(6):
                        high_out(1, ("hT", i), i)
                if l == 0:
                    chunk_high_part(0, n_proj[0] + 1)
                for n, (e, piece) in enumerate(EARLY):
                    if n in (1, 3):
                        chunk_high_part(l, n_proj[l] + 2 + n // 2)
                    high_part(l, e, piece, e)
                square_root(ln_ve, ln_sd, var_ready, sd_ready, l + 1)
                for t in range(TT):
                    if t in NORM1_SHARED:
                        act.wait_ge(moments, l + 1)
                        nc.scalar.activation(X[:, t, :], X[:, t, :], ACT.Identity, scale=ln_rs[:, t:t + 1],
                                             bias=ln_nm[:, t:t + 1]).then_inc(normed, 1)
                for t in range(TT):
                    if t == TT - 1:
                        for k in range(0, KT, 2):
                            drain(l, ("x1T", k), XT[:, k, :])
                    wait_x(act, l, t)
                    nc.scalar.activation(x_parts(t)[:, 0], by_tile(X[:, t, :]), ACT.Copy, scale=X_SCALE)\
                        .then_inc(x_high, 1)
                rv = routing_views(l)
                act.wait_ge(gdiff, l + 1)
                nc.scalar.activation(rv["ge"], rv["gd"], ACT.Exp).then_inc(gexp, 1)
                act.wait_ge(ediff, l + 1)
                nc.scalar.activation(rv["e2"], rv["ed"], ACT.Exp).then_inc(eexp, 1)

                act.wait_ge(x_stored, 16 * (l + 1))
                high_part(l, 1, 2, 1)

                def rows_out(g):
                    act.wait_ge(xgT_full[l], g)
                    nc.scalar.activation(xgT.rearrange("p k s -> p (k s)"), PS[:, 0, :].bitcast(F16), ACT.Copy)\
                        .then_inc(xgT_ready[l], 1)

                def outputs_up(g, stored):
                    act.wait_ge(y_full[l], g)
                    act.wait_ge(y_stored[l], stored)
                    nc.scalar.activation(y_blk.rearrange("p (a b) -> p a b", b=512), PS[CAP:P, 4:6, :], ACT.Copy)\
                        .then_inc(y_upper[l], 1)

                def expert(e):
                    n, g0 = blocks_of(act, e)
                    with act.Fori(0, n) as i:
                        g = g0 + i
                        nc.scalar.activation(warm, ones[0:1, 0:1], ACT.Silu)
                        outputs_up(g, g * 16)
                        for full, bank, dst, upper in ((h1_full, 1, hs, h1_upper), (h3_full, 2, h3, h3_upper)):
                            act.wait_ge(full[l], g)
                            nc.scalar.activation(dst, PS[CAP:P, bank, :], ACT.Copy).then_inc(upper[l], 1)
                        act.wait_ge(h1_summed[l], g)
                        nc.scalar.activation(hs, hs, ACT.Silu, scale=1 / (X_SCALE * W_SCALE))\
                            .then_inc(silu_ready[l], 1)
                        rows_out(g + 1)
                        act.wait_ge(h_ready_e[l], g)
                        nc.scalar.activation(h_parts[:, 0, :], h3, ACT.Copy).then_inc(h_high[l], 1)
                        act.wait_ge(hT_full[l], g)
                        nc.scalar.activation(hT.rearrange("p k s -> p (k s)"), PS[:, 3, 0:256].bitcast(F16), ACT.Copy)\
                            .then_inc(hT_ready[l], 1)
                    return g0 + n

                act.wait_ge(blocks_ready, l + 1)
                rows_out(1)
                with act.Fori(0, NE - 2, 2) as e:
                    for q in range(2):
                        after = expert(e + q)
                        for piece in range(3):
                            if piece == 2:
                                act.wait_ge(y_full[l], act.to_reg(after))
                            high_part(l, e + q + 2, piece, q)
                expert(NE - 2)
                expert(NE - 1)
                end = blocks_end(act)
                outputs_up(end, end * 16)
                for t in range(TT):
                    nc.scalar.activation(X[:, t, :], X[:, t, :], ACT.Copy, scale=ALPHA).then_inc(x_alpha, 1)
                for step, t in NORM2_ACT:
                    if step == "root":
                        act.wait_ge(var2_ready, TT * l + t + 1)
                        nc.scalar.activation(ln_sd[:, t:t + 1], ln_ve[:, t:t + 1], ACT.Sqrt).then_inc(sd2_ready, 1)
                    else:
                        act.wait_ge(moments2, len(NORM2_SHARED) * l + NORM2_SHARED.index(t) + 1)
                        nc.scalar.activation(X[:, t, :], X[:, t, :], ACT.Identity, scale=ln_rs[:, t:t + 1],
                                             bias=ln_nm[:, t:t + 1]).then_inc(normed2, 1)

        @block.vector
        def _(dve):
            done = [0]

            def link(ins):
                done[0] += 1
                ins.then_inc(dve_step, 1)
                dve.wait_ge(dve_step, done[0])

            def drain(l, name, dst):
                wait_full(dve, l, name)
                nc.vector.tensor_copy(dst, bank_of(l, name)).then_inc(dve_drained[l], 1)

            def unscaled(dst, src):
                return nc.vector.tensor_scalar(dst, src, 1 / XW_SCALE, None, ALU.mult)

            def value_low(dst, src, scale, count):
                dve.wait_ge(v_high, count)
                nc.vector.scalar_tensor_tensor(out=dst[:, 1], in0=src, scalar=scale, in1=dst[:, 0],
                                               op0=ALU.mult, op1=ALU.subtract).then_inc(dve_drained[0], 1)

            def low_out(l, name, k):
                dve.wait_ge(t_high, k + 1 + (0, KT + (KT if name[0] == "hT" else 0))[l])
                nc.vector.scalar_tensor_tensor(out=XT16[:, 1, k, :], in0=bank_of(l, name), scalar=X_SCALE,
                                               in1=XT16[:, 0, k, :], op0=ALU.mult, op1=ALU.subtract)\
                    .then_inc(dve_drained[l], 1)

            def chunk_low_part(l, n):
                dve.wait_ge(chunk_high, chunk_number(l, n))
                nc.vector.scalar_tensor_tensor(out=chunk_parts(l, n)[:, 1], in0=chunk_staged(l, n), scalar=W_SCALE,
                                               in1=chunk_parts(l, n)[:, 0], op0=ALU.mult, op1=ALU.subtract)\
                    .then_inc(chunk_low, 1)

            def softmax_front(l, n, u):
                b, par, i, is_mem = u
                dve.wait_ge(scores_full[l], n + 1)
                bank = PS[:, (0, 1, 7)[n % 3], :].rearrange("p (j k) -> p j k", j=2)
                if is_mem:
                    m = n % 8
                    link(nc.vector.tensor_reduce(mraw[:, m, :], bank, AX, ALU.max))
                    nc.vector.tensor_scalar(mneg[:, n, :], mraw[:, m, :], -(HD ** -0.5), None, ALU.mult)\
                        .then_inc(max_ready[l], 1)
                    return
                if n >= 3:
                    dve.wait_ge(probs_ready[l], 2 * (n - 2))
                if n == 0:
                    dve.wait_ge(bias_built, 3)
                h = 4 * i + par
                dst = sneg[:, n % 3, :].rearrange("p (j k) -> p j k", j=2)
                link(nc.vector.scalar_tensor_tensor(
                    out=dst, in0=bank, scalar=-(HD ** -0.5), in1=bias_tab[:, VARIANT[b], h:h + 3:2, :],
                    op0=ALU.mult, op1=ALU.subtract))
                nc.vector.tensor_reduce(mneg[:, n, :], dst, AX, ALU.min).then_inc(max_ready[l], 1)

            def probs_low(l, n):
                dve.wait_ge(probsT_high, n + 1 + (len(units[0]) if l else 0))
                nc.vector.scalar_tensor_tensor(out=probT[l][:, n % 2, 1, :], in0=PS[:, 2 + n % 2, :], scalar=1.0,
                                               in1=probT[l][:, n % 2, 0, :], op0=ALU.mult, op1=ALU.subtract)\
                    .then_inc(probsT_ready[l], 1)

            def heads_out(l, n, u):
                b, par, i, is_mem = u
                k = 2 if is_mem else 6
                first = n - (0 if is_mem else 2)
                dve.wait_ge(probs_ready[l], 2 * (n + 1))
                r = rsum[:, group_no(l, u) % 2, 0:k]
                link(nc.vector.reciprocal(r, msum[:, first:n + 1, :].rearrange("p a b -> p (a b)")))
                dve.wait_ge(values_summed[l], n + 1)
                dst = (o_mem[l][:, b, :] if is_mem else o_na[:, b, :]).rearrange("p (s q d) -> p s q d", q=2, d=HD)
                src = PS[:, 4 + par, 0:k * HD].rearrange("p (s d) -> p s d", d=HD)
                nc.vector.tensor_tensor(dst[:, :, par, :], src, r.unsqueeze(2).to_broadcast([P, k, HD]), ALU.mult)\
                    .then_inc(heads_ready[l], 1)

            def mix_out(l, u, r):
                b, _, _, is_mem = u
                done_ = last_mix_round(l, block_no(l, u) - 1) if block_no(l, u) else 0
                dve.wait_ge(mix_full[l], done_ + r + 1)
                if is_mem:
                    pieces = [(XT16[:, :, 6:8, b * P:(b + 1) * P], PS[:, 6, 0:256].rearrange("p (i c) -> p i c", i=2))]
                else:
                    pieces = [(XT16[:, :, 3 * r + i, :].rearrange("p a (r c) -> p a r c", c=GRID_W)
                               [:, :, :, QC * b:QC * b + QC],
                               PS[:, 6, i * P:(i + 1) * P].rearrange("p (r c) -> p r c", c=QC)) for i in range(3)]
                for dst, src in pieces:
                    ins = nc.vector.tensor_copy(dst[:, 0], src)
                link(ins)
                for dst, src in pieces:
                    ins = nc.vector.scalar_tensor_tensor(out=dst[:, 1], in0=src, scalar=1.0, in1=dst[:, 0],
                                                         op0=ALU.mult, op1=ALU.subtract)
                ins.then_inc(mix_ready[l], 1)

            def attention(l):
                for s, at in steps(l):
                    if at(0):
                        softmax_front(l, s, at(0))
                    if at(2):
                        probs_low(l, s - 2)
                    if ends_group(at(4)):
                        heads_out(l, s - 4, at(4))
                    for u, r in mix_rounds(at):
                        mix_out(l, u, r)

            def low_part(l, e, piece, q):
                count = (lambda v: v) if isinstance(e, int) else dve.to_reg
                high, low = parts[q][piece][:, 0, :], parts[q][piece][:, 1, :]
                if piece == 0:
                    dve.wait_ge(w_in[l][0], count(16 * (e + 1)))
                    nc.vector.tensor_scalar(high[:, 0:DVE_COLS], staged[0][:, 0:DVE_COLS], W_SCALE, None, ALU.mult)\
                        .then_inc(w_first, 1)
                    dve.wait_ge(w_first, count(l * NE + e + 1))
                    nc.vector.scalar_tensor_tensor(out=low[:, 0:DVE_COLS], in0=staged[0][:, 0:DVE_COLS],
                                                   scalar=W_SCALE, in1=high[:, 0:DVE_COLS],
                                                   op0=ALU.mult, op1=ALU.subtract)
                for j, (lo, hi) in enumerate(ACT_RUNS[piece]):
                    dve.wait_ge(w_high[l], count(N_RUNS * e + sum(len(r) for r in ACT_RUNS[:piece]) + j + 1))
                    ins = nc.vector.scalar_tensor_tensor(out=low[:, lo:hi], in0=staged[piece][:, lo:hi],
                                                         scalar=W_SCALE, in1=high[:, lo:hi],
                                                         op0=ALU.mult, op1=ALU.subtract)
                ins.then_inc(w_low[l], 1)

            def finish(l, t, params):
                link(nc.vector.scalar_tensor_tensor(out=X[:, t, :], in0=X[:, t, :], scalar=ln_mv[:, t, 0:1],
                                                    in1=params[:, 0, :], op0=ALU.subtract, op1=ALU.mult))
                return nc.vector.scalar_tensor_tensor(out=X[:, t, :], in0=X[:, t, :], scalar=ln_rs[:, t:t + 1],
                                                      in1=params[:, 1, :], op0=ALU.mult, op1=ALU.add)

            def norm1(l):
                for t in range(TT):
                    ins = nc.vector.bn_aggr(ln_mv[:, t, :], ln_st[:, t, :, :].rearrange("p a s -> p (a s)"))
                link(ins)
                nc.vector.tensor_scalar(ln_ve, ln_mv[:, :, 1], LN_EPS * XW_SCALE ** 2, None, ALU.add)\
                    .then_inc(var_ready, 1)
                dve.wait_ge(sd_ready, l + 1)
                link(nc.vector.reciprocal(ln_rs, ln_sd))
                nc.vector.scalar_tensor_tensor(out=ln_nm, in0=ln_mv[:, :, 0], scalar=-1.0, in1=ln_rs,
                                               op0=ALU.mult, op1=ALU.mult).then_inc(moments, 1)
                dve.wait_ge(ln_in, 32 * (l + 1))
                for t in range(TT):
                    if t not in NORM1_SHARED:
                        finish(l, t, ln1_params(l)).then_inc(x1_dve, 1)

            def combine_and_norm2(l):
                def front(t):
                    dve.wait_ge(y_got_in[t], 32 * l + 32)
                    dve.wait_ge(x_alpha, TT * l + t + 1)
                    for k in range(2):
                        link(nc.vector.scalar_tensor_tensor(out=X[:, t, :], in0=y_got[:, 2 * t + k, :],
                                                            scalar=gates[:, t, k:k + 1], in1=X[:, t, :],
                                                            op0=ALU.mult, op1=ALU.add))
                    for a in range(2):
                        ins = nc.vector.bn_stats(ln_st[:, t, a, :], X[:, t, 512 * a:512 * a + 512])
                    link(ins)
                    link(nc.vector.bn_aggr(ln_mv[:, t, :], ln_st[:, t, 0:2, :].rearrange("p a s -> p (a s)")))
                    nc.vector.tensor_scalar(ln_ve[:, t:t + 1], ln_mv[:, t, 1:2], LN_EPS, None, ALU.add)\
                        .then_inc(var2_ready, 1)

                def back(t):
                    dve.wait_ge(sd2_ready, TT * l + t + 1)
                    link(nc.vector.reciprocal(ln_rs[:, t:t + 1], ln_sd[:, t:t + 1]))
                    if t in NORM2_SHARED:
                        nc.vector.scalar_tensor_tensor(out=ln_nm[:, t:t + 1], in0=ln_mv[:, t, 0:1], scalar=-1.0,
                                                       in1=ln_rs[:, t:t + 1], op0=ALU.mult, op1=ALU.mult)\
                            .then_inc(moments2, 1)
                    else:
                        finish(l, t, ln2_p).then_inc(x2_dve, 1)

                dve.wait_ge(ln2_in, 32 * (l + 1))
                for t in range(TT):
                    front(t)
                    if t >= 1:
                        back(t - 1)
                back(TT - 1)

            def gate_rows():
                wait_full(dve, 1, ("gates", 0))
                dve.wait_ge(mlp_in, 16 * 8)
                done[0] += 1
                nc.vector.scalar_tensor_tensor(
                    out=g_tok, in0=bank_of(1, ("gates", 0))[:, 0:64].rearrange("p (t g) -> p t g", t=TT),
                    scalar=1 / XW_SCALE, in1=g_bias.unsqueeze(1).to_broadcast([P, TT, 16]),
                    op0=ALU.mult, op1=ALU.add)\
                    .then_inc(dve_drained[1], 1)
                done[0] -= 1
                wait_drained(dve, 1, ("gates", 0))
                nc.vector.scalar_tensor_tensor(out=g_abs, in0=g_tok[:, :, 8:16], scalar=-1.0, in1=g_tok[:, :, 8:16],
                                               op0=ALU.mult, op1=ALU.max).then_inc(lf_abs, 1)
                split = lambda v: v.rearrange("p t (a b) -> p t a b", b=32)[:, :, :, 0:4]
                dve.wait_ge(gates_set, 2)
                for dd in range(2):
                    link(nc.vector.tensor_copy(g_in[:, :, 32 * dd:32 * dd + 4], g_tok[:, :, 4 * dd:4 * dd + 4]))

            def forget_rows():
                dve.wait_ge(lf_ln, 1)
                nc.vector.tensor_scalar(g_abs, g_abs, 1.0, None, ALU.add).then_inc(lf_abs, 1)
                dve.wait_ge(lf_ln, 2)
                for dd in range(2):
                    ins = nc.vector.scalar_tensor_tensor(
                        out=g_fo[:, :, 32 * dd:32 * dd + 4], in0=g_tok[:, :, 8 + 4 * dd:12 + 4 * dd], scalar=0.0,
                        in1=g_ln[:, :, 4 * dd:4 * dd + 4], op0=ALU.min, op1=ALU.subtract)
                ins.then_inc(gates_set, 1)

            def convolve(m):
                kind, c, s = "qk"[m // 6], (m % 6) // 2, m % 2
                wait_drained(dve, 1, (kind, c, s))
                src = pre[:, m % 4, :]
                dst = qk[:, m, :]
                link(nc.vector.tensor_scalar(dst, src[:, 0:T], conv_w[:, m, 0:1], conv_b[:, m:m + 1], ALU.mult, ALU.add))
                for j in range(1, CONV_K):
                    ins = nc.vector.scalar_tensor_tensor(out=dst, in0=src[:, j:j + T], scalar=conv_w[:, m, j:j + 1],
                                                         in1=dst, op0=ALU.mult, op1=ALU.add)
                    if j < CONV_K - 1:
                        link(ins)
                ins.then_inc(conv_done, 1)

            def mlstm():
                wait_full(dve, 1, ("rows", 1))
                li, lf = bank_of(1, ("rows", 0)), bank_of(1, ("rows", 1))
                one = ones[:, 0:1]
                for lo, step in ((0, 1), (32, -1)):
                    hi = lo + 32
                    ins = nc.vector.tensor_tensor_scan(r_F[lo:hi, ::step], one[lo:hi].to_broadcast([32, T]),
                                                       lf[lo:hi, ::step], 0.0, ALU.mult, ALU.add)
                    link(ins)
                link(nc.vector.tensor_tensor(r_a[0:64, :], li[0:64, :], r_F[0:64, :], ALU.subtract))
                for lo, step in ((0, 1), (32, -1)):
                    hi = lo + 32
                    link(nc.vector.tensor_tensor_scan(r_M[lo:hi, ::step], r_a[lo:hi, ::step], r_a[lo:hi, ::step], 0.0,
                                                      ALU.max, ALU.max))
                link(nc.vector.tensor_tensor(r_m[0:64, :], r_F[0:64, :], r_M[0:64, :], ALU.add))
                nc.vector.tensor_scalar(r_M[0:64, :], r_M[0:64, :], -1.0, None, ALU.mult).then_inc(rows_set, 1)
                dve.wait_ge(rows_set, 1)
                dve.sem_inc(dve_drained[1], 2)
                wait_full(dve, 1, ("cols", 0))
                view = bank_of(1, ("cols", 0)).rearrange("p (g t a b) -> p g t a b", g=2, t=TT, b=32)
                for dd in range(2):
                    nc.vector.tensor_copy(mcol[:, :, 4 * dd:4 * dd + 4], view[:, 1, :, dd, 0:4])
                    ins = nc.vector.tensor_copy(acol[:, :, 4 * dd:4 * dd + 4], view[:, 0, :, dd, 0:4])
                ins.then_inc(dve_drained[1], 1)
                wait_drained(dve, 1, ("cols", 0))
                dve.sem_inc(mcol_set, 1)
                dve.wait_ge(em_set, 1)
                Hh = H.rearrange("p t (h f) -> p (t h) f", f=ML_DH)

                def head_statistics(n):
                    dve.wait_ge(h_added, n + 1)
                    at = ML_HEADS * (n % TT) + n // TT
                    link(nc.vector.bn_stats(ml_st[:, at, :], Hh[:, at, :]))

                for h in range(ML_HEADS + 1):
                    if h < ML_HEADS:
                        for d in range(2):
                            n = 2 * h + d
                            dve.wait_ge(r_full, n + 1)
                            if n >= 2:
                                dve.wait_ge(e_ready, n - 1)
                            nc.vector.tensor_tensor(Rd[:, d, :].rearrange("p (t c) -> p t c", c=P),
                                                    PS[:, (0, 7)[d], :].rearrange("p (t c) -> p t c", c=P),
                                                    ml_mask[:, d:d + 1, :].to_broadcast([P, TT, P]), ALU.add)\
                                .then_inc(r_masked, 1)
                    if h >= 1:
                        g = h - 1
                        for t in range(TT):
                            n = TT * g + t
                            dve.wait_ge(num_full, n + 1)
                            bank = PS[:, 5 + n % 2, :].rearrange("p (d f) -> p d f", d=2)
                            if n:
                                head_statistics(n - 1)
                            link(nc.vector.tensor_copy(den[:, n, :], bank[:, :, ML_DH]))
                            link(nc.vector.scalar_tensor_tensor(out=den[:, n, :], in0=den[:, n, :], scalar=-1.0,
                                                                in1=den[:, n, :], op0=ALU.mult, op1=ALU.max))
                            link(nc.vector.tensor_tensor(den[:, n, :], den[:, n, :], em[:, t, g:8:4], ALU.max))
                            link(nc.vector.reciprocal(rden[:, n, :], den[:, n, :]))
                            dst = H[:, t, ML_DH * g:ML_DH * (g + 1)]
                            link(nc.vector.tensor_scalar(dst, bank[:, 0, 0:ML_DH], rden[:, n, 0:1], None, ALU.mult))
                            nc.vector.scalar_tensor_tensor(out=dst, in0=bank[:, 1, 0:ML_DH], scalar=rden[:, n, 1:2],
                                                           in1=dst, op0=ALU.mult, op1=ALU.add).then_inc(h_added, 1)
                    if h < ML_HEADS:
                        dve.wait_ge(e_ready, 2 * h + 2)
                        for i in range(TT):
                            dve.wait_ge(s_full, TT * h + i + 1)
                            for d in range(2):
                                lo, hi = (i, TT) if d == 0 else (0, i + 1)
                                ins = nc.vector.scalar_tensor_tensor(
                                    out=W[:, d, i, lo * P:hi * P], in0=PS[:, 1 + i, lo * P:hi * P],
                                    scalar=ML_DH ** -0.5, in1=E[:, d, i, lo * P:hi * P], op0=ALU.mult, op1=ALU.mult)
                            ins.then_inc(w_ready, 1)
                head_statistics(15)
                for n in range(16):
                    ins = nc.vector.bn_aggr(ml_mv[:, n, :], ml_st[:, n, :])
                link(ins)
                nc.vector.tensor_scalar(ml_rstd, ml_mv[:, :, 1], LN_EPS, None, ALU.add).then_inc(ml_var, 1)
                dve.wait_ge(ml_sd, 1)
                link(nc.vector.reciprocal(ml_rstd, ml_rstd))
                nc.vector.scalar_tensor_tensor(out=ml_nm, in0=ml_mv[:, :, 0], scalar=-1.0, in1=ml_rstd,
                                               op0=ALU.mult, op1=ALU.mult).then_inc(ml_moments, 1)
                dve.wait_ge(o_scaled, 1)
                for t in range(TT):
                    if t < 2:
                        for n in range(ML_HEADS * t, ML_HEADS * (t + 1)):
                            ins = nc.vector.tensor_scalar(Hh[:, n, :], Hh[:, n, :], ml_mv[:, n, 0:1],
                                                          ml_rstd[:, n:n + 1], ALU.subtract, ALU.mult)
                        link(ins)
                    else:
                        dve.wait_ge(h_normed, t - 1)
                    nc.vector.tensor_tensor(H[:, t, :], H[:, t, :], o_gate[:, t, :], ALU.mult).then_inc(h_ready, 1)
                chunk_low_part(1, n_proj[1] + 1)
                for i in range(6):
                    low_out(1, ("hT", i), i)

            def routing(l):
                v = routing_views(l)
                nc.vector.memset(v["gp"], -3e38)
                wait_full(dve, l, ("logits", 0))
                nc.vector.tensor_tensor(v["lg"], bank_of(l, ("logits", 0))[:, 0:144].rearrange("p (t g) -> p t g", t=TT),
                                        rbias[:].unsqueeze(1).to_broadcast([P, TT, 36]), ALU.add)\
                    .then_inc(dve_drained[l], 1)
                wait_drained(dve, l, ("logits", 0))
                link(nc.vector.tensor_copy(v["gp"][:, :, 0:NG], v["lg"][:, :, 0:NG]))
                for t in range(TT):
                    ins = nc.vector.max(v["gm"][:, t, :], v["gp"][:, t, :])
                link(ins)
                for t in range(TT):
                    ins = nc.vector.max_index(v["gi"][:, t, :], v["gm"][:, t, :], v["gp"][:, t, :])
                nc.vector.tensor_tensor(v["gd"], v["lg"][:, :, 0:NG], v["gm"][:, :, 0:1].to_broadcast([P, TT, NG]),
                                        ALU.subtract).then_inc(gdiff, 1)
                dve.wait_ge(gdiff, l + 1)
                link(nc.vector.tensor_copy(v["gif"], v["gi"][:, :, 0:1]))
                link(nc.vector.tensor_tensor(v["oh"], count[:, 0:NG].unsqueeze(1).to_broadcast([P, TT, NG]),
                                             v["gif"].to_broadcast([P, TT, NG]), ALU.is_equal))
                link(nc.vector.tensor_tensor(v["prod"], v["lg"][:, :, NG:].rearrange("p t (g e) -> p t g e", g=NG),
                                             v["oh"].unsqueeze(3).to_broadcast([P, TT, NG, EPG]), ALU.mult))
                link(nc.vector.tensor_reduce(v["es"], v["prod"].rearrange("p t g e -> p t e g"), AX, ALU.add))
                for t in range(TT):
                    ins = nc.vector.max(v["e8"][:, t, :], v["es"][:, t, :])
                link(ins)
                for t in range(TT):
                    ins = nc.vector.max_index(v["ei"][:, t, :], v["e8"][:, t, :], v["es"][:, t, :])
                link(ins)
                nc.vector.tensor_tensor(v["ed"], v["e8"][:, :, 1:2], v["e8"][:, :, 0:1], ALU.subtract)\
                    .then_inc(ediff, 1)
                link(nc.vector.tensor_copy(v["eif"], v["ei"][:, :, 0:2]))
                link(nc.vector.scalar_tensor_tensor(out=v["eid"], in0=v["gif"].to_broadcast([P, TT, 2]),
                                                    scalar=float(EPG), in1=v["eif"], op0=ALU.mult, op1=ALU.add))
                link(nc.vector.tensor_tensor(v["pick"],
                                             count.unsqueeze(1).unsqueeze(1).to_broadcast([P, TT, 2, NE]),
                                             v["eid"].unsqueeze(3).to_broadcast([P, TT, 2, NE]), ALU.is_equal))
                nc.vector.tensor_tensor(v["picks"], v["pick"][:, :, 0, :], v["pick"][:, :, 1, :], ALU.add)\
                    .then_inc(picks_ready, 1)
                dve.wait_ge(gexp, l + 1)
                link(nc.vector.tensor_reduce(v["z"], v["ge"], AX, ALU.add))
                dve.wait_ge(eexp, l + 1)
                link(nc.vector.scalar_tensor_tensor(out=v["dn"], in0=v["e2"], scalar=1.0, in1=v["z"],
                                                    op0=ALU.add, op1=ALU.mult))
                link(nc.vector.tensor_scalar(v["dn"], v["dn"], H_SCALE * W_SCALE, None, ALU.mult))
                link(nc.vector.reciprocal(gates[:, :, 0:1], v["dn"]))
                link(nc.vector.tensor_tensor(gates[:, :, 1:2], gates[:, :, 0:1], v["e2"], ALU.mult))
                wait_full(dve, l, ("rank", 0))
                bank = bank_of(l, ("rank", 0))
                link(nc.vector.tensor_scalar(v["ci"], bank[:, NE * TT:NE * TT + NE], float(CAP - 1), None, ALU.add))
                link(nc.vector.tensor_scalar(v["cs"], v["ci"], CAP.bit_length() - 1, None, ALU.logical_shift_right))
                link(nc.vector.tensor_scalar(v["nb"], v["cs"], 1.0, None, ALU.max))
                link(nc.vector.tensor_tensor_scan(v["inc"], ones[:, 0:NE], v["nb"], 1.0, ALU.mult, ALU.add))
                link(nc.vector.tensor_tensor(v["ex"], v["inc"], v["nb"], ALU.subtract))
                nc.vector.tensor_copy(blk_i[:, 0:NE], v["nb"][0:1])
                nc.vector.tensor_copy(blk_i[:, NE:2 * NE], v["ex"][0:1])
                nc.vector.tensor_copy(blk_i[:, 2 * NE:], v["inc"][0:1, NE - 1:NE]).then_inc(blocks_ready, 1)
                nc.vector.scalar_tensor_tensor(
                    out=v["slot"], in0=v["ex"].unsqueeze(1).to_broadcast([P, TT, NE]), scalar=float(CAP),
                    in1=bank[:, 0:NE * TT].rearrange("p (t e) -> p t e", t=TT), op0=ALU.mult, op1=ALU.add)\
                    .then_inc(dve_drained[l], 1)
                wait_drained(dve, l, ("rank", 0))
                link(nc.vector.tensor_tensor(v["ps"], v["pick"], v["slot"].unsqueeze(2).to_broadcast([P, TT, 2, NE]),
                                             ALU.mult))
                link(nc.vector.tensor_reduce(v["df"], v["ps"], AX, ALU.add))
                nc.vector.tensor_copy(dest[:], v["df"]).then_inc(dest_ready, 1)

            def outputs_out(l, g):
                dve.wait_ge(y_upper[l], g)
                y_v = y_blk.rearrange("p (a b) -> p a b", b=512)
                nc.vector.tensor_tensor(y_v, PS[0:CAP, 4:6, :], y_v, ALU.add).then_inc(y_ready[l], 1)

            def expert(l, e):
                n, g0 = blocks_of(dve, e)
                with dve.Fori(0, n) as i:
                    g = g0 + i
                    dve.wait_ge(h1_upper[l], g)
                    nc.vector.tensor_tensor(hs, PS[0:CAP, 1, :], hs, ALU.add).then_inc(h1_summed[l], 1)
                    dve.wait_ge(h3_upper[l], g)
                    nc.vector.tensor_tensor(h3, PS[0:CAP, 2, :], h3, ALU.add).then_inc(h3_summed[l], 1)
                    dve.wait_ge(h3_summed[l], g)
                    dve.wait_ge(silu_ready[l], g)
                    nc.vector.scalar_tensor_tensor(out=h3, in0=h3, scalar=H_SCALE / (X_SCALE * W_SCALE), in1=hs,
                                                   op0=ALU.mult, op1=ALU.mult).then_inc(h_ready_e[l], 1)
                    outputs_out(l, g)
                    dve.wait_ge(h_high[l], g)
                    nc.vector.tensor_tensor(h_parts[:, 1, :], h3, h_parts[:, 0, :], ALU.subtract).then_inc(h_low[l], 1)

            nc.vector.memset(zrow[:], 0.0).then_inc(zero_set, 1)
            dve.wait_ge(const_in, 32)
            for part, src in ((ident16, ident), (earlier16, earlier), (ones16, ones)):
                ins = nc.vector.tensor_copy(part, src)
            ins.then_inc(const16_set, 1)
            for l in range(DEPTH):
                if l == 1:
                    wait_x_all(dve, 0)
                    for i in range(4):
                        nc.vector.memset(pre[:, i, 0:2], 0.0)
                        ins = nc.vector.memset(pre[:, i, T + 2:T + 4], 0.0)
                    ins.then_inc(pads_zero, 1)
                    nc.vector.memset(v_ml[:, :, :, ML_DH:VW], 1.0)
                    nc.vector.memset(g_in, 0.0).then_inc(gates_set, 1)
                    nc.vector.memset(g_fo, 0.0).then_inc(gates_set, 1)
                if l == 1:
                    chunk_low_part(1, 0)
                for k in range(KT):
                    low_out(l, ("xT", k), k)
                if l == 0:
                    chunk_low_part(0, 0)
                    for k2 in (1, 3):
                        drain(0, ("memT", k2), memT[:, 2 * k2:2 * k2 + 2, :].rearrange("p a b -> p (a b)"))
                    for n, (kind, c, _, _) in enumerate(chunks[0]):
                        if n + 1 < n_proj[0]:
                            chunk_low_part(0, n + 1)
                        if kind == "v":
                            for half in range(2):
                                value_low(v_nat[:, 2 * half:2 * half + 2, :, 256 * c:256 * c + 256]
                                          .rearrange("p t a f -> p a t f"),
                                          bank_of(0, (kind, c, half)).rearrange("p (t f) -> p t f", t=2),
                                          X_SCALE / XW_SCALE, 2 * c + half + 1 + (c > 0))
                            if n == 0:
                                value_low(memv[:].rearrange("p a m f -> p a (m f)"), bank_of(0, ("memv", 0)), X_SCALE, 3)
                            continue
                        name = (kind, c, 1)
                        wait_full(dve, 0, name)
                        bank = bank_of(0, name)
                        if kind == "q":
                            ins = unscaled(
                                qT[:, 2 * c + 1, :].rearrange("p (b r c) -> p b r c", r=ROWS, c=QC),
                                bank.rearrange("p (r b c) -> p b r c", b=NBLK, c=QC)[:, :, ::-1, ::-1])
                        elif kind == "k":
                            ins = unscaled(kT[:, 2 * c + 1, :], bank)
                        else:
                            ins = unscaled(qm0[:, 1, :], bank)
                        ins.then_inc(dve_drained[0], 1)
                else:
                    dve.wait_ge(mlp_in, 16 * 8)
                    for m in range(12):
                        if m % 2 == 0:
                            chunk_low_part(1, m // 2 + 1)
                        convolve(m)
                    chunk_low_part(1, 7)
                    gate_rows()
                    for n in range(8, n_proj[1]):
                        chunk_low_part(1, n)
                    forget_rows()
                chunk_low_part(l, n_proj[l])
                attention(l)
                if l == 1:
                    mlstm()
                if l == 0:
                    chunk_low_part(0, n_proj[0] + 1)
                for c in range(4):
                    for s in range(2):
                        name = ("out", c, s)
                        wait_full(dve, l, name)
                        part = X[:, 2 * s:2 * s + 2, 256 * c:256 * c + 256]
                        nc.vector.scalar_tensor_tensor(out=part, in0=part, scalar=ALPHA * XW_SCALE,
                                                       in1=bank_of(l, name).rearrange("p (t f) -> p t f", t=2),
                                                       op0=ALU.mult, op1=ALU.add).then_inc(dve_drained[l], 1)
                        wait_drained(dve, l, name)
                        for t in (2 * s, 2 * s + 1):
                            ins = nc.vector.bn_stats(ln_st[:, t, c, :], X[:, t, 256 * c:256 * c + 256])
                        if s == 1 and c < 2:
                            chunk_low_part(l, n_proj[l] + c + 2)
                        if 2 * c + s < len(EARLY):
                            e, piece = EARLY[2 * c + s]
                            low_part(l, e, piece, e)
                link(ins)
                norm1(l)

                def x_low_part(t):
                    dve.wait_ge(x_high, TT * l + t + 1)
                    xp = x_parts(t)
                    nc.vector.scalar_tensor_tensor(out=xp[:, 1], in0=by_tile(X[:, t, :]), scalar=X_SCALE, in1=xp[:, 0],
                                                   op0=ALU.mult, op1=ALU.subtract).then_inc(x_low, 1)

                x_low_part(0)
                for k in range(1, KT, 2):
                    drain(l, ("x1T", k), XT[:, k, :])
                for t in range(1, TT):
                    x_low_part(t)
                dve.wait_ge(route_in, 64 * l + 64)
                wait_full(dve, l, ("logitsT", 0))
                nc.vector.tensor_copy(logitsT, bank_of(l, ("logitsT", 0))[0:NG + NE, :]).then_inc(dve_drained[l], 1)
                routing(l)
                dve.wait_ge(x_stored, 16 * (l + 1))
                low_part(l, 1, 2, 1)
                dve.sem_inc(y_full[l], 1)
                with dve.Fori(0, NE - 2, 2) as e:
                    for q in range(2):
                        expert(l, e + q)
                        for piece in range(3):
                            low_part(l, e + q + 2, piece, q)
                expert(l, NE - 2)
                expert(l, NE - 1)
                end = blocks_end(dve)
                outputs_out(l, end)
                combine_and_norm2(l)

        @block.gpsimd
        def _(pool):
            steps_done = [0]
            pool.wait_ge(zero_set, 1)
            pool.dma_start(rpb_pad[0:RPB_PAD].rearrange("(a n) -> a n", a=1), zrow[:]).then_inc(pads_in, 16)
            pool.dma_start(rpb_pad[RPB_PAD + NA_HEADS * RPB_HEAD:].rearrange("(a n) -> a n", a=1), zrow[:])\
                .then_inc(pads_in, 16)
            pool.dma_start(rpb_pad[RPB_PAD:RPB_PAD + NA_HEADS * RPB_HEAD].rearrange("(h n) -> h n", h=NA_HEADS),
                           na_rpb[0].rearrange("h r c -> h (r c)")).then_inc(pads_in, 16)
            steps_done[0] += 1
            nc.gpsimd.memset(zeros, 0.0).then_inc(pool_step, 1)
            pool.wait_ge(pool_step, steps_done[0])
            pool.dma_start(slot_token.rearrange("(b s) o -> b (s o)", s=CAP), zeros[0:MAX_BLOCKS + 2, 0:CAP].bitcast(I32))\
                .then_inc(zeros_stored, 16)
            for r in range((NE + 1) * CAP, (MAX_BLOCKS + 1) * CAP, P):
                pool.dma_start(y_rows[r:r + P, :], zeros).then_inc(zeros_stored, 16)
            pool.wait_ge(zeros_stored, 16 * ((MAX_BLOCKS - NE) * CAP // P + 1))
            pool.wait_ge(rpb_in, 16 * ROWS)
            pool.wait_ge(const_in, 32)
            wait_full(pool, 0, ("memv", 0))
            for v, shift in enumerate((SHIFT[0], SHIFT[1], SHIFT[3])):
                for h in range(NA_HEADS):
                    run = rpb_tab[:, h, shift:shift + 1]
                    src = bass.AP(tensor=run.tensor, offset=run.offset, ap=[list(run.ap[0]), [RPB_ROW, ROWS], [1, KC]])
                    ins = nc.gpsimd.tensor_tensor(bias_tab[:, v, h, :].rearrange("p (r c) -> p r c", c=KC), src,
                                                  na_mask[:, v:v + 1, :].to_broadcast([P, ROWS, KC]), ALU.add)
                ins.then_inc(bias_built, 1)

            for l in range(DEPTH):
                if l == 1:
                    wait_drained(pool, 1, ("o", 2, 1))
                    pool.wait_ge(mlp_in, 16 * 8)
                    nc.gpsimd.tensor_tensor(o_gate, o_gate, norm_g.unsqueeze(1).to_broadcast([P, TT, TOKEN_W]),
                                            ALU.mult).then_inc(o_scaled, 1)
                def scale_and_shift(t, params, ready):
                    steps_done[0] += 1
                    nc.gpsimd.tensor_tensor(X[:, t, :], X[:, t, :], params[:, 0, :], ALU.mult).then_inc(pool_step, 1)
                    pool.wait_ge(pool_step, steps_done[0])
                    nc.gpsimd.tensor_tensor(X[:, t, :], X[:, t, :], params[:, 1, :], ALU.add).then_inc(ready, 1)

                pool.wait_ge(ln_in, 32 * (l + 1))
                for n, t in enumerate(NORM1_SHARED):
                    pool.wait_ge(normed, len(NORM1_SHARED) * l + n + 1)
                    scale_and_shift(t, ln1_params(l), x1_pool)
                pool.wait_ge(x_low, TT * (l + 1))
                pool.dma_start(x_rows.rearrange("(t p) d -> p t d", p=P),
                               parts[1][2].rearrange("p a (b n) -> p (a b) n", b=2)).then_inc(x_stored, 16)
                pool.wait_ge(dest_ready, l + 1)
                for t in range(TT):
                    for k in range(2):
                        pool.indirect_dma_start(out=slot_token, out_offset=bass.IndirectOffsetOnAxis(
                            ap=dest[:, t, k:k + 1].bitcast(U32), axis=0), in_=ctok[:, t:t + 1], in_offset=None)\
                            .then_inc(slots_set, 16)
                pool.wait_ge(slots_set, 32 * TT * (l + 1))
                pool.dma_start(slot_tab[:], slot_token.rearrange("(b s) o -> s (b o)", s=CAP)).then_inc(slots_in, 16)
                pool.wait_ge(slots_in, 16 * l + 16)
                pool.wait_ge(x_stored, 16 * (l + 1))
                pool.wait_ge(blocks_ready, l + 1)
                end = blocks_end(pool)

                def gather(g, first):
                    if not first:
                        pool.wait_ge(xgT_full[l], g - 1)
                    nc.gpsimd.tensor_copy(idx_now[:], slot_tab[:, bass.ds(g, 1)]).then_inc(idx_set[l], 1)
                    this = g if isinstance(g, int) else pool.to_reg(g)
                    settle(pool)
                    pool.wait_ge(idx_set[l], this)
                    pool.indirect_dma_start(out=xg, out_offset=None, in_=x_rows, in_offset=bass.IndirectOffsetOnAxis(
                        ap=idx_now[:].bitcast(U32), axis=0)).then_inc(x_gathered[l], 16)
                    pool.wait_ge(x_gathered[l], 16 * g)

                gather(1, True)
                with pool.Fori(2, end + 1) as g:
                    gather(g, False)
                stored = pool.to_reg(16 * (end + 1))
                settle(pool)
                pool.wait_ge(y_stored[l], stored)
                for t in range(TT):
                    for k in range(2):
                        pool.indirect_dma_start(out=y_got[:, 2 * t + k, :], out_offset=None,
                                                in_=y_rows[0:(MAX_BLOCKS + 1) * CAP, :],
                                                in_offset=bass.IndirectOffsetOnAxis(
                                                    ap=dest[:, t, k:k + 1].bitcast(U32), axis=0))\
                            .then_inc(y_got_in[t], 16)
                pool.wait_ge(ln2_in, 32 * (l + 1))
                for n, t in enumerate(NORM2_SHARED):
                    pool.wait_ge(normed2, len(NORM2_SHARED) * l + n + 1)
                    scale_and_shift(t, ln2_p, x2_pool)


_INS = ['x', 'mem', 'w_mem_kv', 'na_w_in', 'na_rpb', 'ml_w_in', 'ml_conv_w', 'ml_conv_b', 'ml_gate_b', 'ml_norm_g',
        'w_out', 'ln1_g', 'ln1_b', 'ln2_g', 'ln2_b', 'moe_wg', 'moe_bg', 'moe_we', 'moe_be', 'moe_w1', 'moe_w3',
        'moe_w2']


def kernel(**inputs):
    import numpy as _np
    import concourse.bacc as _bacc
    from concourse import mybir as _mybir
    from concourse.bass_utils import run_bass_kernel_spmd as _run

    nc = _bacc.Bacc("TRN2", target_bir_lowering=False, num_devices=1)
    const_f, const_tok = constants()
    arrays = {f"in_{name}": _np.ascontiguousarray(inputs[name]) for name in _INS}
    arrays["const_f"], arrays["const_tok"] = const_f, const_tok
    args = [nc.dram_tensor(name, a.shape, _mybir.dt.from_np(a.dtype), kind="ExternalInput").ap()
            for name, a in arrays.items()]
    out = nc.dram_tensor("out_0", (1, T, D), F32, kind="ExternalOutput").ap()
    encoder(nc, *args, out)
    r = _run(nc, [arrays], core_ids=[0])
    return r.results[0]["out_0"]
```
